# Optimizing a Trainium2 kernel written in Bass

```python
import jax, jax.numpy as jnp
from jax import lax
import numpy as np
import math

D_MODEL = 1024
BATCH = 1
SEQ = 512
DEPTH = 2

CHUNK = 64
N_A_LAYERS = DEPTH // 2
N_B_LAYERS = DEPTH - N_A_LAYERS
A_HEADS = 8
A_KEY_DIM = 128
A_VAL_DIM = D_MODEL // A_HEADS
A_FORGET_DIM = A_HEADS * A_KEY_DIM
A_IN_DIM = 2 * A_FORGET_DIM + 2 * D_MODEL
B_HEADS = 16
B_HEAD_DIM = D_MODEL // B_HEADS
B_DIM = B_HEADS * B_HEAD_DIM
B_PAST_CHUNKS = 8
B_BAND = (B_PAST_CHUNKS + 1) * CHUNK
REL_CLIP = 256
N_REL = REL_CLIP + CHUNK
FFN_DIM = -(-8 * D_MODEL // (3 * 256)) * 256
NORM_EPS = 1e-6
N_MOD = 6
MASK_VALUE = -1e30
MIN_FORGET = 1e-30


def rms_norm(x, gain):
    xf = x.astype(jnp.float32)
    y = xf * lax.rsqrt(jnp.mean(xf * xf, axis=-1, keepdims=True) + NORM_EPS)
    return (y * gain.astype(jnp.float32)).astype(x.dtype)

def modulate(x, shift, scale):
    return x * (1 + scale[:, None, :]) + shift[:, None, :]

def swiglu(u, w_in, w_out):
    gate, up = jnp.split(u @ w_in, 2, axis=-1)
    return (jax.nn.silu(gate) * up) @ w_out

def hgrn2_mixer(u, w_in, w_out, lb, o_gain):
    bsz, seq, _ = u.shape
    n_chunks = seq // CHUNK
    q, z_f, v, g = jnp.split(u @ w_in, [A_FORGET_DIM, 2 * A_FORGET_DIM, 2 * A_FORGET_DIM + D_MODEL], axis=-1)
    q = jax.nn.silu(q)
    zf = z_f.astype(jnp.float32)
    lbf = lb.astype(jnp.float32)
    sig = jax.nn.sigmoid(zf)
    f = lbf + (1 - lbf) * sig
    log_f = jnp.log(jnp.maximum(f, MIN_FORGET))
    k = (1 - lbf) * (1 - sig)

    def to_chunks(t, d):
        return t.astype(jnp.float32).reshape(bsz, n_chunks, CHUNK, A_HEADS, d).transpose(1, 0, 2, 3, 4)

    xs = (to_chunks(q, A_KEY_DIM), to_chunks(k, A_KEY_DIM), to_chunks(v, A_VAL_DIM), to_chunks(log_f, A_KEY_DIM))
    causal = jnp.tril(jnp.ones((CHUNK, CHUNK), dtype=bool))

    def step(state, chunk):
        qc, kc, vc, lfc = chunk
        b = jnp.cumsum(lfc, axis=1)
        diff = b[:, :, None] - b[:, None, :]
        decay = jnp.exp(jnp.where(causal[None, :, :, None, None], diff, MASK_VALUE))
        attn = jnp.einsum('bthd,btshd,bshd->bhts', qc, decay, kc)
        o = (jnp.einsum('bhts,bshv->bthv', attn, vc)
             + jnp.einsum('bthd,bhdv->bthv', qc * jnp.exp(b), state))
        b_last = b[:, -1]
        state = (jnp.exp(b_last)[..., None] * state
                 + jnp.einsum('bshd,bshv->bhdv', kc * jnp.exp(b_last[:, None] - b), vc))
        return state, o

    state0 = jnp.zeros((bsz, A_HEADS, A_KEY_DIM, A_VAL_DIM), jnp.float32)
    _, o = lax.scan(step, state0, xs)
    o = o.transpose(1, 0, 2, 3, 4).reshape(bsz, seq, A_HEADS, A_VAL_DIM)
    o = o * lax.rsqrt(jnp.mean(o * o, axis=-1, keepdims=True) + NORM_EPS) * o_gain.astype(jnp.float32)
    o = o * jax.nn.silu(g.astype(jnp.float32)).reshape(bsz, seq, A_HEADS, A_VAL_DIM)
    return o.reshape(bsz, seq, D_MODEL).astype(u.dtype) @ w_out

def shared_kv(h, c_act, gain, mod_w, mod_b, w_kv):
    bsz, seq, _ = h.shape
    shift, scale = jnp.split(c_act @ mod_w + mod_b, 2, axis=-1)
    u = modulate(rms_norm(h, gain), shift, scale)
    k, v = jnp.split(u @ w_kv, 2, axis=-1)
    pad = ((0, 0), (B_PAST_CHUNKS * CHUNK, 0), (0, 0), (0, 0))
    k = jnp.pad(k.reshape(bsz, seq, B_HEADS, B_HEAD_DIM), pad)
    v = jnp.pad(v.reshape(bsz, seq, B_HEADS, B_HEAD_DIM), pad)
    return k, v

def chunk_band_attention(u, k_pad, v_pad, w_q, w_o, rel_bias):
    bsz, seq, _ = u.shape
    n_chunks = seq // CHUNK
    q = (u @ w_q).reshape(bsz, n_chunks, CHUNK, B_HEADS, B_HEAD_DIM).transpose(1, 0, 2, 3, 4)
    q_pos = jnp.arange(CHUNK)[:, None] + B_PAST_CHUNKS * CHUNK
    k_pos = jnp.arange(B_BAND)
    rel = jnp.clip(k_pos[None, :] - q_pos, -REL_CLIP, CHUNK - 1) + REL_CLIP
    bias = rel_bias.astype(jnp.float32)[rel].transpose(2, 0, 1)
    scale = B_HEAD_DIM ** -0.5

    def one_chunk(args):
        qc, idx = args
        kb = lax.dynamic_slice_in_dim(k_pad, idx * CHUNK, B_BAND, axis=1)
        vb = lax.dynamic_slice_in_dim(v_pad, idx * CHUNK, B_BAND, axis=1)
        s = jnp.einsum('bqhd,bkhd->bhqk', qc, kb).astype(jnp.float32) * scale + bias
        valid = k_pos >= (B_PAST_CHUNKS - idx) * CHUNK
        s = jnp.where(valid, s, MASK_VALUE)
        p = jax.nn.softmax(s, axis=-1).astype(vb.dtype)
        return jnp.einsum('bhqk,bkhd->bqhd', p, vb)

    o = lax.map(one_chunk, (q, jnp.arange(n_chunks)))
    o = o.transpose(1, 0, 2, 3, 4).reshape(bsz, seq, B_DIM)
    return o @ w_o

def first_inputs(seed: int = 0) -> dict:
    key = jax.random.key(seed)
    ks = jax.random.split(key, 24)
    f32 = jnp.float32
    nrm = lambda k, shape, s: jax.random.normal(k, shape, f32) * s
    D = D_MODEL
    return {
        "x": nrm(ks[0], (BATCH, SEQ, D), 1.0),
        "c": nrm(ks[1], (BATCH, D), 1.0),
        "mod_w": nrm(ks[2], (DEPTH, D, N_MOD * D), 0.5 * D ** -0.5),
        "mod_b": nrm(ks[3], (DEPTH, N_MOD * D), 0.02),
        "norm_mix": 1.0 + nrm(ks[4], (DEPTH, D), 0.02),
        "norm_ffn": 1.0 + nrm(ks[5], (DEPTH, D), 0.02),
        "ffn_w_in": nrm(ks[6], (DEPTH, D, 2 * FFN_DIM), D ** -0.5),
        "ffn_w_out": nrm(ks[7], (DEPTH, FFN_DIM, D), FFN_DIM ** -0.5),
        "a_w_in": nrm(ks[8], (N_A_LAYERS, D, A_IN_DIM), D ** -0.5),
        "a_w_out": nrm(ks[9], (N_A_LAYERS, D, D), D ** -0.5),
        "a_lb": nrm(ks[10], (N_A_LAYERS, A_FORGET_DIM), 1.0),
        "a_out_norm": 1.0 + nrm(ks[11], (N_A_LAYERS, A_VAL_DIM), 0.02),
        "kv_norm": 1.0 + nrm(ks[12], (D,), 0.02),
        "kv_mod_w": nrm(ks[13], (D, 2 * D), 0.5 * D ** -0.5),
        "kv_mod_b": nrm(ks[14], (2 * D,), 0.02),
        "kv_w": nrm(ks[15], (D, 2 * B_DIM), D ** -0.5),
        "b_w_q": nrm(ks[16], (N_B_LAYERS, D, B_DIM), D ** -0.5),
        "b_w_o": nrm(ks[17], (N_B_LAYERS, B_DIM, D), B_DIM ** -0.5),
        "b_rel_bias": nrm(ks[18], (N_B_LAYERS, N_REL, B_HEADS), 0.5),
        "final_norm": 1.0 + nrm(ks[19], (D,), 0.02),
    }

def first_block(x, c, mod_w, mod_b, norm_mix, norm_ffn, ffn_w_in, ffn_w_out,
              a_w_in, a_w_out, a_lb, a_out_norm,
              kv_norm, kv_mod_w, kv_mod_b, kv_w,
              b_w_q, b_w_o, b_rel_bias, final_norm):
    c_act = jax.nn.silu(c)
    sm = jax.nn.softmax(a_lb.astype(jnp.float32), axis=0)
    lower_bounds = jnp.cumsum(sm, axis=0) - sm[0]
    h = x
    k_pad = None
    v_pad = None
    for layer in range(DEPTH):
        mod = c_act @ mod_w[layer] + mod_b[layer]
        sh1, sc1, g1, sh2, sc2, g2 = jnp.split(mod, N_MOD, axis=-1)
        u = modulate(rms_norm(h, norm_mix[layer]), sh1, sc1)
        if layer < N_A_LAYERS:
            mix = hgrn2_mixer(u, a_w_in[layer], a_w_out[layer], lower_bounds[layer], a_out_norm[layer])
        else:
            j = layer - N_A_LAYERS
            mix = chunk_band_attention(u, k_pad, v_pad, b_w_q[j], b_w_o[j], b_rel_bias[j])
        h = h + g1[:, None, :] * mix
        u = modulate(rms_norm(h, norm_ffn[layer]), sh2, sc2)
        h = h + g2[:, None, :] * swiglu(u, ffn_w_in[layer], ffn_w_out[layer])
        if layer == N_A_LAYERS - 1:
            k_pad, v_pad = shared_kv(h, c_act, kv_norm, kv_mod_w, kv_mod_b, kv_w)
    return rms_norm(h, final_norm)


DEPTH_2 = 1

D_INNER = D_MODEL
M_WIDTH = D_INNER // 2
M_HEADS = 4
M_HEAD_DIM = M_WIDTH // M_HEADS
H_WIDTH = D_INNER - M_WIDTH
H_GROUPS = 8
HYENA_ORDER = 2
N_DIR = 2
CHUNK_2 = 128
FILTER_EMB = 33
FILTER_HIDDEN = 64
N_SIN = 3
DECAY_TARGET = 1e-2
FAST_DECAY_PCT = 0.3
SLOW_DECAY_PCT = 1.5
D_FF = 4 * D_MODEL
N_GATE = 2 * N_DIR * M_HEADS
EPS = 1e-6

OFF_MQ = 0
OFF_MK = OFF_MQ + M_WIDTH
OFF_HV = OFF_MK + M_WIDTH
OFF_HX1 = OFF_HV + H_WIDTH
OFF_HX2 = OFF_HX1 + H_WIDTH
N_CONV = OFF_HX2 + H_WIDTH
OFF_MV = N_CONV
OFF_MO = OFF_MV + M_WIDTH
OFF_GATE = OFF_MO + M_WIDTH
N_IN = OFF_GATE + N_GATE


def rms_norm_2(x, w):
    xf = x.astype(jnp.float32)
    y = xf * lax.rsqrt(jnp.mean(xf * xf, axis=-1, keepdims=True) + EPS)
    return (y * w.astype(jnp.float32)).astype(x.dtype)

def short_conv3(u, w, b):
    up = jnp.pad(u, ((0, 0), (1, 1), (0, 0)))
    return up[:, :-2] * w[0] + up[:, 1:-1] * w[1] + up[:, 2:] * w[2] + b

def mlstm_chunkwise(q, k, v, log_i, log_f):
    B, H, S, D = q.shape
    L = CHUNK_2
    NC = S // L
    qc = q.reshape(B, H, NC, L, D)
    kc = k.reshape(B, H, NC, L, D)
    vc = v.reshape(B, H, NC, L, D)
    li = log_i.reshape(B, H, NC, L)
    bcum = jnp.cumsum(log_f.reshape(B, H, NC, L), axis=-1)
    g = bcum[..., -1]
    a = g[..., None] - bcum + li

    def step(carry, xs):
        C, n, m = carry
        k_c, v_c, a_c, g_c = xs
        m_new = jnp.maximum(g_c + m, jnp.max(a_c, axis=-1))
        decay = jnp.exp(g_c + m - m_new)
        w = jnp.exp(a_c - m_new[..., None])
        C_new = decay[..., None, None] * C + jnp.einsum('bhl,bhld,bhle->bhde', w, k_c, v_c)
        n_new = decay[..., None] * n + jnp.einsum('bhl,bhld->bhd', w, k_c)
        return (C_new, n_new, m_new), (C, n, m)

    init = (jnp.zeros((B, H, D, D), jnp.float32),
            jnp.zeros((B, H, D), jnp.float32),
            jnp.zeros((B, H), jnp.float32))
    xs = (jnp.moveaxis(kc, 2, 0), jnp.moveaxis(vc, 2, 0),
          jnp.moveaxis(a, 2, 0), jnp.moveaxis(g, 2, 0))
    _, (C_s, n_s, m_s) = lax.scan(step, init, xs)
    C_s = jnp.moveaxis(C_s, 0, 2)
    n_s = jnp.moveaxis(n_s, 0, 2)
    m_s = jnp.moveaxis(m_s, 0, 2)

    causal = jnp.tril(jnp.ones((L, L), dtype=bool))
    dmat = bcum[..., :, None] - bcum[..., None, :] + li[..., None, :]
    dmat = jnp.where(causal, dmat, -jnp.inf)
    inter_log = bcum + m_s[..., None]
    m_t = jnp.maximum(inter_log, jnp.max(dmat, axis=-1))
    wts = jnp.exp(dmat - m_t[..., None])
    s_qk = jnp.einsum('bhctd,bhcsd->bhcts', qc, kc) * wts
    inter_scale = jnp.exp(inter_log - m_t)
    num = (jnp.einsum('bhcts,bhcse->bhcte', s_qk, vc)
           + inter_scale[..., None] * jnp.einsum('bhctd,bhcde->bhcte', qc, C_s))
    den = s_qk.sum(-1) + inter_scale * jnp.einsum('bhctd,bhcd->bhct', qc, n_s)
    h = num / jnp.maximum(jnp.abs(den), jnp.exp(-m_t))[..., None]
    return h.reshape(B, H, S, D)

def hyena_filters(L, w1, b1, w2, b2, w3, b3, w4, freq):
    bands = (FILTER_EMB - 1) // 2
    t = jnp.linspace(0.0, 1.0, L, dtype=jnp.float32)[:, None]
    t_resc = jnp.arange(L, dtype=jnp.float32)[:, None]
    ang = 2.0 * math.pi * t_resc / L
    f = jnp.linspace(1e-4, bands - 1, bands, dtype=jnp.float32)[None, :]
    z = jnp.concatenate([t, jnp.cos(f * ang), -jnp.sin(f * ang)], axis=-1)
    fr = freq.astype(jnp.float32)
    h = jnp.sin(fr[0] * (z @ w1.astype(jnp.float32) + b1.astype(jnp.float32)))
    h = jnp.sin(fr[1] * (h @ w2.astype(jnp.float32) + b2.astype(jnp.float32)))
    h = jnp.sin(fr[2] * (h @ w3.astype(jnp.float32) + b3.astype(jnp.float32)))
    h = (h @ w4.astype(jnp.float32)).reshape(L, N_DIR, HYENA_ORDER, H_WIDTH)
    max_decay = math.log(DECAY_TARGET) / FAST_DECAY_PCT
    min_decay = math.log(DECAY_TARGET) / SLOW_DECAY_PCT
    deltas = jnp.linspace(min_decay, max_decay, H_WIDTH, dtype=jnp.float32)
    window = jnp.exp(-t[:, :, None, None] * jnp.abs(deltas))
    return h * window

def two_sided_fft_conv(u, k_fwd, k_bwd, bias):
    S = u.shape[1]
    kern = jnp.concatenate([k_fwd, jnp.zeros_like(k_fwd[:1]), k_bwd[:0:-1]], axis=0)
    K = jnp.fft.rfft(kern, axis=0)
    U = jnp.fft.rfft(u, n=2 * S, axis=1)
    y = jnp.fft.irfft(U * K[None], n=2 * S, axis=1)[:, :S]
    return y + u * bias

def group_rms(u, n_groups, w):
    B, S, C = u.shape
    ug = u.reshape(B, S, n_groups, C // n_groups)
    ug = ug * lax.rsqrt(jnp.mean(ug * ug, axis=-1, keepdims=True) + EPS)
    return ug.reshape(B, S, C) * w.astype(jnp.float32)

def second_inputs(seed: int = 0) -> dict:
    key = jax.random.key(seed)
    ks = jax.random.split(key, 32)
    f32 = jnp.float32
    nrm = lambda k, shape, scale: jax.random.normal(k, shape, f32) * scale
    gain = lambda k, n: 1.0 + 0.05 * jax.random.normal(k, (n,), f32)
    i_bias = nrm(ks[6], (M_HEADS,), 0.1)
    f_bias = jnp.linspace(3.0, 6.0, M_HEADS, dtype=f32) + nrm(ks[7], (M_HEADS,), 0.1)
    i_bias_b = nrm(ks[8], (M_HEADS,), 0.1)
    f_bias_b = jnp.linspace(3.0, 6.0, M_HEADS, dtype=f32) + nrm(ks[9], (M_HEADS,), 0.1)
    return {
        "x": jax.random.normal(ks[0], (BATCH, SEQ, D_MODEL), f32),
        "norm_mix_pre": gain(ks[1], D_MODEL),
        "norm_mix_post": gain(ks[2], D_MODEL),
        "norm_mlp_pre": gain(ks[3], D_MODEL),
        "norm_mlp_post": gain(ks[4], D_MODEL),
        "w_in": nrm(ks[5], (D_MODEL, N_IN), D_MODEL ** -0.5),
        "b_gates": jnp.concatenate([i_bias, f_bias, i_bias_b, f_bias_b]),
        "conv_w": nrm(ks[10], (3, N_CONV), 3 ** -0.5),
        "conv_b": nrm(ks[11], (N_CONV,), 0.02),
        "mlstm_norm_w": gain(ks[12], M_WIDTH),
        "hyena_norm_w": gain(ks[13], H_WIDTH),
        "filt_w1": nrm(ks[14], (FILTER_EMB, FILTER_HIDDEN), FILTER_EMB ** -0.5),
        "filt_b1": nrm(ks[15], (FILTER_HIDDEN,), 0.02),
        "filt_w2": nrm(ks[16], (FILTER_HIDDEN, FILTER_HIDDEN), FILTER_HIDDEN ** -0.5),
        "filt_b2": nrm(ks[17], (FILTER_HIDDEN,), 0.02),
        "filt_w3": nrm(ks[18], (FILTER_HIDDEN, FILTER_HIDDEN), FILTER_HIDDEN ** -0.5),
        "filt_b3": nrm(ks[19], (FILTER_HIDDEN,), 0.02),
        "filt_w4": nrm(ks[20], (FILTER_HIDDEN, N_DIR * HYENA_ORDER * H_WIDTH), FILTER_HIDDEN ** -0.5),
        "filt_freq": 1.0 + 0.05 * jax.random.normal(ks[21], (N_SIN, FILTER_HIDDEN), f32),
        "filt_bias": nrm(ks[22], (HYENA_ORDER, H_WIDTH), 0.1),
        "w_out": nrm(ks[23], (D_INNER, D_MODEL), D_INNER ** -0.5),
        "w_mlp_in": nrm(ks[24], (D_MODEL, D_FF), D_MODEL ** -0.5),
        "w_mlp_out": nrm(ks[25], (D_FF, D_MODEL), D_FF ** -0.5),
    }

def second_block(x, norm_mix_pre, norm_mix_post, norm_mlp_pre, norm_mlp_post, w_in, b_gates,
              conv_w, conv_b, mlstm_norm_w, hyena_norm_w, filt_w1, filt_b1, filt_w2, filt_b2,
              filt_w3, filt_b3, filt_w4, filt_freq, filt_bias, w_out, w_mlp_in, w_mlp_out):
    B, S, _ = x.shape
    f32 = jnp.float32
    for _layer in range(DEPTH_2):
        hn = rms_norm_2(x, norm_mix_pre)
        proj = (hn @ w_in).astype(f32)
        cv = short_conv3(proj[..., :N_CONV], conv_w.astype(f32), conv_b.astype(f32))

        def heads(u):
            return u.reshape(B, S, M_HEADS, M_HEAD_DIM).transpose(0, 2, 1, 3)
        q = heads(jax.nn.silu(cv[..., OFF_MQ:OFF_MQ + M_WIDTH]))
        k = heads(jax.nn.silu(cv[..., OFF_MK:OFF_MK + M_WIDTH])) * (M_HEAD_DIM ** -0.5)
        v = heads(proj[..., OFF_MV:OFF_MV + M_WIDTH])
        o_gate = jax.nn.sigmoid(proj[..., OFF_MO:OFF_MO + M_WIDTH])
        gates = (proj[..., OFF_GATE:OFF_GATE + N_GATE] + b_gates.astype(f32)).transpose(0, 2, 1)
        gates = gates.reshape(B, 2 * N_DIR, M_HEADS, S)
        h_fwd = mlstm_chunkwise(q, k, v, gates[:, 0], jax.nn.log_sigmoid(gates[:, 1]))
        flip = lambda u: jnp.flip(u, axis=2)
        h_bwd = flip(mlstm_chunkwise(flip(q), flip(k), flip(v), flip(gates[:, 2]),
                                     flip(jax.nn.log_sigmoid(gates[:, 3]))))
        h_m = (h_fwd + h_bwd).transpose(0, 2, 1, 3).reshape(B, S, M_WIDTH) * o_gate
        y_m = group_rms(h_m, M_HEADS, mlstm_norm_w)

        filt = hyena_filters(S, filt_w1, filt_b1, filt_w2, filt_b2, filt_w3, filt_b3,
                             filt_w4, filt_freq)
        fb = filt_bias.astype(f32)
        z = cv[..., OFF_HV:OFF_HV + H_WIDTH]
        z = cv[..., OFF_HX1:OFF_HX1 + H_WIDTH] * two_sided_fft_conv(z, filt[:, 0, 0], filt[:, 1, 0], fb[0])
        z = cv[..., OFF_HX2:OFF_HX2 + H_WIDTH] * two_sided_fft_conv(z, filt[:, 0, 1], filt[:, 1, 1], fb[1])
        y_h = group_rms(z, H_GROUPS, hyena_norm_w)

        mix = jnp.concatenate([y_m, y_h], axis=-1).astype(x.dtype) @ w_out
        x = x + rms_norm_2(mix, norm_mix_post)

        hm = rms_norm_2(x, norm_mlp_pre)
        ff = jnp.square(jax.nn.relu(hm @ w_mlp_in)) @ w_mlp_out
        x = x + rms_norm_2(ff, norm_mlp_post)
    return x


def setup_inputs(seed=0):
    out = dict(first_inputs(seed))
    for name, value in second_inputs(seed + 1).items():
        if name != "x":
            out[name + "_2"] = value
    return out


def reference(
    x, c, mod_w, mod_b, norm_mix, norm_ffn, ffn_w_in, ffn_w_out, a_w_in, a_w_out, a_lb,
    a_out_norm, kv_norm, kv_mod_w, kv_mod_b, kv_w, b_w_q, b_w_o, b_rel_bias, final_norm,
    norm_mix_pre_2, norm_mix_post_2, norm_mlp_pre_2, norm_mlp_post_2, w_in_2, b_gates_2,
    conv_w_2, conv_b_2, mlstm_norm_w_2, hyena_norm_w_2, filt_w1_2, filt_b1_2, filt_w2_2,
    filt_b2_2, filt_w3_2, filt_b3_2, filt_w4_2, filt_freq_2, filt_bias_2, w_out_2, w_mlp_in_2,
    w_mlp_out_2,
):
    x = first_block(
        x, c, mod_w, mod_b, norm_mix, norm_ffn, ffn_w_in, ffn_w_out, a_w_in, a_w_out, a_lb,
        a_out_norm, kv_norm, kv_mod_w, kv_mod_b, kv_w, b_w_q, b_w_o, b_rel_bias, final_norm,
    )
    return second_block(
        x, norm_mix_pre_2, norm_mix_post_2, norm_mlp_pre_2, norm_mlp_post_2, w_in_2, b_gates_2,
        conv_w_2, conv_b_2, mlstm_norm_w_2, hyena_norm_w_2, filt_w1_2, filt_b1_2, filt_w2_2,
        filt_b2_2, filt_w3_2, filt_b3_2, filt_w4_2, filt_freq_2, filt_bias_2, w_out_2,
        w_mlp_in_2, w_mlp_out_2,
    )


_drawn_inputs = setup_inputs


def setup_inputs(seed=0):
    import zlib

    import numpy as np

    out = dict(_drawn_inputs(seed))
    spreads = {}
    factors = {'norm_mix': 6.774,
     'norm_ffn': 4.657,
     'a_out_norm': 7.838,
     'kv_norm': 8.0,
     'b_rel_bias': 2.927}
    for name, (base, spread) in spreads.items():
        noise = np.random.default_rng([zlib.crc32(name.encode()), seed]).standard_normal(out[name].shape)
        drawn = base * np.exp(spread * noise) if base else spread * noise
        out[name] = __import__('jax').numpy.asarray(drawn.astype(out[name].dtype))
    for name, factor in factors.items():
        out[name] = (out[name] * factor).astype(out[name].dtype)
    return out
```

```python
import math
from contextlib import ExitStack

import concourse.bass as bass
from concourse import mybir

F32 = mybir.dt.float32
F32R = mybir.dt.float32r
I8 = mybir.dt.int8
ALU = mybir.AluOpType
ACT = mybir.ActivationFunctionType
AX = mybir.AxisListType

P = 128
SEQ = 512
D = 1024
KC = D // P
TB = SEQ // P
SLOT = 2048
A_HEADS = 8
B_HEADS = 16
HD = D // B_HEADS
REL_CLIP = 256
CHUNK = 64
FFN = 2816
M_HEADS = 4
HW = 512
D_FF = 4 * D
FH = 64
FE = 33
NLEV = 7
EPS = 1e-6
MIN_FORGET = 1e-30
MASK_VALUE = -1e30
TWO_PI = 2 * math.pi
TWO_PI_HI = 6.28125
ROUND = 1.5 * 2.0**23

VEC_ORDER = [("c", 8), ("mod_b0", 48), ("kv_mod_b", 16), ("mod_b1", 48), ("norm_mix0", 8), ("norm_mix1", 8),
             ("norm_ffn0", 8), ("norm_ffn1", 8), ("kv_norm", 8), ("final_norm", 8), ("pre2", 8), ("post2", 8),
             ("mlp_pre2", 8), ("mlp_post2", 8), ("a_lb", 8), ("a_out_norm", 1), ("conv_w", 60), ("conv_b", 20),
             ("mlstm_norm", 4), ("hyena_norm", 4), ("filt_b", 3), ("filt_fr", 3), ("b_gates", 1)]
VEC = {}
_at = 0
for _n, _w in VEC_ORDER:
    VEC[_n] = (_at, _at + _w)
    _at += _w
NVEC = _at

FFN_CH = FFN // P
MLP_CH = D_FF // P
FFN_G = FFN_CH // 2
MLP_G = MLP_CH // 2


def plan_stream():
    s = []

    def w(label, n, mods=0):
        for i in range(n):
            s.append(("W", label, i))
            s.extend([("M",)] * mods)

    def one(label, i, mods=0):
        s.append(("W", label, i))
        s.extend([("M",)] * mods)

    one("spec", 0, 2)
    one("spec", 1, 3)
    one("spec", 2, 3)
    one("spec", 3)
    for label, i in A_SLOTS:
        one(label, i, 2 if label == "v0" else 1 if label == "g0" else 0)
    w("wo0", 4, 1)
    left = [32]

    def ffn(layer):
        def put(label, i):
            m = 1 if layer == "0" and left[0] else 0
            left[0] -= m
            one(label + layer, i, m)
        for g in range(FFN_G + 1):
            if g < FFN_G:
                put("fi", 2 * g)
                put("fi", 2 * g + 1)
            if g:
                put("fo", g - 1)

    ffn("0")
    for x in ("kk", "vv", "qq", "wo1"):
        w(x, 4)
    ffn("1")
    w("mqk", 4)
    w("mv", 2)
    w("mgate", 1)
    w("mo", 2)
    w("h2", 6)
    w("dft", 8)
    w("wo2", 4)
    for g in range(MLP_G + 1):
        if g < MLP_G:
            one("mi", g)
        if g:
            one("mout", g - 1)
    return s


A_SLOTS = [("v0", 0), ("v0", 1), ("p0", 0), ("p0", 1), ("g0", 0), ("p0", 2), ("p0", 3), ("g0", 1), ("v0", 2), ("v0", 3),
           ("p0", 4), ("p0", 5), ("p0", 6), ("g0", 2), ("p0", 7), ("g0", 3)]
A_GRAM = {4: 0, 5: 1, 7: 2, 8: 3, 12: 4, 13: 5, 14: 6, 15: 7}
A_NORM = {5: [0], 6: [1], 8: [2], 9: [3], 14: [4], 15: [5]}
A_TAIL = [6, 7]

STREAM = plan_stream()
W_AT, W_LIST, M_BEFORE = {}, [], []
for _s in STREAM:
    if _s[0] == "W":
        W_AT[_s[1:]] = len(W_LIST)
        W_LIST.append(_s[1:])
    else:
        M_BEFORE.append(len(W_LIST))
NW = len(W_LIST)
NM = len(M_BEFORE)
NVMOD = NM // 4
(SH1_0, SC1_0, G1_0, SH2_0, SC2_0, G2_0, KSH, KSC, SH1_1, SC1_1, G1_1, SH2_1, SC2_1, G2_1) = range(14)
SCALES = {SC1_0: (0, "norm_mix0"), SC2_0: (1, "norm_ffn0"), KSC: (2, "kv_norm"), SC1_1: (3, "norm_mix1"), SC2_1: (4, "norm_ffn1")}


MODS_MIX0, MODS_WO0, MODS_FFN0, MODS_OUT0, MODS_ALL = range(5)
MOD_POINTS = [(sum(b <= w for b in M_BEFORE), v) for w, v in (
    (W_AT[("spec", 3)], 2), (W_AT[("g0", 3)], 4), (W_AT[("wo0", 3)], 5), (W_AT[("fo0", 0)] - 1, 6), (NW, NVMOD))]


def plan_outputs():
    first, ready, frees, used = {}, [], [], {}
    count = {"act": 0, "dve": 0}
    events = [0]

    def out(label, n, who, share=1, slots=()):
        first.setdefault(label, len(ready))
        for i in range(n):
            if i % share == 0:
                count[who] += 1
            frees.append((who, count[who]))
            events[0] += 1
            ready.append(events[0])
            if slots and (i + 1) % (n // len(slots)) == 0:
                used[W_AT[slots[(i + 1) // (n // len(slots)) - 1]]] = events[0]

    def part(slot):
        events[0] += 1
        used[W_AT[slot]] = events[0]

    out("filt", 3, "act")
    for o in (0, 1):
        out(f"taps{o}", 2 * TB, "dve")
        out(f"spec{o}", 4, "act", slots=[("spec", 2 * o)])
        out(f"spec{o}", 5, "act", slots=[("spec", 2 * o + 1)])
    for label, i in A_SLOTS:
        if label == "p0":
            out(f"zf{i}", 1, "act")
            out(f"q{i}", 1, "act", slots=[(label, i)])
        elif label == "g0":
            out(f"g{i}", 2, "act", slots=[(label, i)])
        elif i % 2 == 0:
            part((label, i))
        else:
            out(f"v{i // 2}", 4, "act", slots=[(label, i)])
    out("wo0", 8, "dve", slots=[("wo0", i) for i in range(4)])

    def ffn(layer):
        for g in range(FFN_G + 1):
            if g < FFN_G:
                for i in (2 * g, 2 * g + 1):
                    out(f"fi{layer}_{i}", 2, "dve", 2, [(f"fi{layer}", i)])
            if g:
                out(f"fo{layer}_{g - 1}", 8, "dve", 1, [(f"fo{layer}", g - 1)])

    ffn("0")
    out("kk", 8, "act", slots=[("kk", i) for i in range(4)])
    for i in (0, 1):
        part(("vv", 2 * i))
        out(f"vv{i}", 4, "act", slots=[("vv", 2 * i + 1)])
    out("qq", 8, "act", slots=[("qq", i) for i in range(4)])
    out("wo1", 8, "dve", slots=[("wo1", i) for i in range(4)])
    ffn("1")
    out("mqk", 8, "dve", slots=[("mqk", i) for i in range(4)])
    part(("mv", 0))
    out("mv", 4, "act", slots=[("mv", 1)])
    out("mgate", 1, "act", slots=[("mgate", 0)])
    out("mo", 4, "act", slots=[("mo", 0), ("mo", 1)])
    out("h2", 12, "dve", slots=[("h2", i) for i in range(6)])
    for o in (0, 1):
        out(f"fa{o}", 4, "act", slots=[("dft", 4 * o)])
        out(f"fb{o}", 4, "dve", slots=[("dft", 4 * o + 1)])
        part(("dft", 4 * o + 2))
        out(f"iy{o}", 4, "dve", slots=[("dft", 4 * o + 3)])
    out("wo2", 8, "dve", slots=[("wo2", i) for i in range(4)])
    for g in range(MLP_G + 1):
        if g < MLP_G:
            out(f"mi{g}", 2, "dve", 1, [("mi", g)])
        if g:
            out(f"mout{g - 1}", 8, "dve", 1, [("mout", g - 1)])
    return first, ready, frees, used


FIRST, READY, FREES, USED = plan_outputs()

GRAM_PER_HEAD = 11


def gram_free(j):
    h, i = divmod(j, GRAM_PER_HEAD)
    return ("dve", NLEV * h + i + 1) if i < NLEV else ("act", (GRAM_PER_HEAD - NLEV) * h + i - NLEV + 1)


NORM = {"mix0": 0, "ffn0": 9, "kv": 10, "ffn1": 11, "final": 12, "pre2": 13, "post2": 14, "mlp_pre2": 15, "mlp_post2": 16}
MAIN = {"mix0": 0, "ffn0": 1, "kv": 2, "ffn1": 3, "final": 4, "pre2": 5, "post2": 6, "mlp_pre2": 7, "mlp_post2": 8}
U_SPEC, U_MIX0, U_YA, U_FFN0, U_KV, U_MIX1, U_O, U_FFN1, U_PRE2 = 0, 8, 16, 24, 32, 40, 48, 56, 64
U_Y = [72, 80]
U_MIX2, U_MLP = 88, 96
G_SPEC, G_FFN0, G_FFN1 = 0, 8, 8 + FFN_CH
G_Z = [8 + 2 * FFN_CH, 12 + 2 * FFN_CH]
G_MLP = 16 + 2 * FFN_CH
NG = 4
MRING = 6
FROM_NORM = {"mix0": 0, "ffn0": 8, "kv": 16, "mix1": 24, "ffn1": 32, "pre2": 40, "mlp_pre2": 48}


def build(nc, A, stop=None):
    hi_ring, raw_ring = 2, 3
    ctx = ExitStack()
    with ctx:
        def sb(name, shape, dt=F32):
            return ctx.enter_context(nc.sbuf_tensor(name, shape, dt))

        def sem(name):
            return ctx.enter_context(nc.semaphore(name))

        bank = [ctx.enter_context(nc.psum_tensor(f"bank{i}", [P, SEQ], F32)) for i in range(8)]

        raw = [sb(f"raw{i}", [P, SLOT]) for i in range(raw_ring)]
        w_hi = [sb(f"w_hi{i}", [P, SLOT], F32R) for i in range(hi_ring)]
        w_lo = [sb(f"w_lo{i}", [P, SLOT], F32R) for i in range(hi_ring)]
        u_hi = sb("u_hi", [P, KC, SEQ], F32R)
        u_lo = sb("u_lo", [P, KC, SEQ], F32R)
        g_hi = sb("g_hi", [P, NG, SEQ], F32R)
        g_lo = sb("g_lo", [P, NG, SEQ], F32R)
        H = sb("H", [P, KC, SEQ])
        vec = sb("vec", [P, NVEC])
        modc = sb("modc", [P, NVMOD * KC])
        macc = sb("macc", [P, MRING, 256])
        acol = sb("acol", [P, 5 * KC])
        cact = sb("cact", [P, KC])
        zcol = sb("zcol", [P, 2])
        onec = sb("onec", [P, 1])
        ident = sb("ident", [P, P])
        ones = sb("ones", [P, P])
        lbt = sb("lbt", [P, 7, KC])
        rt = sb("rt", [P, 16])
        rc = sb("rc", [P, 16])
        scr = sb("scr", [P, 8, SEQ])
        sq = [scr[:, 0, :], scr[:, 1, :]]
        tn = [scr[:, 2, :], scr[:, 3, :]]
        uf = [scr[:, 4, :], scr[:, 5, :]]
        ssum = scr[:, 6, :]
        diag = scr[:, 7, :].rearrange("p (a b) -> p a b", a=TB)
        pool_words = 15700
        pool = sb("pool", [P, pool_words])

        class Arena:
            def __init__(self, at=0):
                self.at = at

            def __call__(self, words):
                a = self.at
                self.at += words
                assert self.at <= pool_words, self.at
                return pool[:, a:a + words]

        def view(ap, *dims):
            letters = "abcd"[:len(dims)]
            return ap.rearrange(f"p ({' '.join(letters)}) -> p {' '.join(letters)}", **dict(zip(letters, dims)))

        ar = Arena()
        f_w1 = ar(FH)
        f_w2 = view(ar(2 * FH), 2, FH)
        f_w4 = ar(4 * HW)
        f_z = ar(SEQ)
        f_h = view(ar(3 * SEQ), 3, SEQ)
        f_a = view(ar(4 * SEQ), 4, SEQ)
        f_bias = ar(2 * HW)
        win = view(ar(TB * HW), TB, HW)
        tap = view(ar(4 * HW), 4, HW)
        spec_st = view(ar(2 * HW), 2, HW)
        spec_ny = ar(HW)
        f_tf, f_tb = scr[:, 0, :], scr[:, 1, :]
        ar = Arena()
        a_v = view(ar(TB * D), TB, D)
        a_y = view(ar(KC * SEQ), KC, SEQ)
        a_gate = view(ar(4 * SEQ), 4, SEQ)
        a_q = view(ar(2 * SEQ), 2, SEQ)
        a_k = view(ar(2 * SEQ), 2, SEQ)
        a_tot = view(ar(2 * SEQ), 2, SEQ)
        a_p = view(ar(2 * SEQ), 2, TB, P)
        a_off = ar(6 * P)
        a_mask = ar(NLEV * P // 4).bitcast(I8).rearrange("p (l t) -> p l t", l=NLEV)
        ar = Arena()
        ff_s = view(ar(2 * SEQ), 2, SEQ)
        ff_h = view(ar(2 * SEQ), 2, SEQ)
        Facc = view(ar(KC * SEQ), KC, SEQ)
        ar = Arena()
        b_k = view(ar(KC * SEQ), KC, SEQ)
        b_q = view(ar(KC * SEQ), KC, SEQ)
        b_v = view(ar(TB * D), TB, D)
        b_T = view(ar(2 * SEQ), 2, SEQ)
        b_off = [0, 128, 384, 768]
        b_s = [ar(1280), scr[:, 4:7, :].rearrange("p a b -> p (a b)")[:, 0:1280]]
        b_pt = scr[:, 0:4, :]
        b_mx = ar(8)
        b_sm = ar(8)
        b_rc = ar(8)
        ar = Arena()
        m_h = view(ar(M_HEADS * SEQ), M_HEADS, SEQ)
        m_qk = view(ar(8 * SEQ), 8, SEQ)
        m_v = view(ar(TB * HW), TB, HW)
        m_og = view(ar(M_HEADS * SEQ), M_HEADS, SEQ)
        m_w = view(ar(2 * 1280), 2, 1280)
        m_tri = view(ar(2 * P), 2, P)
        m_sel = view(ar(M_HEADS * P), M_HEADS, P)
        cv = view(ar(2 * SEQ), 2, SEQ)
        m_cc = ar(32)
        m_em = ar(32)
        m_rd = ar(16)
        m_dd = ar(16)
        g_all = ar(SEQ)
        gi = scr[:, 0:2, :]
        gf = scr[:, 2:4, :]
        gt = scr[:, 4:6, :]
        gs = scr[:, 6:8, :]
        m_off = [[0, 512, 896, 1152], [0, 128, 384, 768]]
        ar = Arena(M_HEADS * SEQ)
        h_tok = [view(ar(TB * HW), TB, HW) for _ in range(3)]
        h_A = view(ar(TB * HW), TB, HW)
        h_kA = view(ar(2 * HW), 2, HW)
        h_kB = view(ar(2 * HW), 2, HW)
        h_r = ar(32)
        h_m = ar(32)
        h_t = scr[:, 0:6, :]
        h_y = h_tok[0]
        spec_dram = nc.dram_tensor("spectra", (2, 2, TB, P, HW), F32).ap()

        raw_in = [sem(f"raw_in{i}") for i in range(raw_ring)]
        hi_done, lo_done, m_done = sem("hi_done"), sem("lo_done"), sem("m_done")
        mod_sum, mod_col, acol_done = sem("mod_sum"), sem("mod_col"), sem("acol_done")
        product = sem("product")
        free = {"act": sem("out_free_act"), "dve": sem("out_free_dve")}
        gfree = {"act": sem("gram_free_act"), "dve": sem("gram_free_dve")}
        gram_ready = sem("gram_ready")
        vec_in, filt_in, x_in, mask_in, rel_in0, rel_in1, m_in = (
            sem(x) for x in ("vec_in", "filt_in", "x_in", "mask_in", "rel_in0", "rel_in1", "m_in"))
        rel_in = [rel_in0, rel_in1]
        rel_ready, mask_ready = sem("rel_ready"), sem("mask_ready")
        const_ready = sem("const_ready")
        cact_ready, lb_d, lb_e, lb_ready = sem("cact_ready"), sem("lb_d"), sem("lb_e"), sem("lb_ready")
        h_upd, sq_done, sq_add = sem("h_upd"), sem("sq_done"), sem("sq_add")
        n_col, n_root, n_diag, n_bc = (sem(x) for x in ("n_col", "n_root", "n_diag", "n_bc"))
        u_t, u_f, u_h, u_l = sem("u_t"), sem("u_f"), sem("u_h"), sem("u_l")
        g_h, g_l = sem("g_h"), sem("g_l")
        vlink, slink = sem("vlink"), sem("slink")
        f_arg, f_red, f_sin, tap_done = sem("f_arg"), sem("f_red"), sem("f_sin"), sem("tap_done")
        spec_ev = sem("spec_ev")
        spec_out = [sem("spec_out0"), sem("spec_out1")]
        a_keys, a_qf, a_lvl, a_os, a_yd = (sem(x) for x in ("a_keys", "a_qf", "a_lvl", "a_os", "a_yd"))
        sg_done = sem("sg_done")
        at_s, at_sc, at_mx, at_e, at_p, at_tr, at_pt, at_o = (
            sem(x) for x in ("at_s", "at_sc", "at_mx", "at_e", "at_p", "at_tr", "at_pt", "at_o"))
        cv_y, cv_q, tr_done, tr_ev = (sem(x) for x in ("cv_y", "cv_q", "tr_done", "tr_ev"))
        mg_q, mg_e, mg_l, mg_rows, mg_tr, mg_cc, mg_em = (
            sem(x) for x in ("mg_q", "mg_e", "mg_l", "mg_rows", "mg_tr", "mg_cc", "mg_em"))
        ml_mb, ml_a, ml_w, ml_m, ml_s, ml_p, ml_num, ml_nev, ml_den, ml_rd, ml_bc, ml_h, ml_sq, ml_bf = (
            sem(x) for x in ("ml_mb", "ml_a", "ml_w", "ml_m", "ml_s", "ml_p", "ml_num", "ml_nev", "ml_den", "ml_rd",
                             "ml_bc", "ml_h", "ml_sq", "ml_bf"))
        ml_col, ml_root, ml_diag, ml_nbc, ml_y = (sem(x) for x in ("ml_col", "ml_root", "ml_diag", "ml_nbc", "ml_y"))
        sp_in = [sem("sp_in0"), sem("sp_in1")]
        hy_y, hy_sq, hy_rs, hy_rt, hy_n, hy_tr, hy_yf = (
            sem(x) for x in ("hy_y", "hy_sq", "hy_rs", "hy_rt", "hy_n", "hy_tr", "hy_yf"))
        out_done = sem("out_done")
        block = ctx.enter_context(nc.Block())

        def vcol(name, i=0):
            return vec[:, VEC[name][0] + i:VEC[name][0] + i + 1]

        def vcols(name):
            return vec[:, VEC[name][0]:VEC[name][1]]

        def mcol(v, c):
            return modc[:, v * KC + c:v * KC + c + 1]

        def free_of(n):
            who, value = FREES[n]
            return free[who], value

        def used(label, i):
            return USED[W_AT[(label, i)]]

        def released(n):
            names = {v: k for k, v in NORM.items()}
            if n not in names:
                return a_yd, n
            name = names[n]
            if name in ("final", "post2"):
                return h_upd, 8 if name == "final" else 16
            return u_t, FROM_NORM["mix1" if name == "kv" else name] + 8

        def finished(name, c):
            first = {"ffn0": "wo0", "kv": f"fo0_{FFN_G - 1}", "ffn1": "wo1", "final": f"fo1_{FFN_G - 1}", "post2": "wo2",
                     "mlp_post2": f"mout{MLP_G - 1}"}
            if name == "mix0":
                return x_in, 16
            if name in ("pre2", "mlp_pre2"):
                return h_upd, (0 if name == "pre2" else 8) + c + 1
            return free_of(FIRST[first[name]] + c)

        def left_half(ap, m):
            return ap.rearrange("p (n two m) -> p n two m", two=2, m=m)[:, :, 0, :]

        def right_half(ap, m):
            return ap.rearrange("p (n two m) -> p n two m", two=2, m=m)[:, :, 1, :]

        @block.sync
        def _(sp):
            sp.dma_start(vec[:, :], A["vec"]).then_inc(vec_in, 16)
            where = []
            w = m = 0
            for s, item in enumerate(STREAM):
                if s >= raw_ring:
                    kind, n = where[s - raw_ring]
                    sp.wait_ge(lo_done if kind == "W" else m_done, n + 1)
                if item[0] == "W":
                    src = A["wts"][W_SOURCE[w]]
                    where.append(("W", w))
                    w += 1
                else:
                    src = A["wts"][M_SOURCE + m]
                    where.append(("M", m))
                    m += 1
                sp.dma_start(raw[s % raw_ring][:, :], src).then_inc(raw_in[s % raw_ring], 16)
            sp.wait_ge(h_upd, 24)
            sp.dma_start(A["out"].rearrange("(c p) t -> p c t", p=P), H[:, :, :]).then_inc(out_done, 16)
            sp.wait_ge(out_done, 16)

        @block.gpsimd
        def _(pl):
            pl.memset(zcol[:, 0:1], 0.0).then_inc(const_ready, 1)
            pl.memset(zcol[:, 1:2], EPS).then_inc(const_ready, 1)
            pl.memset(onec[:, :], 1.0).then_inc(const_ready, 1)
            pl.memset(ones[:, :], 1.0).then_inc(const_ready, 1)
            pl.dma_start(f_w1[0:FE, :], A["filt_w1"]).then_inc(filt_in, 16)
            pl.dma_start(f_z[0:FE, :], A["filt_z"]).then_inc(filt_in, 16)
            pl.dma_start(f_w2[0:FH, :, :], A["filt_w23"]).then_inc(filt_in, 16)
            pl.dma_start(f_w4[0:FH, :], A["filt_w4"]).then_inc(filt_in, 16)
            pl.dma_start(win, A["window"]).then_inc(filt_in, 16)
            pl.dma_start(f_bias[0:1, :], A["filt_bias"]).then_inc(filt_in, 16)
            pl.dma_start(ident[:, :], A["ident"]).then_inc(filt_in, 16)
            pl.dma_start(H[:, :, :], A["x"].rearrange("(c p) t -> p c t", p=P)).then_inc(x_in, 16)
            masks = scr[:, 6:8, :].rearrange("p a b -> p (a b)")[:, 0:NLEV * P]
            pl.dma_start(masks, A["masks"]).then_inc(mask_in, 16)
            pl.wait_ge(mask_in, 16)
            pl.tensor_copy(a_mask, masks.rearrange("p (l t) -> p l t", l=NLEV)).then_inc(mask_ready, 1)
            pl.wait_ge(*finished("kv", KC - 1))
            for h in range(B_HEADS):
                if h >= 2:
                    pl.wait_ge(at_sc, 4 * (h - 1))
                pl.dma_start(b_T[:, h % 2, :], A["rel"][h]).then_inc(rel_in[h % 2], 16)
                pl.wait_ge(rel_in[h % 2], 16 * (h // 2 + 1))
                pl.memset(b_T[0:CHUNK, h % 2, SEQ - CHUNK:SEQ], MASK_VALUE).then_inc(rel_ready, 1)
            pl.wait_ge(*finished("final", KC - 1))
            pl.dma_start(m_tri, A["tri"]).then_inc(m_in, 16)
            pl.dma_start(m_sel[0:M_HEADS, :, :], A["sel"]).then_inc(m_in, 16)
            pl.wait_ge(m_in, 32)
            for h in range(M_HEADS):
                for d in range(2):
                    pl.wait_ge(ml_w, 2 * h + d + 1)
                    for i in range(TB):
                        c = m_off[d][i] + (0 if d == 0 else i * P)
                        w = m_w[:, d, c:c + P]
                        last = pl.tensor_tensor(w, w, m_tri[:, d, :], ALU.mult)
                    last.then_inc(ml_m, 1)
            pl.wait_ge(ml_y, M_HEADS)
            for o in (0, 1):
                for f in range(4):
                    if 4 * o + f >= 2:
                        pl.wait_ge(hy_y, 4 * o + f - 1)
                    pl.dma_start(h_kA[:, f % 2, :], spec_dram[o, 0, f]).then_inc(sp_in[f % 2], 16)
                    pl.dma_start(h_kB[:, f % 2, :], spec_dram[o, 1, f]).then_inc(sp_in[f % 2], 16)

        @block.tensor
        def _(pe):
            events = [0]

            def three(out, lh, ll, rh, rl, start, stop):
                pe.matmul(out, lh, rh, start=start, stop=False, skip_group_check=True)
                pe.matmul(out, lh, rl, start=False, stop=False, skip_group_check=True)
                return pe.matmul(out, ll, rh, start=False, stop=stop, skip_group_check=True)

            def complete(mm, n=None, slot=None):
                mm.then_inc(product, 1)
                events[0] += 1
                assert n is None or READY[n] == events[0], (n, READY[n], events[0])
                assert slot is None or USED[slot] == events[0], (slot, USED[slot], events[0])

            def claim(n):
                if n >= 4:
                    pe.wait_ge(*free_of(n - 4))
                return bank[n % 4]

            def weights(label, i):
                w = W_AT[(label, i)]
                pe.wait_ge(lo_done, w + 1)
                return w, w_hi[w % hi_ring], w_lo[w % hi_ring]

            def mods(w):
                for m in range(NM):
                    if M_BEFORE[m] == w:
                        pe.wait_ge(m_done, m + 1)
                        for sums, vectors in MOD_POINTS:
                            if sums == m:
                                pe.wait_ge(mod_col, vectors)
                        for j in range(2):
                            mm = pe.matmul(bank[7][:, 2 * m + j:2 * m + j + 1],
                                           macc[:, m % MRING, j * P:(j + 1) * P], onec[:, :], start=True, stop=True)
                        mm.then_inc(mod_sum, 1)

            def wait_u(count):
                pe.wait_ge(u_l, count)

            def slot_std(label, i, first, count, nout=2, hook=None):
                w, hi, lo = weights(label, i)
                banks = [claim(first + j) for j in range(nout)]
                for k in range(KC):
                    wait_u(count + k + 1)
                    for j in range(nout):
                        c = k * 256 + j * P
                        mm = three(banks[j][:, :], hi[:, c:c + P], lo[:, c:c + P], u_hi[:, k, :], u_lo[:, k, :],
                                   k == 0, k == KC - 1)
                        if k == KC - 1:
                            complete(mm, first + j, w if j == nout - 1 else None)
                    if hook:
                        hook(k)
                mods(w)

            def slot_tok(label, i, first, count, hook=None):
                w, hi, lo = weights(label, i)
                if i % 2 == 0:
                    for j in range(4):
                        claim(first + j)
                for kk in range(4):
                    k = 4 * (i % 2) + kk
                    wait_u(count + k + 1)
                    for j in range(4):
                        mm = three(bank[(first + j) % 4][:, :], u_hi[:, k, j * P:(j + 1) * P], u_lo[:, k, j * P:(j + 1) * P],
                                   hi[:, kk * 512:(kk + 1) * 512], lo[:, kk * 512:(kk + 1) * 512], k == 0, k == KC - 1)
                        if k == KC - 1:
                            complete(mm, first + j, w if j == 3 else None)
                        elif kk == 3 and j == 3:
                            complete(mm, slot=w)
                        if hook and j % 2:
                            hook(2 * kk + j // 2)
                mods(w)

            def slot_four(label, i, first, hi_src, lo_src, ready, start=True, stop=True):
                w, hi, lo = weights(label, i)
                if start:
                    for j in range(4):
                        claim(first + j)
                for k in range(4):
                    pe.wait_ge(*ready(k))
                    for j in range(4):
                        c = k * 512 + j * P
                        mm = three(bank[(first + j) % 4][:, :], hi[:, c:c + P], lo[:, c:c + P], hi_src[:, k, :], lo_src[:, k, :],
                                   start and k == 0, stop and k == 3)
                        if k == 3 and stop:
                            complete(mm, first + j, w if j == 3 and i >= 0 else None)
                        elif k == 3 and j == 3:
                            complete(mm, slot=w)
                mods(w)

            def slot_out(label, g, first, gcount):
                w, hi, lo = weights(label, g)
                for j in range(8):
                    b = claim(first + j)
                    for k in range(2):
                        pe.wait_ge(g_l, gcount + 2 * g + k + 1)
                        c = k * D + j * P
                        r = (2 * g + k + gcount) % NG
                        mm = three(b[:, :], hi[:, c:c + P], lo[:, c:c + P], g_hi[:, r, :], g_lo[:, r, :], k == 0, k == 1)
                    complete(mm, first + j, w if j == 7 else None)
                mods(w)

            def norm_cols(n, src):
                for j in range(TB):
                    mm = pe.matmul(bank[6][:, j:j + 1], src[:, j * P:(j + 1) * P], onec[:, :], start=True, stop=True)
                mm.then_inc(n_col, 1)

            def norm_bc(n):
                pe.wait_ge(n_diag, n + 1)
                pe.matmul(bank[6][:, :], ones[:, :], diag[:, :, :], start=True, stop=True).then_inc(n_bc, 1)

            def norm(name):
                n = NORM[name]
                pe.wait_ge(sq_add, 8 * (MAIN[name] + 1))
                if n:
                    pe.wait_ge(*released(n - 1))
                norm_cols(n, ssum)
                norm_bc(n)

            pe.wait_ge(filt_in, 16 * 7)
            pe.wait_ge(const_ready, 4)
            for i in range(3):
                b = claim(i)
                if i == 0:
                    mm = pe.matmul(b[0:FH, :], f_w1[0:FE, :], f_z[0:FE, :], start=True, stop=True)
                else:
                    pe.wait_ge(f_sin, i)
                    mm = pe.matmul(b[0:FH, :], f_w2[0:FH, i - 1, :], f_h[0:FH, i - 1, :], start=True, stop=True)
                complete(mm, i)
            pe.wait_ge(f_sin, 3)
            for o in (0, 1):
                for t in range(TB):
                    for d in (0, 1):
                        n = FIRST[f"taps{o}"] + 2 * t + d
                        b = claim(n)
                        c = (2 * d + o) * HW
                        complete(pe.matmul(b[:, :], f_h[0:FH, 2, t * P:(t + 1) * P], f_w4[0:FH, c:c + HW], start=True, stop=True), n)
                first = FIRST[f"spec{o}"]
                sums = (g_hi, g_lo) if o == 0 else (u_hi[:, 4:8, :], u_lo[:, 4:8, :])
                difs = (u_hi[:, 0:4, :], u_lo[:, 0:4, :]) if o == 0 else (g_hi, g_lo)
                slot_four("spec", 2 * o, first, *sums,
                          (lambda k: (g_l, k + 1)) if o == 0 else (lambda k: (u_l, 4 + k + 1)))
                w, hi, lo = weights("spec", 2 * o + 1)
                for j in range(5):
                    b = claim(first + 4 + j)
                    sh, sl = difs if j else sums
                    for k in range(4):
                        pe.wait_ge(*((u_l, k + 1) if o == 0 else (g_l, 4 + k + 1)))
                        c = k * 512 + max(j - 1, 0) * P
                        mm = three(b[:, :], hi[:, c:c + P], lo[:, c:c + P], sh[:, k, :], sl[:, k, :], k == 0, k == 3)
                    complete(mm, first + 4 + j, w if j == 4 else None)
                mods(w)

            norm("mix0")

            def gram_bank(j):
                if j >= 2:
                    who, value = gram_free(j - 2)
                    pe.wait_ge(gfree[who], value)
                return bank[4 + j % 2]

            def pairs(h, step):
                j = GRAM_PER_HEAD * h + step
                q, k = a_q[:, h % 2, :], a_k[:, h % 2, :]
                if step == 0:
                    pe.wait_ge(a_keys, h + 1)
                    pe.wait_ge(*free_of(FIRST[f"q{h}"]))
                elif step == 1:
                    pe.wait_ge(a_qf, h + 1)
                else:
                    pe.wait_ge(a_lvl, 8 * h + step - 1)
                b = gram_bank(j)
                if step <= NLEV:
                    for t in range(TB):
                        mm = pe.matmul(b[:, t * P:(t + 1) * P], k[:, t * P:(t + 1) * P], q[:, t * P:(t + 1) * P],
                                       start=True, stop=True)
                elif step == NLEV + 1:
                    for t in (0, 2):
                        mm = pe.matmul(b[:, t * P:(t + 1) * P], k[:, t * P:(t + 1) * P], q[:, (t + 1) * P:(t + 2) * P],
                                       start=True, stop=True)
                else:
                    for t in (0, 1):
                        mm = pe.matmul(b[:, t * 256:(t + 1) * 256], k[:, t * P:(t + 1) * P], q[:, 256:512],
                                       start=True, stop=True)
                mm.then_inc(gram_ready, 1)

            def head_out(h):
                if h == 0:
                    pe.wait_ge(free["act"], FREES[FIRST["v0"] + 3][1])
                if h == 4:
                    pe.wait_ge(free["act"], FREES[FIRST["v1"] + 3][1])
                pe.wait_ge(gfree["dve"], NLEV * (h + 1))
                pe.wait_ge(gfree["act"], 4 * h + 3)
                b = gram_bank(GRAM_PER_HEAD * h + 10)
                v = a_v[:, :, h * P:(h + 1) * P]
                for t in range(TB):
                    pe.matmul(b[:, t * P:(t + 1) * P], v[:, t, :], a_p[:, h % 2, t, :], start=(t == 0), stop=False,
                              skip_group_check=True)
                for t in (0, 2):
                    pe.matmul(b[:, (t + 1) * P:(t + 2) * P], v[:, t, :], a_off[:, t * P // 2:t * P // 2 + P],
                              start=False, stop=False, skip_group_check=True)
                for t in (0, 1):
                    mm = pe.matmul(b[:, 256:512], v[:, t, :], a_off[:, 256 + t * 256:512 + t * 256], start=False, stop=(t == 1),
                                   skip_group_check=True)
                mm.then_inc(gram_ready, 1)

            def head_cols(h):
                pe.wait_ge(gfree["act"], 4 * (h + 1))
                pe.wait_ge(*released(h))
                norm_cols(1 + h, sq[h % 2])

            for idx, (label, i) in enumerate(A_SLOTS):
                gram = A_GRAM.get(idx)
                nrm = A_NORM.get(idx, [])

                def hook(step, gram=gram, nrm=nrm):
                    if gram is not None:
                        pairs(gram, step)
                    if nrm and step == 1:
                        head_cols(nrm[0])
                    if nrm and step == 3:
                        norm_bc(1 + nrm[0])

                if label == "p0":
                    slot_std(label, i, FIRST[f"zf{i}"], U_MIX0, hook=hook)
                elif label == "g0":
                    slot_std(label, i, FIRST[f"g{i}"], U_MIX0, hook=hook)
                else:
                    slot_tok(label, i, FIRST[f"v{i // 2}"], U_MIX0, hook=hook)
                if gram is not None:
                    pairs(gram, 8)
                    pairs(gram, 9)
                    head_out(gram)
            for h in A_TAIL:
                head_cols(h)
                norm_bc(1 + h)
            for i in range(4):
                slot_std("wo0", i, FIRST["wo0"] + 2 * i, U_YA)

            def ffn(layer, ucount, gcount):
                for g in range(FFN_G + 1):
                    if g < FFN_G:
                        for i in (2 * g, 2 * g + 1):
                            slot_std(f"fi{layer}", i, FIRST[f"fi{layer}_{i}"], ucount)
                    if g:
                        slot_out(f"fo{layer}", g - 1, FIRST[f"fo{layer}_{g - 1}"], gcount)

            norm("ffn0")
            ffn("0", U_FFN0, G_FFN0)

            norm("kv")
            for i in range(4):
                slot_std("kk", i, FIRST["kk"] + 2 * i, U_KV)
            for i in range(4):
                slot_tok("vv", i, FIRST[f"vv{i // 2}"], U_KV)
            for i in range(4):
                slot_std("qq", i, FIRST["qq"] + 2 * i, U_MIX1)
            pe.wait_ge(free["act"], FREES[FIRST["qq"] + 7][1])

            def scores(h):
                r = (h % 2) * HD
                for j in range(TB):
                    if h:
                        pe.wait_ge(at_sc, 4 * (h - 1) + j + 1)
                    n = (j + 1) * P
                    pe.matmul(bank[j][:, 0:n], b_q[r:r + HD, h // 2, j * P:n], b_k[r:r + HD, h // 2, 0:n],
                              start=True, stop=True).then_inc(at_s, 1)

            def turn(h):
                for j in range(TB):
                    pe.wait_ge(at_p, 4 * h + j + 1)
                    n = 4 * h + j
                    if n >= 2:
                        pe.wait_ge(at_pt, n - 1)
                    for i in range(j + 1):
                        c = b_off[j] + i * P
                        mm = pe.transpose(bank[4 + j % 2][:, i * P:(i + 1) * P], b_s[h % 2][:, c:c + P], ident[:, :])
                    mm.then_inc(at_tr, 1)

            def weighted(h):
                pe.wait_ge(at_pt, 4 * (h + 1))
                r = (h % 2) * HD
                if h % 2 == 0 and h >= 4:
                    pe.wait_ge(u_l, U_O + h // 2 - 1)
                for i in range(TB):
                    mm = pe.matmul(bank[6 + h // 2 % 2][r:r + HD, i * P:SEQ], b_v[:, i, h * HD:(h + 1) * HD], b_pt[:, i, i * P:SEQ],
                                   start=(i == 0), stop=(i == 3), skip_group_check=True)
                mm.then_inc(at_o, 1)

            pe.wait_ge(mod_col, NVMOD)
            pe.wait_ge(*released(NORM["kv"]))
            scores(0)
            for h in range(B_HEADS):
                if h + 1 < B_HEADS:
                    scores(h + 1)
                if h:
                    weighted(h - 1)
                turn(h)
            weighted(B_HEADS - 1)
            for i in range(4):
                slot_std("wo1", i, FIRST["wo1"] + 2 * i, U_O)
            norm("ffn1")
            ffn("1", U_FFN1, G_FFN1)

            norm("final")
            norm("pre2")
            for i in range(4):
                slot_std("mqk", i, FIRST["mqk"] + 2 * i, U_PRE2)
            for i in range(2):
                slot_tok("mv", i, FIRST["mv"], U_PRE2)
            slot_std("mgate", 0, FIRST["mgate"], U_PRE2, nout=1)
            for i in range(2):
                slot_std("mo", i, FIRST["mo"] + 2 * i, U_PRE2)
            pe.wait_ge(mg_rows, 1)
            for what in range(2):
                for d in range(2):
                    for j in range(TB):
                        c = (what * 8 + d * TB + j) * M_HEADS
                        rows = (gs if what == 0 else gt)[0:M_HEADS, d, j * P:(j + 1) * P]
                        mm = pe.transpose(bank[7][:, c:c + M_HEADS], rows, ident[0:M_HEADS, 0:M_HEADS])
            mm.then_inc(mg_tr, 1)
            pe.wait_ge(m_in, 32)
            pe.wait_ge(mg_cc, 2)
            pe.wait_ge(free["act"], FREES[FIRST["mv"] + 3][1])
            pe.wait_ge(cv_q, 8)
            pe.wait_ge(free["act"], FREES[FIRST["mo"] + 3][1])
            for h in range(M_HEADS):
                if h:
                    pe.wait_ge(ml_h, h)
                for d in range(2):
                    pe.matmul(bank[6 + d][:, :], m_sel[0:M_HEADS, h, :], gi[0:M_HEADS, d, :],
                              start=True, stop=True).then_inc(ml_mb, 1)
                for i in range(TB):
                    n = 4 * h + i
                    if i >= 2:
                        pe.wait_ge(ml_p, 2 * (n - 1))
                    elif h:
                        pe.wait_ge(ml_nev, 2 * h)
                    pe.matmul(bank[4 + i % 2][:, :], m_qk[:, 4 + h, i * P:(i + 1) * P], m_qk[:, h, :],
                              start=True, stop=True).then_inc(ml_s, 1)
                pe.wait_ge(ml_p, 8 * (h + 1))
                for d in range(2):
                    order = range(TB) if d == 0 else range(TB - 1, -1, -1)
                    for i in order:
                        a, z = (i * P, SEQ) if d == 0 else (0, (i + 1) * P)
                        o = m_off[d][i]
                        mm = pe.matmul(bank[4 + d][:, a:z], m_v[:, i, h * P:(h + 1) * P], m_w[:, d, o:o + z - a],
                                       start=(i == order[0]), stop=(i == order[-1]), skip_group_check=True)
                    mm.then_inc(ml_num, 1)
                for d in range(2):
                    for j in range(TB):
                        src = [i for i in range(TB) if (i <= j if d == 0 else i >= j)]
                        for i in src:
                            o = m_off[d][i] + (j - i if d == 0 else j) * P
                            mm = pe.matmul(bank[6][:, d * TB + j:d * TB + j + 1], m_w[:, d, o:o + P], onec[:, :],
                                           start=(i == src[0]), stop=(i == src[-1]))
                mm.then_inc(ml_den, 1)
                for d in range(2):
                    pe.wait_ge(ml_rd, 2 * h + d + 1)
                    pe.matmul(bank[6 + d][:, :], ones[:, :], gs[:, d, :], start=True, stop=True).then_inc(ml_bc, 1)
            pe.wait_ge(ml_h, M_HEADS)
            for h in range(M_HEADS):
                pe.wait_ge(ml_sq, h + 1)
                for j in range(TB):
                    mm = pe.matmul(bank[7][:, h * TB + j:h * TB + j + 1], sq[h % 2][:, j * P:(j + 1) * P], onec[:, :],
                                   start=True, stop=True)
                mm.then_inc(ml_col, 1)
            for h in range(M_HEADS):
                pe.wait_ge(ml_diag, h + 1)
                if h:
                    pe.wait_ge(ml_y, h)
                pe.matmul(bank[6][:, :], ones[:, :], diag[:, :, :], start=True, stop=True).then_inc(ml_nbc, 1)
            for i in range(6):
                slot_std("h2", i, FIRST["h2"] + 2 * i, U_PRE2)
                for c in (2 * i - 2, 2 * i - 1):
                    if c >= 0:
                        pe.wait_ge(*free_of(FIRST["h2"] + c))
                        if c >= 2:
                            pe.wait_ge(tr_ev, c - 1)
                        elif c == 0:
                            pe.wait_ge(ml_y, 4)
                        for j in range(TB):
                            mm = pe.transpose(bank[4 + c % 2][:, j * P:(j + 1) * P], cv[:, c % 2, j * P:(j + 1) * P], ident[:, :])
                        mm.then_inc(tr_done, 1)
            for c in (10, 11):
                pe.wait_ge(*free_of(FIRST["h2"] + c))
                pe.wait_ge(tr_ev, c - 1)
                for j in range(TB):
                    mm = pe.transpose(bank[4 + c % 2][:, j * P:(j + 1) * P], cv[:, c % 2, j * P:(j + 1) * P], ident[:, :])
                mm.then_inc(tr_done, 1)
            for o in (0, 1):
                zs = lambda k, o=o: (g_l, G_Z[o] + k + 1)
                slot_four("dft", 4 * o, FIRST[f"fa{o}"], g_hi, g_lo, zs)
                slot_four("dft", 4 * o + 1, FIRST[f"fb{o}"], g_hi, g_lo, zs)
                slot_four("dft", 4 * o + 2, FIRST[f"iy{o}"], u_hi[:, 0:4, :], u_lo[:, 0:4, :],
                          lambda k, o=o: (u_l, U_Y[o] + 2 * k + 1), stop=False)
                slot_four("dft", 4 * o + 3, FIRST[f"iy{o}"], u_hi[:, 4:8, :], u_lo[:, 4:8, :],
                          lambda k, o=o: (u_l, U_Y[o] + 2 * k + 2), start=False)
            pe.wait_ge(hy_n, 4)
            for c in range(4):
                if c >= 2:
                    pe.wait_ge(hy_yf, c - 1)
                for j in range(TB):
                    mm = pe.transpose(bank[4 + c % 2][:, j * P:(j + 1) * P], h_A[:, j, c * P:(c + 1) * P], ident[:, :])
                mm.then_inc(hy_tr, 1)
            for i in range(4):
                slot_std("wo2", i, FIRST["wo2"] + 2 * i, U_MIX2)
            norm("post2")
            norm("mlp_pre2")
            for g in range(MLP_G + 1):
                if g < MLP_G:
                    slot_std("mi", g, FIRST[f"mi{g}"], U_MLP)
                if g:
                    slot_out("mout", g - 1, FIRST[f"mout{g - 1}"], G_MLP)
            norm("mlp_post2")


        @block.scalar
        def _(act):
            fed = [0]
            at_stream = [s for s, item in enumerate(STREAM) if item[0] == "W"]

            def feed(upto):
                while fed[0] <= min(upto, NW - 1):
                    w = fed[0]
                    s = at_stream[w]
                    act.wait_ge(raw_in[s % raw_ring], 16 * (s // raw_ring + 1))
                    if w >= hi_ring:
                        act.wait_ge(product, USED[w - hi_ring])
                    act.activation(w_hi[w % hi_ring][:, :], raw[s % raw_ring][:, :], ACT.Copy).then_inc(hi_done, 1)
                    fed[0] += 1

            def ahead(label, i):
                feed(W_AT[(label, i)] + hi_ring - 1)

            def read(n):
                act.wait_ge(product, READY[n])
                return bank[n % 4]

            def evacuate(n, dst, func=ACT.Copy, **kw):
                act.activation(dst, read(n)[:, :], func, **kw).then_inc(free["act"], 1)

            def squares(name, src):
                for c in range(KC):
                    act.wait_ge(*finished(name, c))
                    if 8 * MAIN[name] + c >= 2:
                        act.wait_ge(sq_add, 8 * MAIN[name] + c - 1)
                    act.activation(sq[c % 2], src[:, c, :], ACT.Square).then_inc(sq_done, 1)

            def root(n):
                act.wait_ge(n_col, n + 1)
                scale = 1.0 / P if 1 <= n <= A_HEADS else 1.0 / D
                act.activation(rt[:, 0:TB], bank[6][:, 0:TB], ACT.Sqrt, bias=zcol[:, 1:2], scale=scale).then_inc(n_root, 1)

            def split_u(name, count, gain, shift, reuse):
                fp = FROM_NORM[name]
                for c in range(KC):
                    act.wait_ge(u_t, fp + c + 1)
                    if c >= 2:
                        act.wait_ge(u_l, count + c - 1)
                    elif count:
                        act.wait_ge(u_l, count)
                    act.activation(uf[c % 2], tn[c % 2], ACT.Identity, bias=shift(c), scale=gain(c)).then_inc(u_f, 1)
                    act.wait_ge(u_f, fp + c + 1)
                    act.wait_ge(product, reuse(c))
                    act.activation(u_hi[:, c, :], uf[c % 2], ACT.Copy).then_inc(u_h, 1)

            def modulated(name, count, scale, shift, reuse):
                idx = SCALES[scale][0]
                act.wait_ge(acol_done, idx + 1)
                act.wait_ge(mod_col, shift + 1)
                split_u(name, count, lambda c: acol[:, idx * KC + c:idx * KC + c + 1], lambda c: mcol(shift, c), reuse)

            def plain(name, count, gain, reuse):
                split_u(name, count, lambda c: vcol(gain, c), lambda c: zcol[:, 0:1], reuse)

            act.wait_ge(vec_in, 16)
            act.wait_ge(const_ready, 4)
            act.activation(cact[:, :], vcols("c"), ACT.Silu).then_inc(cact_ready, 1)
            act.wait_ge(lb_d, 1)
            act.activation(lbt[:, 1, :], lbt[:, 0, :], ACT.Exp).then_inc(lb_e, 1)
            for i in range(3):
                b = read(i)
                act.activation(f_a[0:FH, 0, :], b[0:FH, :], ACT.Identity, bias=vcol("filt_b", i)[0:FH]).then_inc(free["act"], 1)
                act.wait_ge(free["act"], i + 1)
                act.activation(f_a[0:FH, 1, :], f_a[0:FH, 0, :], ACT.Identity, bias=zcol[0:FH, 0:1],
                               scale=vcol("filt_fr", i)[0:FH]).then_inc(f_arg, 1)
                act.wait_ge(f_red, i + 1)
                act.activation(f_h[0:FH, i, :], f_a[0:FH, 3, :], ACT.Sin).then_inc(f_sin, 1)
            feed(1)
            half = 0
            for o in (0, 1):
                for t in range(TB):
                    for x in (0, 1):
                        act.wait_ge(tap_done, 8 * o + 2 * t + x + 1)
                        src = tap[:, 2 * x + t % 2, :]
                        if o:
                            act.wait_ge(product, used("spec", 1))
                        if o == x:
                            act.activation(g_hi[:, t, :], src, ACT.Copy).then_inc(g_h, 1)
                        else:
                            act.activation(u_hi[:, t + 4 * o, :], src, ACT.Copy).then_inc(u_h, 1)
                first = FIRST[f"spec{o}"]
                for f in range(2 * TB):
                    if f % TB == 0:
                        ahead("spec", 2 * o + f // TB)
                    if f == TB:
                        b = read(first + TB)
                        act.activation(spec_ny[0:1, :], b[0:1, :], ACT.Copy, scale=1.0 / (2 * SEQ)).then_inc(free["act"], 1)
                        act.wait_ge(free["act"], FREES[first + TB][1])
                    n = first + f + f // TB
                    e = 8 * o + f
                    if e >= 2:
                        act.wait_ge(spec_out[e % 2], 16 * (e // 2))
                    st = spec_st[:, e % 2, :]
                    b = read(n)
                    if f % TB:
                        act.activation(st, b[:, :], ACT.Copy, scale=2.0 / (2 * SEQ)).then_inc(free["act"], 1)
                    else:
                        act.activation(st, b[:, :], ACT.Copy, scale=2.0 / (2 * SEQ)).then_inc(spec_ev, 1)
                        half += 1
                        act.wait_ge(spec_ev, half)
                        src, scale = (b[0:1, :], 1.0 / (2 * SEQ)) if f == 0 else (spec_ny[0:1, :], 1.0)
                        act.activation(st[0:1, :], src, ACT.Copy, scale=scale).then_inc(free["act"], 1)
                    act.wait_ge(free["act"], FREES[n][1])
                    act.dma_start(spec_dram[o, f // TB, f % TB], st).then_inc(spec_out[e % 2], 16)

            squares("mix0", H)
            root(0)
            modulated("mix0", U_MIX0, SC1_0, SH1_0, lambda c: used("spec", 1 if c < 4 else 3))
            act.wait_ge(spec_out[0], 16 * 8)
            act.wait_ge(spec_out[1], 16 * 8)

            def head_pairs(h):
                j = GRAM_PER_HEAD * h
                act.wait_ge(gram_ready, j + 8)
                act.wait_ge(gfree["dve"], NLEV * (h + 1))
                b = bank[4 + (j + 7) % 2]
                blocks = b[:, :].rearrange("p (t s) -> p t s", t=TB)
                act.activation(a_p[0:64, h % 2, :, 64:P], blocks[0:64, :, 64:P], ACT.Copy).then_inc(gfree["act"], 1)
                act.wait_ge(gram_ready, j + 9)
                b = bank[4 + (j + 8) % 2]
                blocks = b[:, :].rearrange("p (t two s) -> p t two s", t=2, two=2)
                act.activation(a_off[:, 0:256].rearrange("p (t s) -> p t s", t=2), blocks[:, :, 0, :], ACT.Copy).then_inc(gfree["act"], 1)
                act.wait_ge(gram_ready, j + 10)
                b = bank[4 + (j + 9) % 2]
                act.activation(a_off[:, 256:768], b[:, :], ACT.Copy).then_inc(gfree["act"], 1)
                act.wait_ge(gram_ready, j + 11)
                b = bank[4 + (j + 10) % 2]
                if h >= 2:
                    act.wait_ge(a_yd, h - 1)
                act.activation(uf[h % 2], b[:, :], ACT.Copy).then_inc(a_os, 1)
                act.wait_ge(n_col, h + 1 if h < 2 else h)
                act.activation(sq[h % 2], b[:, :], ACT.Square).then_inc(gfree["act"], 1)

            for idx, (label, i) in enumerate(A_SLOTS):
                gram = A_GRAM.get(idx)
                ahead(label, i)
                for h in A_NORM.get(idx, []):
                    root(1 + h)
                if label == "p0":
                    if i >= 1:
                        act.wait_ge(a_keys, i)
                    evacuate(FIRST[f"zf{i}"], tn[0], ACT.Sigmoid)
                    if gram is not None:
                        head_pairs(gram)
                    if i >= 2:
                        act.wait_ge(gram_ready, GRAM_PER_HEAD * (i - 2) + 10)
                    evacuate(FIRST[f"q{i}"], a_q[:, i % 2, :], ACT.Silu)
                elif label == "g0":
                    for j in (0, 1):
                        h = 2 * i + j
                        if h >= 4:
                            act.wait_ge(a_yd, h - 3)
                        evacuate(FIRST[f"g{i}"] + j, a_gate[:, h % 4, :], ACT.Silu)
                    if gram is not None:
                        head_pairs(gram)
                else:
                    if i % 2:
                        for j in range(TB):
                            evacuate(FIRST[f"v{i // 2}"] + j, a_v[:, j, (i // 2) * 512:(i // 2 + 1) * 512])
                    if gram is not None:
                        head_pairs(gram)

            def split_y(heads):
                for h in heads:
                    act.wait_ge(a_yd, h + 1)
                    act.wait_ge(product, used("g0", 3))
                    act.activation(u_hi[:, h, :], a_y[:, h, :], ACT.Copy).then_inc(u_h, 1)

            root(7)
            split_y(range(0, 6))
            root(8)
            split_y((6, 7))
            for i in range(4):
                ahead("wo0", i)

            def ffn(layer, ucount, gcount, sg):
                ahead_done = 0
                for g in range(FFN_G + 1):
                    if g < FFN_G:
                        for i in (2 * g, 2 * g + 1):
                            n = FIRST[f"fi{layer}_{i}"]
                            ahead(f"fi{layer}", i)
                            if i >= 2:
                                act.wait_ge(*free_of(FIRST[f"fi{layer}_{i - 2}"] + 1))
                            act.activation(ff_s[:, i % 2, :], read(n)[:, :], ACT.Silu).then_inc(sg_done, 1)
                            act.wait_ge(*free_of(n + 1))
                            if g >= 2:
                                act.wait_ge(product, used(f"fo{layer}", g - 2))
                            act.activation(g_hi[:, (gcount + i) % NG, :], ff_h[:, i % 2, :], ACT.Copy).then_inc(g_h, 1)
                    if g:
                        ahead(f"fo{layer}", g - 1)

            squares("ffn0", H)
            root(NORM["ffn0"])
            modulated("ffn0", U_FFN0, SC2_0, SH2_0, lambda c: used("wo0", 3))
            ffn("0", U_FFN0, G_FFN0, 0)

            squares("kv", H)
            root(NORM["kv"])
            modulated("kv", U_KV, KSC, KSH, lambda c: used("fi0", FFN_CH - 1))
            for i in range(4):
                ahead("kk", i)
                for j in (0, 1):
                    evacuate(FIRST["kk"] + 2 * i + j, b_k[:, 2 * i + j, :])
            for i in range(4):
                ahead("vv", i)
                if i % 2:
                    for j in range(TB):
                        evacuate(FIRST[f"vv{i // 2}"] + j, b_v[:, j, (i // 2) * 512:(i // 2 + 1) * 512])
            modulated("mix1", U_MIX1, SC1_1, SH1_1, lambda c: used("vv", 3))
            for i in range(4):
                ahead("qq", i)
                for j in (0, 1):
                    evacuate(FIRST["qq"] + 2 * i + j, b_q[:, 2 * i + j, :])

            def exponentials(h):
                for j in range(TB):
                    x = 4 * (h % 2) + j
                    act.wait_ge(at_mx, 4 * h + j + 1)
                    s = b_s[h % 2][:, b_off[j]:b_off[j] + (j + 1) * P]
                    act.activation(s, s, ACT.Exp, bias=b_mx[:, x:x + 1], accum_out=b_sm[:, x:x + 1]).then_inc(at_e, 1)

            exponentials(0)
            for h in range(B_HEADS):
                if h + 1 < B_HEADS:
                    exponentials(h + 1)
                if h:
                    act.wait_ge(at_o, h)
                    if h % 2 == 0:
                        pc = h // 2 - 1
                        act.wait_ge(product, used("qq", 3))
                        act.activation(u_hi[:, pc, :], bank[6 + pc % 2][:, :], ACT.Copy).then_inc(u_h, 1)
                for j in range(TB):
                    act.wait_ge(at_tr, 4 * h + j + 1)
                    b = bank[4 + j % 2][:, 0:(j + 1) * P].rearrange("p (i q) -> p i q", q=P)
                    act.activation(b_pt[:, 0:j + 1, j * P:(j + 1) * P], b, ACT.Copy).then_inc(at_pt, 1)
            act.wait_ge(at_o, B_HEADS)
            act.activation(u_hi[:, 7, :], bank[7][:, :], ACT.Copy).then_inc(u_h, 1)
            for i in range(4):
                ahead("wo1", i)
            squares("ffn1", H)
            root(NORM["ffn1"])
            modulated("ffn1", U_FFN1, SC2_1, SH2_1, lambda c: used("wo1", 3))
            ffn("1", U_FFN1, G_FFN1, FFN_CH)

            squares("final", H)
            root(NORM["final"])
            squares("pre2", H)
            root(NORM["pre2"])
            plain("pre2", U_PRE2, "pre2", lambda c: used("fi1", FFN_CH - 1))

            def middle_tap(n, c, count):
                act.activation(cv[:, count % 2, :], read(n)[:, :], ACT.Identity, bias=vcol("conv_b", c),
                               scale=vcol("conv_w", 20 + c)).then_inc(cv_y, 1)

            def query_key(c):
                act.wait_ge(*free_of(FIRST["mqk"] + c))
                act.activation(m_qk[:, c, :], cv[:, c % 2, :], ACT.Silu).then_inc(cv_q, 1)

            for i in range(4):
                ahead("mqk", i)
                for c in (2 * i, 2 * i + 1):
                    if c >= 2:
                        act.wait_ge(cv_q, c - 1)
                    middle_tap(FIRST["mqk"] + c, c, c)
                for c in (2 * i, 2 * i + 1):
                    query_key(c)
            for i in range(2):
                ahead("mv", i)
            for j in range(TB):
                evacuate(FIRST["mv"] + j, m_v[:, j, :])
            ahead("mgate", 0)
            evacuate(FIRST["mgate"], g_all, ACT.Identity, bias=vcol("b_gates"))
            for i in range(2):
                ahead("mo", i)
                for j in (0, 1):
                    evacuate(FIRST["mo"] + 2 * i + j, m_og[:, 2 * i + j, :], ACT.Sigmoid)
            act.wait_ge(mg_q, 1)
            act.activation(gt[0:M_HEADS], gt[0:M_HEADS], ACT.Exp, scale=-1.0).then_inc(mg_e, 1)
            act.wait_ge(mg_e, 1)
            act.activation(gt[0:M_HEADS], gt[0:M_HEADS], ACT.Ln, bias=onec[0:M_HEADS, 0:1]).then_inc(mg_l, 1)
            act.wait_ge(mg_tr, 1)
            act.wait_ge(mg_cc, 1)
            act.activation(m_em, bank[7][:, 32:64], ACT.Exp, scale=-1.0).then_inc(mg_cc, 1)
            for h in range(M_HEADS):
                for d in range(2):
                    act.wait_ge(ml_a, 2 * h + d + 1)
                    act.activation(m_w[:, d, :], m_w[:, d, :], ACT.Exp, scale=-1.0).then_inc(ml_w, 1)
                for d in range(2):
                    act.wait_ge(ml_num, 2 * h + d + 1)
                    if h:
                        act.wait_ge(ml_h, h)
                    act.activation(scr[:, 2 + d, :], bank[4 + d][:, :], ACT.Copy).then_inc(ml_nev, 1)
            act.wait_ge(ml_h, M_HEADS)
            for h in range(M_HEADS):
                if h >= 2:
                    act.wait_ge(ml_col, h - 1)
                act.activation(sq[h % 2], m_h[:, h, :], ACT.Square).then_inc(ml_sq, 1)
            act.wait_ge(ml_col, M_HEADS)
            act.activation(rt[:, :], bank[7][:, 0:16], ACT.Sqrt, bias=zcol[:, 1:2], scale=1.0 / P).then_inc(ml_root, 1)

            def turned(c):
                act.wait_ge(tr_done, c + 1)
                b = bank[4 + c % 2][:, :].rearrange("p (j f) -> p j f", j=TB)
                act.activation(h_tok[c // 4][:, :, (c % 4) * P:(c % 4 + 1) * P], b, ACT.Copy).then_inc(tr_ev, 1)

            for i in range(6):
                ahead("h2", i)
                for c in (2 * i, 2 * i + 1):
                    if c >= 2:
                        act.wait_ge(tr_done, c - 1)
                    middle_tap(FIRST["h2"] + c, 8 + c, c)
                    if c >= 2:
                        turned(c - 2)
            turned(10)
            turned(11)
            for o in (0, 1):
                for k in range(4):
                    if o == 0:
                        act.wait_ge(tr_ev, 4)
                    else:
                        act.wait_ge(*free_of(FIRST["iy0"] + k))
                        act.wait_ge(product, used("dft", 1))
                    act.activation(g_hi[:, k, :], h_tok[o][:, k, :], ACT.Copy).then_inc(g_h, 1)
                ahead("dft", 4 * o)
                for f in range(4):
                    if o:
                        act.wait_ge(hy_y, 4)
                    evacuate(FIRST[f"fa{o}"] + f, h_A[:, f, :])
                ahead("dft", 4 * o + 1)
                for f in range(4):
                    act.wait_ge(hy_y, 4 * o + f + 1)
                    act.wait_ge(product, used("h2", 5) if o == 0 else used("dft", 3))
                    for x in (0, 1):
                        act.activation(u_hi[:, 4 * x + f, :], h_t[:, 2 + 2 * (f % 2) + x, :], ACT.Copy).then_inc(u_h, 1)
                ahead("dft", 4 * o + 2)
                if o == 0:
                    ahead("dft", 3)
            act.wait_ge(product, used("dft", 6))
            for h in range(M_HEADS):
                act.activation(u_hi[:, h, :], m_h[:, h, :], ACT.Copy).then_inc(u_h, 1)
            ahead("dft", 7)
            for j in range(TB):
                act.wait_ge(*free_of(FIRST["iy1"] + j))
                if j >= 2:
                    act.wait_ge(hy_rs, j - 1)
                act.activation(sq[j % 2], h_tok[2][:, j, :], ACT.Square).then_inc(hy_sq, 1)
            act.wait_ge(hy_rs, TB)
            act.activation(h_r, h_m, ACT.Sqrt, bias=zcol[:, 1:2], scale=1.0 / 64).then_inc(hy_rt, 1)
            for c in range(4):
                act.wait_ge(hy_tr, c + 1)
                act.wait_ge(u_l, U_MIX2 + 4 + max(c - 1, 0))
                act.activation(uf[c % 2], bank[4 + c % 2][:, :], ACT.Identity, bias=zcol[:, 0:1],
                               scale=vcol("hyena_norm", c)).then_inc(hy_yf, 1)
                act.wait_ge(hy_yf, c + 1)
                act.wait_ge(product, used("dft", 7))
                act.activation(u_hi[:, 4 + c, :], uf[c % 2], ACT.Copy).then_inc(u_h, 1)
            for i in range(4):
                ahead("wo2", i)
            squares("post2", Facc)
            root(NORM["post2"])
            squares("mlp_pre2", H)
            root(NORM["mlp_pre2"])
            plain("mlp_pre2", U_MLP, "mlp_pre2", lambda c: used("wo2", 3))
            for g in range(MLP_G + 1):
                if g < MLP_G:
                    ahead("mi", g)
                    for i in (2 * g, 2 * g + 1):
                        n = FIRST[f"mi{g}"] + i % 2
                        if i >= 2:
                            act.wait_ge(*free_of(FIRST[f"mi{g - 1}"] + i % 2))
                        act.activation(ff_s[:, i % 2, :], read(n)[:, :], ACT.Relu).then_inc(sg_done, 1)
                        act.wait_ge(*free_of(n))
                        if g >= 2:
                            act.wait_ge(product, used("mout", g - 2))
                        act.activation(g_hi[:, (G_MLP + i) % NG, :], ff_h[:, i % 2, :], ACT.Copy).then_inc(g_h, 1)
                if g:
                    ahead("mout", g - 1)
            squares("mlp_post2", Facc)
            root(NORM["mlp_post2"])

        @block.vector
        def _(dve):
            links = [0]

            def link(ins):
                ins.then_inc(vlink, 1)
                links[0] += 1
                dve.wait_ge(vlink, links[0])

            pos, fed, summed = [0], [0], [0]

            def take_mods(point):
                sums, vectors = MOD_POINTS[point]
                dve.wait_ge(mod_sum, sums)
                for e in range(MOD_POINTS[point - 1][1] if point else 0, vectors):
                    b0 = VEC["mod_b0"][0] + e * KC
                    dve.tensor_tensor(modc[:, e * KC:(e + 1) * KC], bank[7][:, e * KC:(e + 1) * KC], vec[:, b0:b0 + KC],
                                      ALU.add).then_inc(mod_col, 1)
                    if e in SCALES:
                        idx, gain = SCALES[e]
                        dve.wait_ge(mod_col, e + 1)
                        dve.scalar_tensor_tensor(acol[:, idx * KC:(idx + 1) * KC], modc[:, e * KC:(e + 1) * KC], 1.0, vcols(gain),
                                                 ALU.add, ALU.mult).then_inc(acol_done, 1)
                dve.wait_ge(mod_col, vectors)

            def feed(upto):
                while pos[0] < len(STREAM) and not (STREAM[pos[0]][0] == "W" and fed[0] > min(upto, NW - 1)):
                    s = pos[0]
                    src = raw[s % raw_ring]
                    if STREAM[s][0] == "W":
                        w = fed[0]
                        dve.wait_ge(hi_done, w + 1)
                        dve.tensor_tensor(w_lo[w % hi_ring][:, :], src[:, :], w_hi[w % hi_ring][:, :].bitcast(F32),
                                          ALU.subtract).then_inc(lo_done, 1)
                        fed[0] += 1
                    else:
                        m = summed[0]
                        if m == 0:
                            dve.wait_ge(cact_ready, 1)
                        dve.wait_ge(raw_in[s % raw_ring], 16 * (s // raw_ring + 1))
                        if m >= MRING:
                            dve.wait_ge(mod_sum, m - MRING + 1)
                        acc = macc[:, m % MRING, :]
                        link(dve.tensor_scalar(acc, src[:, 0:256], cact[:, 0:1], None, ALU.mult))
                        for k in range(1, KC):
                            ins = dve.scalar_tensor_tensor(acc, src[:, k * 256:(k + 1) * 256], cact[:, k:k + 1], acc, ALU.mult, ALU.add)
                            if k < KC - 1:
                                link(ins)
                            else:
                                ins.then_inc(m_done, 1)
                        summed[0] += 1
                    pos[0] += 1

            def ahead(label, i):
                feed(W_AT[(label, i)] + hi_ring - 1)

            def read(n):
                dve.wait_ge(product, READY[n])
                return bank[n % 4]

            def lower_u(n, k, src):
                dve.wait_ge(u_h, n + 1)
                dve.tensor_tensor(u_lo[:, k, :], src, u_hi[:, k, :].bitcast(F32), ALU.subtract).then_inc(u_l, 1)

            def lower_g(n, src):
                dve.wait_ge(g_h, n + 1)
                dve.tensor_tensor(g_lo[:, n % NG, :], src, g_hi[:, n % NG, :].bitcast(F32), ALU.subtract).then_inc(g_l, 1)

            def sums(name):
                k = MAIN[name]
                for c in range(KC):
                    dve.wait_ge(sq_done, 8 * k + c + 1)
                    if c == 0:
                        if NORM[name]:
                            dve.wait_ge(n_col, NORM[name])
                        dve.tensor_copy(ssum, sq[0]).then_inc(sq_add, 1)
                    else:
                        dve.wait_ge(sq_add, 8 * k + c)
                        dve.tensor_tensor(ssum, ssum, sq[c % 2], ALU.add).then_inc(sq_add, 1)

            def on_diagonal(dst, col):
                return dve.tensor_tensor(dst, ident[:, :].unsqueeze(1).broadcast_to((P, TB, P)),
                                         col.unsqueeze(2).broadcast_to((P, TB, P)), ALU.mult)

            def factors(n):
                dve.wait_ge(n_root, n + 1)
                link(dve.reciprocal(rc[:, 0:TB], rt[:, 0:TB]))
                if n:
                    dve.wait_ge(n_bc, n)
                on_diagonal(diag, rc[:, 0:TB]).then_inc(n_diag, 1)

            def normalised(name, n, count):
                fp = FROM_NORM[name]
                dve.wait_ge(n_bc, n + 1)
                for c in range(KC):
                    if fp + c >= 2:
                        dve.wait_ge(u_f, fp + c - 1)
                    dve.tensor_tensor(tn[c % 2], H[:, c, :], bank[6][:, :], ALU.mult).then_inc(u_t, 1)
                    if c:
                        lower_u(count + c - 1, c - 1, uf[(c - 1) % 2])
                lower_u(count + 7, 7, uf[1])

            def residual(first, c, gate, before):
                n = FIRST[first] + c
                b = read(n)
                dve.wait_ge(*before)
                dve.scalar_tensor_tensor(H[:, c, :], b[:, :], mcol(gate, c), H[:, c, :], ALU.mult, ALU.add).then_inc(free["dve"], 1)

            dve.wait_ge(vec_in, 16)
            dve.wait_ge(const_ready, 4)
            dve.tensor_tensor(lbt[:, 0, :], vcols("a_lb"), vcols("a_lb"), ALU.subtract).then_inc(lb_d, 1)
            dve.wait_ge(lb_e, 1)
            link(dve.reciprocal(lbt[:, 2, :], lbt[:, 1, :]))
            link(dve.tensor_tensor(lbt[:, 3, :], lbt[:, 1, :], lbt[:, 2, :], ALU.mult))
            link(dve.tensor_tensor(lbt[:, 4, :], lbt[:, 3, :], lbt[:, 3, :], ALU.subtract))
            link(dve.tensor_scalar(lbt[:, 5, :], lbt[:, 4, :], -1.0, 1.0, ALU.mult, ALU.add))
            link(dve.tensor_scalar(lbt[:, 6, :], lbt[:, 5, :], -1.0, None, ALU.mult))
            for i in range(3):
                a, k, r, s = (f_a[0:FH, x, :] for x in (1, 2, 0, 3))
                dve.wait_ge(f_arg, i + 1)
                link(dve.tensor_scalar(k, a, 1.0 / TWO_PI, ROUND, ALU.mult, ALU.add))
                link(dve.tensor_scalar(k, k, -ROUND, None, ALU.add))
                link(dve.scalar_tensor_tensor(r, k, -TWO_PI_HI, a, ALU.mult, ALU.add))
                link(dve.scalar_tensor_tensor(r, k, -(TWO_PI - TWO_PI_HI), r, ALU.mult, ALU.add))
                dve.tensor_scalar(s, r, 3.1415925, -3.1415925, ALU.min, ALU.max).then_inc(f_red, 1)
            feed(1)
            dve.wait_ge(filt_in, 16 * 7)

            def lower_taps(o, t):
                for x in (0, 1):
                    src = tap[:, 2 * x + t % 2, :]
                    if o == x:
                        lower_g(4 * o + t, src)
                    else:
                        lower_u(4 * o + t, 4 * o + t, src)

            for o in (0, 1):
                for t in range(TB):
                    first = FIRST[f"taps{o}"] + 2 * t
                    for d, dst in ((0, f_tf), (1, f_tb)):
                        dve.tensor_tensor(dst, read(first + d)[:, :], win[:, t, :], ALU.mult).then_inc(free["dve"], 1)
                    dve.wait_ge(*free_of(first + 1))
                    if t == 0:
                        dve.memset(f_tb[0:1, :], 0.0)
                        link(dve.tensor_tensor(f_tf[0:1, :], f_tf[0:1, :], f_bias[0:1, o * HW:(o + 1) * HW], ALU.add))
                    dve.tensor_tensor(tap[:, t % 2, :], f_tf, f_tb, ALU.add).then_inc(tap_done, 1)
                    dve.tensor_tensor(tap[:, 2 + t % 2, :], f_tf, f_tb, ALU.subtract).then_inc(tap_done, 1)
                    dve.wait_ge(tap_done, 8 * o + 2 * t + 2)
                    if t:
                        lower_taps(o, t - 1)
                lower_taps(o, TB - 1)
                ahead("spec", 2 * o)
                ahead("spec", 2 * o + 1)

            dve.wait_ge(x_in, 16)
            dve.wait_ge(mask_ready, 1)
            sums("mix0")
            factors(0)
            take_mods(MODS_MIX0)
            normalised("mix0", 0, U_MIX0)
            dve.wait_ge(spec_out[0], 16 * 8)
            dve.wait_ge(spec_out[1], 16 * 8)
            link(dve.memset(a_p, 0.0))

            def head_keys(h):
                lb, oml, noml = (lbt[:, x, h:h + 1] for x in (4, 5, 6))
                f, k = a_tot[:, h % 2, :], a_k[:, h % 2, :]
                dve.wait_ge(*free_of(FIRST[f"zf{h}"]))
                link(dve.tensor_scalar(f, tn[0], oml, lb, ALU.mult, ALU.add))
                dve.tensor_scalar(f, f, MIN_FORGET, None, ALU.max)
                if h >= 2:
                    dve.wait_ge(gram_ready, GRAM_PER_HEAD * (h - 2) + 10)
                dve.tensor_scalar(k, tn[0], 1.0, noml, ALU.subtract, ALU.mult).then_inc(a_keys, 1)

            def level(h, step):
                f, k, q = a_tot[:, h % 2, :], a_k[:, h % 2, :], a_q[:, h % 2, :]
                j = GRAM_PER_HEAD * h + step
                dve.wait_ge(gram_ready, j + 1)
                if step == 0:
                    dve.wait_ge(a_keys, h + 1)
                    dve.tensor_tensor(q, q, f, ALU.mult).then_inc(a_qf, 1)
                    dve.wait_ge(a_qf, h + 1)
                else:
                    m = 1 << (step - 1)
                    n = SEQ // m
                    tot = f if m == 1 else ssum[:, SEQ - 2 * n:SEQ - n]
                    even, odd = (tot.rearrange("p (n two) -> p n two", two=2)[:, :, x] for x in (0, 1))
                    if step > 1:
                        dve.wait_ge(a_lvl, 8 * h + step - 1)
                    if m < 128:
                        dve.tensor_tensor(ssum[:, SEQ - n:SEQ - n // 2], even, odd, ALU.mult)
                    spread = (P, n // 2, m)
                    dve.tensor_tensor(right_half(q, m), right_half(q, m), even.unsqueeze(2).broadcast_to(spread), ALU.mult)
                    dve.tensor_tensor(left_half(k, m), left_half(k, m), odd.unsqueeze(2).broadcast_to(spread), ALU.mult).then_inc(a_lvl, 1)
                if step < NLEV:
                    b = bank[4 + j % 2]
                    if step:
                        dve.wait_ge(gfree["dve"], NLEV * h + step)
                    dve.copy_predicated(a_p[:, h % 2, :, :], a_mask[:, step, :].unsqueeze(1).broadcast_to((P, TB, P)),
                                        b[:, :].rearrange("p (t s) -> p t s", t=TB)).then_inc(gfree["dve"], 1)

            def head_result(h):
                dve.wait_ge(a_os, h + 1)
                dve.wait_ge(*free_of(FIRST[f"g{h // 2}"] + h % 2))
                link(dve.tensor_tensor(uf[h % 2], uf[h % 2], a_gate[:, h % 4, :], ALU.mult))
                dve.wait_ge(n_bc, 1 + h + 1)
                dve.scalar_tensor_tensor(a_y[:, h, :], bank[6][:, :], vcol("a_out_norm"), uf[h % 2], ALU.mult, ALU.mult).then_inc(a_yd, 1)

            for idx, (label, i) in enumerate(A_SLOTS):
                gram = A_GRAM.get(idx)
                nrm = A_NORM.get(idx, [])
                ahead(label, i)
                for step in range(9):
                    if gram is not None:
                        level(gram, step)
                    if step == 2:
                        for h in nrm:
                            factors(1 + h)
                    if step == 5:
                        for h in nrm:
                            head_result(h)
                if label == "p0":
                    head_keys(i)
            factors(7)
            take_mods(MODS_WO0)
            head_result(6)
            factors(8)
            for h in range(6):
                lower_u(U_YA + h, h, a_y[:, h, :])
            head_result(7)
            for h in (6, 7):
                lower_u(U_YA + h, h, a_y[:, h, :])
            
            for i in range(4):
                ahead("wo0", i)
                for c in (2 * i, 2 * i + 1):
                    residual("wo0", c, G1_0, (x_in, 16))

            def ffn(layer, gcount, sg, gate, mixer):
                def lag(i):
                    if i >= 0:
                        lower_g(gcount + i, ff_h[:, i % 2, :])

                for g in range(FFN_G + 1):
                    if g < FFN_G:
                        for i in (2 * g, 2 * g + 1):
                            n = FIRST[f"fi{layer}_{i}"]
                            ahead(f"fi{layer}", i)
                            lag(i - 1)
                            dve.wait_ge(sg_done, sg + i + 1)
                            dve.tensor_tensor(ff_h[:, i % 2, :], ff_s[:, i % 2, :], read(n + 1)[:, :], ALU.mult).then_inc(free["dve"], 1)
                    else:
                        lag(FFN_CH - 1)
                    if g:
                        ahead(f"fo{layer}", g - 1)
                        if g == 1 and layer == "0":
                            take_mods(MODS_OUT0)
                        for c in range(KC):
                            before = FIRST[mixer] if g == 1 else FIRST[f"fo{layer}_{g - 2}"]
                            residual(f"fo{layer}_{g - 1}", c, gate, free_of(before + c))

            sums("ffn0")
            factors(NORM["ffn0"])
            take_mods(MODS_FFN0)
            normalised("ffn0", NORM["ffn0"], U_FFN0)
            ffn("0", G_FFN0, 0, G2_0, "wo0")

            sums("kv")
            factors(NORM["kv"])
            take_mods(MODS_ALL)
            normalised("kv", NORM["kv"], U_KV)
            for label in ("kk", "vv"):
                for i in range(4):
                    ahead(label, i)
            normalised("mix1", NORM["kv"], U_MIX1)
            for i in range(4):
                ahead("qq", i)

            def scores(h):
                dve.wait_ge(rel_ready, h + 1)
                if h >= 2:
                    dve.wait_ge(at_tr, 4 * (h - 1))
                for j in range(TB):
                    n = (j + 1) * P
                    dve.wait_ge(at_s, 4 * h + j + 1)
                    y = SEQ - P - j * P
                    dve.scalar_tensor_tensor(b_s[h % 2][:, b_off[j]:b_off[j] + n], bank[j][:, 0:n], HD ** -0.5,
                                             b_T[:, h % 2, y:y + n], ALU.mult, ALU.add).then_inc(at_sc, 1)
                for j in range(TB):
                    x = 4 * (h % 2) + j
                    dve.wait_ge(at_sc, 4 * h + j + 1)
                    dve.tensor_reduce(b_mx[:, x:x + 1], b_s[h % 2][:, b_off[j]:b_off[j] + (j + 1) * P], AX.X, ALU.max,
                                      negate=True).then_inc(at_mx, 1)

            def normalise(h):
                x = 4 * (h % 2)
                dve.wait_ge(at_e, 4 * (h + 1))
                link(dve.reciprocal(b_rc[:, x:x + 4], b_sm[:, x:x + 4]))
                for j in range(TB):
                    s = b_s[h % 2][:, b_off[j]:b_off[j] + (j + 1) * P]
                    dve.tensor_scalar(s, s, b_rc[:, x + j:x + j + 1], None, ALU.mult).then_inc(at_p, 1)

            scores(0)
            for h in range(B_HEADS):
                if h + 1 < B_HEADS:
                    scores(h + 1)
                normalise(h)
                if h and h % 2 == 0:
                    lower_u(U_O + h // 2 - 1, h // 2 - 1, bank[6 + (h // 2 - 1) % 2][:, :])
            lower_u(U_O + 7, 7, bank[7][:, :])
            for i in range(4):
                ahead("wo1", i)
                for c in (2 * i, 2 * i + 1):
                    residual("wo1", c, G1_1, free_of(FIRST[f"fo0_{FFN_G - 1}"] + c))
            sums("ffn1")
            factors(NORM["ffn1"])
            normalised("ffn1", NORM["ffn1"], U_FFN1)
            ffn("1", G_FFN1, FFN_CH, G2_1, "wo1")

            sums("final")
            factors(NORM["final"])
            dve.wait_ge(n_bc, NORM["final"] + 1)
            for c in range(KC):
                dve.scalar_tensor_tensor(H[:, c, :], bank[6][:, :], vcol("final_norm", c), H[:, c, :], ALU.mult, ALU.mult).then_inc(h_upd, 1)
            dve.wait_ge(h_upd, KC)
            sums("pre2")
            factors(NORM["pre2"])
            normalised("pre2", NORM["pre2"], U_PRE2)

            def outer_taps(n, c, count):
                y, b = cv[:, count % 2, :], read(n)
                w = VEC["conv_w"][0]
                dve.wait_ge(cv_y, count + 1)
                link(dve.scalar_tensor_tensor(y[:, 1:SEQ], b[:, 0:SEQ - 1], vec[:, w + c:w + c + 1], y[:, 1:SEQ], ALU.mult, ALU.add))
                dve.scalar_tensor_tensor(y[:, 0:SEQ - 1], b[:, 1:SEQ], vec[:, w + 40 + c:w + 40 + c + 1], y[:, 0:SEQ - 1],
                                         ALU.mult, ALU.add).then_inc(free["dve"], 1)

            for i in range(4):
                ahead("mqk", i)
                for c in (2 * i, 2 * i + 1):
                    outer_taps(FIRST["mqk"] + c, c, c)
            for i in range(2):
                ahead("mv", i)
            ahead("mgate", 0)
            dve.wait_ge(*free_of(FIRST["mgate"]))
            for d in range(2):
                dve.tensor_copy(gi[0:M_HEADS, d, :], g_all[64 * d:64 * d + M_HEADS, :])
                link(dve.tensor_copy(gf[0:M_HEADS, d, :], g_all[64 * d + 32:64 * d + 32 + M_HEADS, :]))
            rows = [x[0:M_HEADS] for x in (gi, gf, gt, gs)]
            r_i, r_f, r_t, r_s = rows
            dve.scalar_tensor_tensor(r_t, r_f, -1.0, r_f, ALU.mult, ALU.max).then_inc(mg_q, 1)
            for i in range(2):
                ahead("mo", i)
            dve.wait_ge(mg_l, 1)

            def order(ap, d):
                return ap[:, d, :] if d == 0 else ap[:, d, ::-1]

            link(dve.scalar_tensor_tensor(r_f, r_f, 0.0, r_t, ALU.min, ALU.subtract))
            for d in range(2):
                ins = dve.tensor_tensor_scan(order(r_t, d), order(r_f, d), order(r_f, d), 0.0, ALU.add, ALU.bypass)
            link(ins)
            link(dve.tensor_tensor(r_s, r_i, r_t, ALU.subtract))
            for d in range(2):
                ins = dve.tensor_tensor_scan(order(r_i, d), order(r_s, d), order(r_s, d), 0.0, ALU.max, ALU.max)
            link(ins)
            dve.tensor_tensor(r_t, r_t, r_i, ALU.add).then_inc(mg_rows, 1)
            dve.wait_ge(mg_tr, 1)
            dve.tensor_copy(m_cc, bank[7][:, 0:32]).then_inc(mg_cc, 1)
            dve.wait_ge(mg_cc, 2)
            em = m_em.rearrange("p (x h) -> p x h", h=M_HEADS)
            for h in range(M_HEADS):
                if h:
                    dve.wait_ge(ml_den, h)
                for d in range(2):
                    dve.wait_ge(ml_mb, 2 * h + d + 1)
                    for i in range(TB):
                        a, z = (i * P, SEQ) if d == 0 else (0, (i + 1) * P)
                        o = m_off[d][i]
                        x = (d * TB + i) * M_HEADS + h
                        ins = dve.tensor_scalar(m_w[:, d, o:o + z - a], bank[6 + d][:, a:z], m_cc[:, x:x + 1], 0.0,
                                                ALU.subtract, ALU.max)
                    ins.then_inc(ml_a, 1)
                dve.wait_ge(ml_m, 2 * h + 2)
                for i in range(TB):
                    dve.wait_ge(ml_s, 4 * h + i + 1)
                    for d in range(2):
                        a, z = (i * P, SEQ) if d == 0 else (0, (i + 1) * P)
                        o = m_off[d][i]
                        dve.scalar_tensor_tensor(m_w[:, d, o:o + z - a], bank[4 + i % 2][:, a:z], P ** -0.5, m_w[:, d, o:o + z - a],
                                                 ALU.mult, ALU.mult).then_inc(ml_p, 1)
                dve.wait_ge(ml_den, h + 1)
                link(dve.tensor_tensor(m_dd[:, 0:8], bank[6][:, 0:8], em[:, :, h], ALU.max))
                link(dve.scalar_tensor_tensor(m_dd[:, 0:8], bank[6][:, 0:8], -1.0, m_dd[:, 0:8], ALU.mult, ALU.max))
                link(dve.reciprocal(m_rd[:, 0:8], m_dd[:, 0:8]))
                for d in range(2):
                    on_diagonal(gs[:, d, :].rearrange("p (a b) -> p a b", a=TB), m_rd[:, d * TB:(d + 1) * TB]).then_inc(ml_rd, 1)
                dve.wait_ge(ml_nev, 2 * h + 2)
                dve.wait_ge(ml_bc, 2 * h + 2)
                dve.tensor_tensor(m_h[:, h, :], scr[:, 2, :], bank[6][:, :], ALU.mult)
                link(dve.tensor_tensor(scr[:, 3, :], scr[:, 3, :], bank[7][:, :], ALU.mult))
                link(dve.tensor_tensor(m_h[:, h, :], m_h[:, h, :], scr[:, 3, :], ALU.add))
                dve.wait_ge(*free_of(FIRST["mo"] + 3))
                dve.tensor_tensor(m_h[:, h, :], m_h[:, h, :], m_og[:, h, :], ALU.mult).then_inc(ml_h, 1)
            dve.wait_ge(ml_root, 1)
            link(dve.reciprocal(rc[:, :], rt[:, :]))
            for h in range(M_HEADS):
                if h:
                    dve.wait_ge(ml_nbc, h)
                on_diagonal(diag, rc[:, h * TB:(h + 1) * TB]).then_inc(ml_diag, 1)
                dve.wait_ge(ml_nbc, h + 1)
                dve.scalar_tensor_tensor(m_h[:, h, :], bank[6][:, :], vcol("mlstm_norm", h), m_h[:, h, :], ALU.mult, ALU.mult).then_inc(ml_y, 1)

            for i in range(6):
                ahead("h2", i)
                for c in (2 * i, 2 * i + 1):
                    outer_taps(FIRST["h2"] + c, 8 + c, 8 + c)
            for o in (0, 1):
                for k in range(4):
                    lower_g(G_Z[o] + k, h_tok[o][:, k, :])
                ahead("dft", 4 * o)
                ahead("dft", 4 * o + 1)
                for f in range(4):
                    e = 4 * o + f
                    dve.wait_ge(sp_in[f % 2], 32 * (e // 2 + 1))
                    dve.wait_ge(*free_of(FIRST[f"fa{o}"] + f))
                    b = read(FIRST[f"fb{o}"] + f)
                    za, ka, kb = h_A[:, f, :], h_kA[:, f % 2, :], h_kB[:, f % 2, :]
                    aa, bb, ab, ba = h_t[:, 0, :], h_t[:, 1, :], scr[:, 6, :], scr[:, 7, :]
                    yc, ys = h_t[:, 2 + 2 * (f % 2), :], h_t[:, 3 + 2 * (f % 2), :]
                    dve.tensor_tensor(aa, za, ka, ALU.mult)
                    dve.tensor_tensor(bb, b[:, :], kb, ALU.mult)
                    dve.tensor_tensor(ab, za, kb, ALU.mult)
                    dve.tensor_tensor(ba, b[:, :], ka, ALU.mult).then_inc(free["dve"], 1)
                    dve.wait_ge(*free_of(FIRST[f"fb{o}"] + f))
                    dve.tensor_tensor(yc, aa, bb, ALU.subtract)
                    ins = dve.tensor_tensor(ys, ab, ba, ALU.add)
                    if f == 0:
                        link(ins)
                        dve.tensor_copy(yc[0:1, :], aa[0:1, :])
                        ins = dve.tensor_copy(ys[0:1, :], bb[0:1, :])
                    ins.then_inc(hy_y, 1)
                    dve.wait_ge(hy_y, e + 1)
                    lower_u(U_Y[o] + 2 * f, f, yc)
                    lower_u(U_Y[o] + 2 * f + 1, 4 + f, ys)
                ahead("dft", 4 * o + 2)
                ahead("dft", 4 * o + 3)
                for j in range(TB):
                    x = h_tok[o + 1][:, j, :]
                    dve.tensor_tensor(x, read(FIRST[f"iy{o}"] + j)[:, :], x, ALU.mult).then_inc(free["dve"], 1)
            groups = h_m.rearrange("p (j g) -> p j g", j=TB)
            for h in range(M_HEADS):
                lower_u(U_MIX2 + h, h, m_h[:, h, :])
            for j in range(TB):
                dve.wait_ge(hy_sq, j + 1)
                dve.tensor_reduce(groups[:, j, :], sq[j % 2].rearrange("p (g e) -> p g e", g=8), AX.X, ALU.add).then_inc(hy_rs, 1)
            dve.wait_ge(hy_rt, 1)
            link(dve.reciprocal(h_m, h_r))
            for j in range(TB):
                dve.tensor_tensor(h_A[:, j, :].rearrange("p (g e) -> p g e", g=8),
                                  h_tok[2][:, j, :].rearrange("p (g e) -> p g e", g=8),
                                  groups[:, j, :].unsqueeze(2).broadcast_to((P, 8, 64)), ALU.mult).then_inc(hy_n, 1)
            for c in range(4):
                lower_u(U_MIX2 + 4 + c, 4 + c, uf[c % 2])
            for i in range(4):
                ahead("wo2", i)
                for c in (2 * i, 2 * i + 1):
                    dve.tensor_copy(Facc[:, c, :], read(FIRST["wo2"] + c)[:, :]).then_inc(free["dve"], 1)

            def add_normalised(name, gain, before):
                dve.wait_ge(n_bc, NORM[name] + 1)
                for c in range(KC):
                    link(dve.scalar_tensor_tensor(tn[c % 2], Facc[:, c, :], vcol(gain, c), bank[6][:, :], ALU.mult, ALU.mult))
                    dve.tensor_tensor(H[:, c, :], H[:, c, :], tn[c % 2], ALU.add).then_inc(h_upd, 1)
                dve.wait_ge(h_upd, before + KC)

            sums("post2")
            factors(NORM["post2"])
            add_normalised("post2", "post2", 8)
            sums("mlp_pre2")
            factors(NORM["mlp_pre2"])
            normalised("mlp_pre2", NORM["mlp_pre2"], U_MLP)

            def lag(i):
                if i >= 0:
                    lower_g(G_MLP + i, ff_h[:, i % 2, :])

            for g in range(MLP_G + 1):
                if g < MLP_G:
                    ahead("mi", g)
                    for i in (2 * g, 2 * g + 1):
                        lag(i - 1)
                        dve.wait_ge(sg_done, 2 * FFN_CH + i + 1)
                        n = FIRST[f"mi{g}"] + i % 2
                        dve.tensor_tensor(ff_h[:, i % 2, :], ff_s[:, i % 2, :], read(n)[:, :], ALU.mult).then_inc(free["dve"], 1)
                else:
                    lag(MLP_CH - 1)
                if g:
                    ahead("mout", g - 1)
                    for c in range(KC):
                        b = read(FIRST[f"mout{g - 1}"] + c)
                        if g == 1:
                            dve.tensor_copy(Facc[:, c, :], b[:, :]).then_inc(free["dve"], 1)
                        else:
                            dve.wait_ge(*free_of(FIRST[f"mout{g - 2}"] + c))
                            dve.tensor_tensor(Facc[:, c, :], Facc[:, c, :], b[:, :], ALU.add).then_inc(free["dve"], 1)
            sums("mlp_post2")
            factors(NORM["mlp_post2"])
            add_normalised("mlp_post2", "mlp_post2", 16)


def table_of(label, i):
    if label == "spec":
        return "cos" if i % 2 == 0 else "sin"
    if label == "dft":
        return ("cos", "sin", "cos", "sin_back")[i % 4]
    return None


W_SOURCE, PACKED = [], []
for _item in W_LIST:
    _key = table_of(*_item) or _item
    if _key not in PACKED:
        PACKED.append(_key)
    W_SOURCE.append(PACKED.index(_key))
M_SOURCE = len(PACKED)


def pack(inputs):
    import numpy as np
    f = {k: np.asarray(v) for k, v in inputs.items()}
    out = {}

    def columns(v):
        return np.asarray(v).reshape(-1, P).T

    table = np.zeros((P, NVEC), np.float32)

    def put(name, value):
        a, z = VEC[name]
        assert value.shape[1] == z - a, name
        table[:value.shape[0], a:z] = value

    put("c", columns(f["c"]))
    put("mod_b0", columns(f["mod_b"][0]))
    put("kv_mod_b", columns(f["kv_mod_b"]))
    put("mod_b1", columns(f["mod_b"][1]))
    for i in (0, 1):
        put(f"norm_mix{i}", columns(f["norm_mix"][i]))
        put(f"norm_ffn{i}", columns(f["norm_ffn"][i]))
    for name, key in (("kv_norm", "kv_norm"), ("final_norm", "final_norm"), ("pre2", "norm_mix_pre_2"),
                      ("post2", "norm_mix_post_2"), ("mlp_pre2", "norm_mlp_pre_2"), ("mlp_post2", "norm_mlp_post_2"),
                      ("a_lb", "a_lb"), ("a_out_norm", "a_out_norm"), ("conv_w", "conv_w_2"), ("conv_b", "conv_b_2"),
                      ("mlstm_norm", "mlstm_norm_w_2"), ("hyena_norm", "hyena_norm_w_2")):
        put(name, columns(f[key]))
    put("filt_b", np.stack([f["filt_b1_2"], f["filt_b2_2"], f["filt_b3_2"]], 1))
    put("filt_fr", f["filt_freq_2"].T)
    gate_rows = np.array([32 * q + h for q in range(4) for h in range(M_HEADS)])
    gates = np.zeros((P, 1), np.float32)
    gates[gate_rows, 0] = f["b_gates_2"]
    put("b_gates", gates)
    out["vec"] = table

    t = np.arange(SEQ)
    turns = (t[:, None] * t[None, :]) % (2 * SEQ)
    cos = np.cos(np.pi * turns / SEQ)
    sin = np.sin(np.pi * turns / SEQ)
    sign = 1.0 - 2.0 * (t % 2)
    forward, back = sin.copy(), sin.copy()
    forward[:, 0] = sign
    back[0, :] = sign
    tables = {"cos": cos, "sin": forward, "sin_back": back}

    def by_rows(w, k):
        return w.reshape(k, P, -1).transpose(1, 0, 2)

    w_in, w2 = f["a_w_in"][0], f["w_in_2"]
    kv = f["kv_w"]

    def std(w, i):
        return by_rows(w[:, 256 * i:256 * (i + 1)], KC)

    def pair(w, a, b):
        return by_rows(np.concatenate([w[:, a:a + P], w[:, b:b + P]], 1), KC)

    def tok(w, i):
        n, half = divmod(i, 2)
        return by_rows(w[half * 512:(half + 1) * 512, n * 512:(n + 1) * 512], 4)

    def rows(w, g):
        return by_rows(w[256 * g:256 * (g + 1)], 2)

    def slot(label, i):
        if label == "v0":
            return tok(w_in[:, 2048:3072], i)
        if label == "p0":
            return pair(w_in, 1024 + P * i, P * i)
        if label == "g0":
            return std(w_in[:, 3072:], i)
        if label[:2] in ("fi", "fo"):
            n = int(label[2])
            return pair(f["ffn_w_in"][n], P * i, FFN + P * i) if label[1] == "i" else rows(f["ffn_w_out"][n], i)
        if label == "vv":
            return tok(kv[:, D:], i)
        if label == "mv":
            return tok(w2[:, 2560:3072], i)
        if label == "mgate":
            w = np.zeros((D, 256), np.float32)
            w[:, gate_rows] = w2[:, 3584:3600]
            return by_rows(w, KC)
        if label == "mout":
            return rows(f["w_mlp_out_2"], i)
        src = {"wo0": f["a_w_out"][0], "kk": kv[:, :D], "qq": f["b_w_q"][0], "wo1": f["b_w_o"][0], "mqk": w2, "mo": w2[:, 3072:],
               "h2": w2[:, 1024:], "wo2": f["w_out_2"], "mi": f["w_mlp_in_2"]}[label]
        return std(src, i)

    wts = np.empty((M_SOURCE + NM, P, SLOT), np.float32)
    for n, key in enumerate(PACKED):
        wts[n] = (by_rows(tables[key], TB) if isinstance(key, str) else slot(*key)).reshape(P, SLOT)
    mods = [f["mod_w"][0], f["kv_mod_w"], f["mod_w"][1]]
    n = M_SOURCE
    for w in mods:
        for i in range(w.shape[1] // 256):
            wts[n] = std(w, i).reshape(P, SLOT)
            n += 1
    out["wts"] = wts

    out["filt_w1"] = f["filt_w1_2"]
    f32 = np.float32
    bands = (FE - 1) // 2
    lin = np.linspace(0.0, 1.0, SEQ, dtype=f32)[:, None]
    ang = f32(TWO_PI) * np.arange(SEQ, dtype=f32)[:, None] / f32(SEQ)
    fq = np.linspace(1e-4, bands - 1, bands, dtype=f32)[None, :]
    out["filt_z"] = np.concatenate([lin, np.cos(fq * ang), -np.sin(fq * ang)], -1).T.astype(f32)
    out["filt_w23"] = np.stack([f["filt_w2_2"], f["filt_w3_2"]], 1)
    out["filt_w4"] = f["filt_w4_2"]
    deltas = np.linspace(math.log(1e-2) / 1.5, math.log(1e-2) / 0.3, HW, dtype=f32)
    out["window"] = by_rows(np.exp(-lin * np.abs(deltas)[None, :]).astype(f32), TB)
    out["filt_bias"] = f["filt_bias_2"].reshape(1, 2 * HW)
    out["ident"] = np.eye(P, dtype=f32)
    out["x"] = f["x"][0].T
    s, q = np.arange(P)[:, None], np.arange(P)[None, :]
    masks = [s == q]
    for lev in range(NLEV - 1):
        m = 1 << lev
        masks.append((s // (2 * m) == q // (2 * m)) & (s // m % 2 == 0) & (q // m % 2 == 1))
    out["masks"] = np.stack(masks, 1).reshape(P, NLEV * P).astype(f32)
    far = np.clip(np.arange(SEQ)[None, :] - np.arange(SEQ - P, SEQ)[:, None], -REL_CLIP, CHUNK - 1) + REL_CLIP
    out["rel"] = f["b_rel_bias"][0][far].transpose(2, 0, 1)
    out["tri"] = np.stack([q >= s, q <= s], 1).astype(f32)
    out["sel"] = np.stack([np.repeat((np.arange(M_HEADS) == h)[:, None], P, 1) for h in range(M_HEADS)], 1).astype(f32)
    return out


def kernel(**inputs):
    import numpy as np
    import concourse.bacc as bacc
    from concourse.bass_utils import run_bass_kernel_spmd

    nc = bacc.Bacc("TRN2", target_bir_lowering=False, num_devices=1)
    arrays, A = {}, {}
    for name, a in pack(inputs).items():
        a = np.ascontiguousarray(a)
        arrays[f"in_{name}"] = a
        A[name] = nc.dram_tensor(f"in_{name}", a.shape, mybir.dt.from_np(a.dtype), kind="ExternalInput").ap()
    A["out"] = nc.dram_tensor("out", (D, SEQ), F32, kind="ExternalOutput").ap()
    build(nc, A)
    r = run_bass_kernel_spmd(nc, [arrays], core_ids=[0])
    return np.ascontiguousarray(r.results[0]["out"].T).reshape(1, SEQ, D)
```

```python
import math
from contextlib import ExitStack

import concourse.bass as bass
from concourse import mybir

F32 = mybir.dt.float32
F32R = mybir.dt.float32r
I8 = mybir.dt.int8
ALU = mybir.AluOpType
ACT = mybir.ActivationFunctionType
AX = mybir.AxisListType

P = 128
SEQ = 512
D = 1024
KC = D // P
TB = SEQ // P
SLOT = 2048
A_HEADS = 8
B_HEADS = 16
HD = D // B_HEADS
REL_CLIP = 256
CHUNK = 64
FFN = 2816
M_HEADS = 4
HW = 512
D_FF = 4 * D
FH = 64
FE = 33
NLEV = 7
EPS = 1e-6
MIN_FORGET = 1e-30
MASK_VALUE = -1e30
TWO_PI = 2 * math.pi
TWO_PI_HI = 6.28125
ROUND = 1.5 * 2.0**23

VEC_ORDER = [("c", 8), ("mod_b0", 48), ("kv_mod_b", 16), ("mod_b1", 48), ("norm_mix0", 8), ("norm_mix1", 8),
             ("norm_ffn0", 8), ("norm_ffn1", 8), ("kv_norm", 8), ("final_norm", 8), ("pre2", 8), ("post2", 8),
             ("mlp_pre2", 8), ("mlp_post2", 8), ("a_lb", 8), ("a_out_norm", 1), ("conv_w", 60), ("conv_b", 20),
             ("mlstm_norm", 4), ("hyena_norm", 4), ("filt_b", 3), ("filt_fr", 3), ("b_gates", 1)]
VEC = {}
_at = 0
for _n, _w in VEC_ORDER:
    VEC[_n] = (_at, _at + _w)
    _at += _w
NVEC = _at

FFN_CH = FFN // P
MLP_CH = D_FF // P
FFN_G = FFN_CH // 2
MLP_G = MLP_CH // 2


def plan_stream():
    s = []

    def w(label, n, mods=0):
        for i in range(n):
            s.append(("W", label, i))
            s.extend([("M",)] * mods)

    def one(label, i, mods=0):
        s.append(("W", label, i))
        s.extend([("M",)] * mods)

    s.extend([("M",)] * 5)
    one("spec", 0, 1)
    one("spec", 1, 2)
    one("spec", 2)
    one("spec", 3)
    for label, i in A_SLOTS:
        one(label, i, 2 if label == "v0" else 1 if label == "g0" else 0)
    w("wo0", 4, 1)
    left = [32]

    def ffn(layer):
        def put(label, i):
            m = 1 if layer == "0" and left[0] else 0
            left[0] -= m
            one(label + layer, i, m)
        for g in range(FFN_G + 1):
            if g < FFN_G:
                put("fi", 2 * g)
                put("fi", 2 * g + 1)
            if g:
                put("fo", g - 1)

    ffn("0")
    for x in ("kk", "vv", "qq", "wo1"):
        w(x, 4)
    ffn("1")
    w("mgate", 1)
    w("mqk", 4)
    w("mv", 2)
    w("mo", 2)
    w("h2", 6)
    w("dft", 8)
    w("wo2", 4)
    for g in range(MLP_G + 1):
        if g < MLP_G:
            one("mi", g)
        if g:
            one("mout", g - 1)
    return s


A_SLOTS = [("p0", 0), ("p0", 1), ("v0", 0), ("v0", 1), ("p0", 2), ("g0", 0), ("p0", 3), ("p0", 4), ("v0", 2), ("v0", 3),
           ("p0", 5), ("p0", 6), ("g0", 1), ("p0", 7), ("g0", 2), ("g0", 3)]
HOOKS = 8
PAIR_STEPS = 10
HEAD_START = [16, 35, 46, 58, 70, 90, 101, 114, 125]


def plan_heads():
    at = {}
    for h in range(A_HEADS):
        first, gap = HEAD_START[h], HEAD_START[h + 1] - HEAD_START[h]
        for i in range(PAIR_STEPS + 1):
            at.setdefault(first + i * gap // (PAIR_STEPS + 1), []).append(("pair", h, i) if i < PAIR_STEPS else ("out", h, 0))
        out = first + PAIR_STEPS * gap // (PAIR_STEPS + 1)
        for later, kind in ((2, "columns"), (3, "diagonal"), (4, "spread"), (6, "result")):
            at.setdefault(out + later, []).append((kind, h, 0))
    return at


A_EVENTS = plan_heads()
A_PLACES = HOOKS * len(A_SLOTS)
A_LATE = [e for x in sorted(A_EVENTS) if x >= A_PLACES for e in A_EVENTS[x]]


def events_at(idx, hook):
    return A_EVENTS.get(idx * HOOKS + hook, [])


STREAM = plan_stream()
W_AT, W_LIST, M_BEFORE = {}, [], []
for _s in STREAM:
    if _s[0] == "W":
        W_AT[_s[1:]] = len(W_LIST)
        W_LIST.append(_s[1:])
    else:
        M_BEFORE.append(len(W_LIST))
W_STREAM = [s for s, item in enumerate(STREAM) if item[0] == "W"]
M_STREAM = [s for s, item in enumerate(STREAM) if item[0] == "M"]
NW = len(W_LIST)
NM = len(M_BEFORE)
M_START = 3
NVMOD = NM // 4
(SH1_0, SC1_0, G1_0, SH2_0, SC2_0, G2_0, KSH, KSC, SH1_1, SC1_1, G1_1, SH2_1, SC2_1, G2_1) = range(14)
SCALES = {SC1_0: (0, "norm_mix0"), SC2_0: (1, "norm_ffn0"), KSC: (2, "kv_norm"), SC1_1: (3, "norm_mix1"), SC2_1: (4, "norm_ffn1")}


MODS_MIX0, MODS_WO0, MODS_FFN0, MODS_OUT0, MODS_ALL = range(5)
MOD_POINTS = [(sum(b <= w for b in M_BEFORE), v) for w, v in (
    (W_AT[("spec", 3)], 2), (W_AT[("g0", 3)], 4), (W_AT[("wo0", 3)], 5), (W_AT[("fo0", 0)] - 1, 6), (NW, NVMOD))]


def plan_outputs():
    first, ready, frees, used = {}, [], [], {}
    count = {"act": 0, "dve": 0}
    events = [0]

    def out(label, n, who, share=1, slots=()):
        first.setdefault(label, len(ready))
        for i in range(n):
            if i % share == 0:
                count[who] += 1
            frees.append((who, count[who]))
            events[0] += 1
            ready.append(events[0])
            if slots and (i + 1) % (n // len(slots)) == 0:
                used[W_AT[slots[(i + 1) // (n // len(slots)) - 1]]] = events[0]

    def part(slot):
        events[0] += 1
        used[W_AT[slot]] = events[0]

    out("filt", 3, "act")
    for o in (0, 1):
        out(f"taps{o}", 2 * TB, "dve")
        out(f"spec{o}", 4, "act", slots=[("spec", 2 * o)])
        out(f"spec{o}", 5, "act", slots=[("spec", 2 * o + 1)])
    for label, i in A_SLOTS:
        if label == "p0":
            out(f"zf{i}", 1, "act")
            out(f"q{i}", 1, "act", slots=[(label, i)])
        elif label == "g0":
            out(f"g{i}", 2, "act", slots=[(label, i)])
        elif i % 2 == 0:
            part((label, i))
        else:
            out(f"v{i // 2}", 4, "act", slots=[(label, i)])
    out("wo0", 8, "dve", slots=[("wo0", i) for i in range(4)])

    def ffn(layer):
        for g in range(FFN_G + 1):
            if g < FFN_G:
                for i in (2 * g, 2 * g + 1):
                    out(f"fi{layer}_{i}", 2, "dve", 2, [(f"fi{layer}", i)])
            if g:
                out(f"fo{layer}_{g - 1}", 8, "dve", 1, [(f"fo{layer}", g - 1)])

    ffn("0")
    out("kk", 8, "act", slots=[("kk", i) for i in range(4)])
    for i in (0, 1):
        part(("vv", 2 * i))
        out(f"vv{i}", 4, "act", slots=[("vv", 2 * i + 1)])
    out("qq", 8, "act", slots=[("qq", i) for i in range(4)])
    out("wo1", 8, "dve", slots=[("wo1", i) for i in range(4)])
    ffn("1")
    out("mgate", 1, "act", slots=[("mgate", 0)])
    out("mqk", 8, "dve", slots=[("mqk", i) for i in range(4)])
    part(("mv", 0))
    out("mv", 4, "act", slots=[("mv", 1)])
    out("mo", 4, "act", slots=[("mo", 0), ("mo", 1)])
    out("h2", 12, "dve", slots=[("h2", i) for i in range(6)])
    for o in (0, 1):
        for f in range(4):
            out(f"fa{o}_{f}", 1, "act", slots=[("dft", 4 * o)] if f == 3 else ())
            out(f"fb{o}_{f}", 1, "dve", slots=[("dft", 4 * o + 1)] if f == 3 else ())
        part(("dft", 4 * o + 2))
        out(f"iy{o}", 4, "dve", slots=[("dft", 4 * o + 3)])
    out("wo2", 8, "dve", slots=[("wo2", i) for i in range(4)])
    for g in range(MLP_G + 1):
        if g < MLP_G:
            out(f"mi{g}", 2, "dve", 1, [("mi", g)])
        if g:
            out(f"mout{g - 1}", 8, "dve", 1, [("mout", g - 1)])
    return first, ready, frees, used


FIRST, READY, FREES, USED = plan_outputs()

GRAM_PER_HEAD = 11


def gram_free(j):
    h, i = divmod(j, GRAM_PER_HEAD)
    return ("dve", NLEV * h + i + 1) if i < NLEV else ("act", (GRAM_PER_HEAD - NLEV) * h + i - NLEV + 1)


NORM = {"mix0": 0, "ffn0": 9, "kv": 10, "ffn1": 11, "final": 12, "pre2": 13, "post2": 14, "mlp_pre2": 15, "mlp_post2": 16}
MAIN = {"mix0": 0, "ffn0": 1, "kv": 2, "ffn1": 3, "final": 4, "pre2": 5, "post2": 6, "mlp_pre2": 7, "mlp_post2": 8}
U_SPEC, U_MIX0, U_YA, U_FFN0, U_KV, U_MIX1, U_O, U_FFN1, U_PRE2 = 0, 8, 16, 24, 32, 40, 48, 56, 64
U_Y = [72, 80]
U_MIX2, U_MLP = 88, 96
G_SPEC, G_FFN0, G_FFN1 = 0, 8, 8 + FFN_CH
G_Z = [8 + 2 * FFN_CH, 12 + 2 * FFN_CH]
G_MLP = 16 + 2 * FFN_CH
NG = 4
MRING = 6
FROM_NORM = {"mix0": 0, "ffn0": 8, "kv": 16, "mix1": 24, "ffn1": 32, "pre2": 40, "mlp_pre2": 48}


def build(nc, A, stop=None):
    hi_ring, raw_ring = 2, 3
    ctx = ExitStack()
    with ctx:
        def sb(name, shape, dt=F32):
            return ctx.enter_context(nc.sbuf_tensor(name, shape, dt))

        def sem(name):
            return ctx.enter_context(nc.semaphore(name))

        bank = [ctx.enter_context(nc.psum_tensor(f"bank{i}", [P, SEQ], F32)) for i in range(8)]

        raw = [sb(f"raw{i}", [P, SLOT]) for i in range(raw_ring)]
        w_hi = [sb(f"w_hi{i}", [P, SLOT], F32R) for i in range(hi_ring)]
        w_lo = [sb(f"w_lo{i}", [P, SLOT], F32R) for i in range(hi_ring)]
        u_hi = sb("u_hi", [P, KC, SEQ], F32R)
        u_lo = sb("u_lo", [P, KC, SEQ], F32R)
        g_hi = sb("g_hi", [P, NG, SEQ], F32R)
        g_lo = sb("g_lo", [P, NG, SEQ], F32R)
        H = sb("H", [P, KC, SEQ])
        vec = sb("vec", [P, NVEC])
        modc = sb("modc", [P, NVMOD * KC])
        macc = sb("macc", [P, MRING, 256])
        acol = sb("acol", [P, 5 * KC])
        cact = sb("cact", [P, KC])
        zcol = sb("zcol", [P, 2])
        onec = sb("onec", [P, 1])
        ident = sb("ident", [P, P])
        ones = sb("ones", [P, P])
        lbt = sb("lbt", [P, 7, KC])
        rt = sb("rt", [P, 16])
        rc = sb("rc", [P, 16])
        scr = sb("scr", [P, 8, SEQ])
        sq = [scr[:, 0, :], scr[:, 1, :]]
        tn = [scr[:, 2 + x, :] for x in range(4)]
        uf = [scr[:, 4, :], scr[:, 5, :]]
        ssum = scr[:, 6, :]
        diag = scr[:, 7, :].rearrange("p (a b) -> p a b", a=TB)
        pool_words = 15700
        pool = sb("pool", [P, pool_words])

        class Arena:
            def __init__(self, at=0):
                self.at = at

            def __call__(self, words):
                a = self.at
                self.at += words
                assert self.at <= pool_words, self.at
                return pool[:, a:a + words]

        def view(ap, *dims):
            letters = "abcd"[:len(dims)]
            return ap.rearrange(f"p ({' '.join(letters)}) -> p {' '.join(letters)}", **dict(zip(letters, dims)))

        ar = Arena()
        f_w1 = ar(FH)
        f_w2 = view(ar(2 * FH), 2, FH)
        f_w4 = ar(4 * HW)
        f_z = ar(SEQ)
        f_h = view(ar(3 * SEQ), 3, SEQ)
        f_a = view(ar(4 * SEQ), 4, SEQ)
        f_bias = ar(2 * HW)
        win = view(ar(TB * HW), TB, HW)
        tap = view(ar(4 * HW), 4, HW)
        spec_st = view(ar(2 * HW), 2, HW)
        spec_ny = ar(HW)
        f_tf, f_tb = scr[:, 0, :], scr[:, 1, :]
        masks = ar(NLEV * P)
        ar = Arena()
        a_v = view(ar(TB * D), TB, D)
        a_y = view(ar(KC * SEQ), KC, SEQ)
        a_gate = view(ar(4 * SEQ), 4, SEQ)
        a_q = view(ar(2 * SEQ), 2, SEQ)
        a_k = view(ar(2 * SEQ), 2, SEQ)
        a_tot = view(ar(2 * SEQ), 2, SEQ)
        a_p = view(ar(2 * SEQ), 2, TB, P)
        a_off = ar(6 * P)
        a_mask = ar(NLEV * P // 4).bitcast(I8).rearrange("p (l t) -> p l t", l=NLEV)
        zf = scr[:, 2, :]
        ar = Arena()
        ff_s = view(ar(2 * SEQ), 2, SEQ)
        ff_h = view(ar(2 * SEQ), 2, SEQ)
        Facc = view(ar(KC * SEQ), KC, SEQ)
        ar = Arena()
        b_k = view(ar(KC * SEQ), KC, SEQ)
        b_q = view(ar(KC * SEQ), KC, SEQ)
        b_v = view(ar(TB * D), TB, D)
        b_T = view(ar(2 * SEQ), 2, SEQ)
        b_off = [0, 128, 384, 768]
        b_s = [ar(1280), scr[:, 4:7, :].rearrange("p a b -> p (a b)")[:, 0:1280]]
        b_pt = scr[:, 0:4, :]
        b_mx = ar(8)
        b_sm = ar(8)
        b_rc = ar(8)
        b_dg = view(ar(2 * TB * P), 2, TB, P)
        ar = Arena()
        m_qk = view(ar(8 * SEQ), 8, SEQ)
        m_h = m_qk[:, 0:M_HEADS, :]
        m_v = view(ar(TB * HW), TB, HW)
        m_og = view(ar(M_HEADS * SEQ), M_HEADS, SEQ)
        m_w = view(ar(4 * 1280), 4, 1280)
        m_tri = view(ar(2 * P), 2, P)
        m_sel = view(ar(M_HEADS * P), M_HEADS, P)
        cv = view(ar(2 * SEQ), 2, SEQ)
        m_cc = ar(32)
        m_em = ar(32)
        m_rd = ar(16)
        m_dd = ar(16)
        g_all = cv[:, 1, :]
        gi = scr[:, 0:2, :]
        gf = scr[:, 2:4, :]
        gt = scr[:, 4:6, :]
        gs = scr[:, 6:8, :]
        m_sum = scr[:, 4:6, :]
        m_dg = [scr[:, x, :].rearrange("p (a b) -> p a b", a=TB) for x in (2, 3, 6, 7)]
        m_off = [[0, 512, 896, 1152], [0, 128, 384, 768]]
        ar = Arena(M_HEADS * SEQ)
        h_tok = [view(ar(TB * HW), TB, HW) for _ in range(3)]
        h_A = view(ar(TB * HW), TB, HW)
        h_kA = view(ar(2 * HW), 2, HW)
        h_kB = view(ar(2 * HW), 2, HW)
        h_r = ar(32)
        h_m = ar(32)
        h_t = scr[:, 0:6, :]
        spec_dram = nc.dram_tensor("spectra", (2, 2, TB, P, HW), F32).ap()

        raw_in = [sem(f"raw_in{i}") for i in range(raw_ring)]
        hi_done, lo_done, m_done = sem("hi_done"), sem("lo_done"), sem("m_done")
        mod_sum, mod_col, acol_done = sem("mod_sum"), sem("mod_col"), sem("acol_done")
        product = sem("product")
        free = {"act": sem("out_free_act"), "dve": sem("out_free_dve")}
        gfree = {"act": sem("gram_free_act"), "dve": sem("gram_free_dve")}
        gram_ready = sem("gram_ready")
        vec_in, filt_in, x_in, mask_in, rel_in0, rel_in1, m_in = (
            sem(x) for x in ("vec_in", "filt_in", "x_in", "mask_in", "rel_in0", "rel_in1", "m_in"))
        rel_in = [rel_in0, rel_in1]
        rel_ready, mask_ready, taps_in = sem("rel_ready"), sem("mask_ready"), sem("taps_in")
        const_ready = sem("const_ready")
        cact_ready, lb_d, lb_e = sem("cact_ready"), sem("lb_d"), sem("lb_e")
        h_upd, sq_done, sq_add = sem("h_upd"), sem("sq_done"), sem("sq_add")
        n_col, n_root, n_diag, n_bc = (sem(x) for x in ("n_col", "n_root", "n_diag", "n_bc"))
        u_t, u_h, u_l = sem("u_t"), sem("u_h"), sem("u_l")
        g_h, g_l = sem("g_h"), sem("g_l")
        vlink, plink = sem("vlink"), sem("plink")
        f_arg, f_red, f_sin, tap_done = sem("f_arg"), sem("f_red"), sem("f_sin"), sem("tap_done")
        spec_ev = sem("spec_ev")
        spec_out = [sem("spec_out0"), sem("spec_out1")]
        a_keys, a_qf, a_lvl, a_os, a_yd, a_gated = (sem(x) for x in ("a_keys", "a_qf", "a_lvl", "a_os", "a_yd", "a_gated"))
        sg_done = sem("sg_done")
        at_s, at_sc, at_mx, at_e, at_p, at_tr, at_pt, at_o = (
            sem(x) for x in ("at_s", "at_sc", "at_mx", "at_e", "at_p", "at_tr", "at_pt", "at_o"))
        cv_y, cv_q, tr_done, tr_ev = (sem(x) for x in ("cv_y", "cv_q", "tr_done", "tr_ev"))
        ml_sum = sem("ml_sum")
        mg_q, mg_e, mg_l, mg_rows, mg_tr, mg_cc = (
            sem(x) for x in ("mg_q", "mg_e", "mg_l", "mg_rows", "mg_tr", "mg_cc"))
        ml_mb, ml_a, ml_w, ml_m, ml_s, ml_p, ml_num, ml_nev, ml_den, ml_rd, ml_bc, ml_h, ml_sq = (
            sem(x) for x in ("ml_mb", "ml_a", "ml_w", "ml_m", "ml_s", "ml_p", "ml_num", "ml_nev", "ml_den", "ml_rd",
                             "ml_bc", "ml_h", "ml_sq"))
        ml_col, ml_root, ml_diag, ml_nbc, ml_y = (sem(x) for x in ("ml_col", "ml_root", "ml_diag", "ml_nbc", "ml_y"))
        sp_in = [sem("sp_in0"), sem("sp_in1")]
        hy_y, hy_sq, hy_rs, hy_rt, hy_n, hy_tr, hy_yf = (
            sem(x) for x in ("hy_y", "hy_sq", "hy_rs", "hy_rt", "hy_n", "hy_tr", "hy_yf"))
        out_done = sem("out_done")
        block = ctx.enter_context(nc.Block())

        def vcol(name, i=0):
            return vec[:, VEC[name][0] + i:VEC[name][0] + i + 1]

        def vcols(name):
            return vec[:, VEC[name][0]:VEC[name][1]]

        def mcol(v, c):
            return modc[:, v * KC + c:v * KC + c + 1]

        def free_of(n):
            who, value = FREES[n]
            return free[who], value

        def used(label, i):
            return USED[W_AT[(label, i)]]

        def released(n):
            names = {v: k for k, v in NORM.items()}
            if n not in names:
                return a_yd, n
            name = names[n]
            if name in ("final", "post2"):
                return h_upd, 8 if name == "final" else 16
            return u_t, FROM_NORM["mix1" if name == "kv" else name] + 8

        def finished(name, c):
            first = {"ffn0": "wo0", "kv": f"fo0_{FFN_G - 1}", "ffn1": "wo1", "final": f"fo1_{FFN_G - 1}", "post2": "wo2",
                     "mlp_post2": f"mout{MLP_G - 1}"}
            if name == "mix0":
                return x_in, 16
            if name in ("pre2", "mlp_pre2"):
                return h_upd, (0 if name == "pre2" else 8) + c + 1
            return free_of(FIRST[first[name]] + c)

        def left_half(ap, m):
            return ap.rearrange("p (n two m) -> p n two m", two=2, m=m)[:, :, 0, :]

        def right_half(ap, m):
            return ap.rearrange("p (n two m) -> p n two m", two=2, m=m)[:, :, 1, :]

        @block.sync
        def _(sp):
            sp.dma_start(vec[:, :], A["vec"]).then_inc(vec_in, 16)
            sp.dma_start(f_w1[0:FE, :], A["filt_w1"]).then_inc(filt_in, 16)
            sp.dma_start(f_z[0:FE, :], A["filt_z"]).then_inc(filt_in, 16)
            sp.dma_start(f_w2[0:FH, :, :], A["filt_w23"]).then_inc(filt_in, 16)
            where = []
            w = m = 0
            for s, item in enumerate(STREAM):
                if s >= raw_ring:
                    kind, n = where[s - raw_ring]
                    sp.wait_ge(lo_done if kind == "W" else m_done, n + 1)
                if item[0] == "W":
                    src = A["wts"][W_SOURCE[w]]
                    where.append(("W", w))
                    w += 1
                else:
                    src = A["wts"][M_SOURCE + m]
                    where.append(("M", m))
                    m += 1
                sp.dma_start(raw[s % raw_ring][:, :], src).then_inc(raw_in[s % raw_ring], 16)
            sp.wait_ge(h_upd, 24)
            sp.dma_start(A["out"].rearrange("(c p) t -> p c t", p=P), H[:, :, :]).then_inc(out_done, 16)
            sp.wait_ge(out_done, 16)

        @block.gpsimd
        def _(pl):
            links = [0]

            def link(ins):
                ins.then_inc(plink, 1)
                links[0] += 1
                pl.wait_ge(plink, links[0])

            def sum_mods():
                pl.wait_ge(m_done, M_START)
                for m in range(M_START, NM):
                    s = M_STREAM[m]
                    src = raw[s % raw_ring]
                    pl.wait_ge(raw_in[s % raw_ring], 16 * (s // raw_ring + 1))
                    chunks = src[:, :].rearrange("p (k c) -> p k c", k=KC)
                    link(pl.tensor_tensor(chunks, chunks, cact[:, :].unsqueeze(2).broadcast_to((P, KC, 256)), ALU.mult))
                    link(pl.tensor_tensor(src[:, 0:1024], src[:, 0:1024], src[:, 1024:2048], ALU.add))
                    link(pl.tensor_tensor(src[:, 0:512], src[:, 0:512], src[:, 512:1024], ALU.add))
                    if m >= MRING:
                        pl.wait_ge(mod_sum, m - MRING + 1)
                    pl.tensor_tensor(macc[:, m % MRING, :], src[:, 0:256], src[:, 256:512], ALU.add).then_inc(m_done, 1)

            pl.memset(zcol[:, 0:1], 0.0).then_inc(const_ready, 1)
            pl.memset(zcol[:, 1:2], EPS).then_inc(const_ready, 1)
            pl.memset(onec[:, :], 1.0).then_inc(const_ready, 1)
            pl.memset(ones[:, :], 1.0).then_inc(const_ready, 1)
            pl.dma_start(f_w4[0:FH, :], A["filt_w4"]).then_inc(taps_in, 16)
            pl.dma_start(win, A["window"]).then_inc(taps_in, 16)
            pl.dma_start(f_bias[0:1, :], A["filt_bias"]).then_inc(taps_in, 16)
            pl.dma_start(ident[:, :], A["ident"]).then_inc(taps_in, 16)
            pl.dma_start(masks, A["masks"]).then_inc(mask_in, 16)
            pl.wait_ge(mask_in, 16)
            pl.tensor_copy(a_mask, masks.rearrange("p (l t) -> p l t", l=NLEV)).then_inc(mask_ready, 1)
            sum_mods()
            pl.wait_ge(*finished("kv", KC - 1))
            for h in range(B_HEADS + 1):
                if h < B_HEADS:
                    if h >= 2:
                        pl.wait_ge(at_sc, 4 * (h - 1))
                    pl.dma_start(b_T[:, h % 2, :], A["rel"][h]).then_inc(rel_in[h % 2], 16)
                if h:
                    g = h - 1
                    pl.wait_ge(rel_in[g % 2], 16 * (g // 2 + 1))
                    pl.memset(b_T[0:CHUNK, g % 2, SEQ - CHUNK:SEQ], MASK_VALUE).then_inc(rel_ready, 1)
            pl.wait_ge(*finished("final", KC - 1))
            pl.dma_start(m_tri, A["tri"]).then_inc(m_in, 16)
            pl.dma_start(m_sel[0:M_HEADS, :, :], A["sel"]).then_inc(m_in, 16)
            pl.wait_ge(m_in, 32)

            def mask_of(h):
                for d in range(2):
                    pl.wait_ge(ml_w, 2 * h + d + 1)
                    for i in range(TB):
                        c = m_off[d][i] + (0 if d == 0 else i * P)
                        w = m_w[:, 2 * (h % 2) + d, c:c + P]
                        last = pl.tensor_tensor(w, w, m_tri[:, d, :], ALU.mult)
                    last.then_inc(ml_m, 1)

            mask_of(0)
            for h in range(M_HEADS):
                pl.wait_ge(ml_p, 8 * (h + 1))
                if h:
                    pl.wait_ge(ml_den, h)
                for d in range(2):
                    blocks = [m_w[:, 2 * (h % 2) + d, m_off[d][i]:] for i in range(TB)]
                    total = m_sum[:, d, :]
                    if d == 0:
                        pl.tensor_copy(total[:, 0:P], blocks[0][:, 0:P])
                        link(pl.tensor_tensor(total[:, P:SEQ], blocks[0][:, P:SEQ], blocks[1][:, 0:SEQ - P], ALU.add))
                        link(pl.tensor_tensor(total[:, 2 * P:SEQ], total[:, 2 * P:SEQ], blocks[2][:, 0:2 * P], ALU.add))
                        ins = pl.tensor_tensor(total[:, 3 * P:SEQ], total[:, 3 * P:SEQ], blocks[3][:, 0:P], ALU.add)
                    else:
                        pl.tensor_copy(total[:, 3 * P:SEQ], blocks[3][:, 3 * P:SEQ])
                        link(pl.tensor_tensor(total[:, 0:3 * P], blocks[3][:, 0:3 * P], blocks[2][:, 0:3 * P], ALU.add))
                        link(pl.tensor_tensor(total[:, 0:2 * P], total[:, 0:2 * P], blocks[1][:, 0:2 * P], ALU.add))
                        ins = pl.tensor_tensor(total[:, 0:P], total[:, 0:P], blocks[0][:, 0:P], ALU.add)
                    ins.then_inc(ml_sum, 1)
                if h + 1 < M_HEADS:
                    mask_of(h + 1)
            pl.wait_ge(ml_y, M_HEADS)
            for o in (0, 1):
                for f in range(4):
                    if 4 * o + f >= 2:
                        pl.wait_ge(hy_y, 4 * o + f - 1)
                    pl.dma_start(h_kA[:, f % 2, :], spec_dram[o, 0, f]).then_inc(sp_in[f % 2], 16)
                    pl.dma_start(h_kB[:, f % 2, :], spec_dram[o, 1, f]).then_inc(sp_in[f % 2], 16)

        @block.tensor
        def _(pe):
            events = [0]

            def three(out, lh, ll, rh, rl, start, stop):
                pe.matmul(out, lh, rh, start=start, stop=False, skip_group_check=True)
                pe.matmul(out, lh, rl, start=False, stop=False, skip_group_check=True)
                return pe.matmul(out, ll, rh, start=False, stop=stop, skip_group_check=True)

            def complete(mm, n=None, slot=None):
                mm.then_inc(product, 1)
                events[0] += 1
                assert n is None or READY[n] == events[0], (n, READY[n], events[0])
                assert slot is None or USED[slot] == events[0], (slot, USED[slot], events[0])

            def claim(n):
                if n >= 4:
                    pe.wait_ge(*free_of(n - 4))
                return bank[n % 4]

            def weights(label, i):
                w = W_AT[(label, i)]
                pe.wait_ge(lo_done, w + 1)
                return w, w_hi[w % hi_ring], w_lo[w % hi_ring]

            def mods(w):
                for m in range(NM):
                    if M_BEFORE[m] == w:
                        pe.wait_ge(m_done, m + 1)
                        for sums, vectors in MOD_POINTS:
                            if sums == m:
                                pe.wait_ge(mod_col, vectors)
                        for j in range(2):
                            mm = pe.matmul(bank[7][:, 2 * m + j:2 * m + j + 1],
                                           macc[:, m % MRING, j * P:(j + 1) * P], onec[:, :], start=True, stop=True)
                        mm.then_inc(mod_sum, 1)

            def wait_u(count):
                pe.wait_ge(u_l, count)

            def slot_std(label, i, first, count, nout=2, hook=None):
                w, hi, lo = weights(label, i)
                banks = [claim(first + j) for j in range(nout)]
                for k in range(KC):
                    wait_u(count + k + 1)
                    for j in range(nout):
                        c = k * 256 + j * P
                        mm = three(banks[j][:, :], hi[:, c:c + P], lo[:, c:c + P], u_hi[:, k, :], u_lo[:, k, :],
                                   k == 0, k == KC - 1)
                        if k == KC - 1:
                            complete(mm, first + j, w if j == nout - 1 else None)
                    if hook:
                        hook(k)
                mods(w)

            def slot_tok(label, i, first, count, hook=None):
                w, hi, lo = weights(label, i)
                for kk in range(4):
                    k = 4 * (i % 2) + kk
                    wait_u(count + k + 1)
                    for j in range(4):
                        if k == 0:
                            claim(first + j)
                        mm = three(bank[(first + j) % 4][:, :], u_hi[:, k, j * P:(j + 1) * P], u_lo[:, k, j * P:(j + 1) * P],
                                   hi[:, kk * 512:(kk + 1) * 512], lo[:, kk * 512:(kk + 1) * 512], k == 0, k == KC - 1)
                        if k == KC - 1:
                            complete(mm, first + j, w if j == 3 else None)
                        elif kk == 3 and j == 3:
                            complete(mm, slot=w)
                        if hook and j % 2:
                            hook(2 * kk + j // 2)
                mods(w)

            def slot_four(label, i, first, hi_src, lo_src, ready, start=True, stop=True):
                w, hi, lo = weights(label, i)
                if start:
                    for j in range(4):
                        claim(first + j)
                for k in range(4):
                    pe.wait_ge(*ready(k))
                    for j in range(4):
                        c = k * 512 + j * P
                        mm = three(bank[(first + j) % 4][:, :], hi[:, c:c + P], lo[:, c:c + P], hi_src[:, k, :], lo_src[:, k, :],
                                   start and k == 0, stop and k == 3)
                        if k == 3 and stop:
                            complete(mm, first + j, w if j == 3 and i >= 0 else None)
                        elif k == 3 and j == 3:
                            complete(mm, slot=w)
                mods(w)

            def slot_out(label, g, first, gcount):
                w, hi, lo = weights(label, g)
                for j in range(8):
                    b = claim(first + j)
                    for k in range(2):
                        pe.wait_ge(g_l, gcount + 2 * g + k + 1)
                        c = k * D + j * P
                        r = (2 * g + k + gcount) % NG
                        mm = three(b[:, :], hi[:, c:c + P], lo[:, c:c + P], g_hi[:, r, :], g_lo[:, r, :], k == 0, k == 1)
                    complete(mm, first + j, w if j == 7 else None)
                mods(w)

            def norm_cols(n, src):
                for j in range(TB):
                    mm = pe.matmul(bank[6][:, j:j + 1], src[:, j * P:(j + 1) * P], onec[:, :], start=True, stop=True)
                mm.then_inc(n_col, 1)

            def norm_bc(n):
                pe.wait_ge(n_diag, n + 1)
                pe.matmul(bank[6][:, :], ones[:, :], diag[:, :, :], start=True, stop=True).then_inc(n_bc, 1)

            def norm(name):
                n = NORM[name]
                pe.wait_ge(sq_add, 8 * (MAIN[name] + 1))
                if n:
                    pe.wait_ge(*released(n - 1))
                norm_cols(n, ssum)
                norm_bc(n)

            pe.wait_ge(filt_in, 16 * 3)
            pe.wait_ge(const_ready, 4)
            for i in range(3):
                b = claim(i)
                if i == 0:
                    mm = pe.matmul(b[0:FH, :], f_w1[0:FE, :], f_z[0:FE, :], start=True, stop=True)
                else:
                    pe.wait_ge(f_sin, i)
                    mm = pe.matmul(b[0:FH, :], f_w2[0:FH, i - 1, :], f_h[0:FH, i - 1, :], start=True, stop=True)
                complete(mm, i)
            pe.wait_ge(f_sin, 3)
            pe.wait_ge(taps_in, 16 * 4)
            for o in (0, 1):
                for t in range(TB):
                    for d in (0, 1):
                        n = FIRST[f"taps{o}"] + 2 * t + d
                        b = claim(n)
                        c = (2 * d + o) * HW
                        complete(pe.matmul(b[:, :], f_h[0:FH, 2, t * P:(t + 1) * P], f_w4[0:FH, c:c + HW], start=True, stop=True), n)
                first = FIRST[f"spec{o}"]
                sums = (g_hi, g_lo) if o == 0 else (u_hi[:, 4:8, :], u_lo[:, 4:8, :])
                difs = (u_hi[:, 0:4, :], u_lo[:, 0:4, :]) if o == 0 else (g_hi, g_lo)
                slot_four("spec", 2 * o, first, *sums,
                          (lambda k: (g_l, k + 1)) if o == 0 else (lambda k: (u_l, 4 + k + 1)))
                if o == 0:
                    pe.wait_ge(sq_add, 8)
                    norm_cols(0, ssum)
                w, hi, lo = weights("spec", 2 * o + 1)
                for j in range(5):
                    b = claim(first + 4 + j)
                    sh, sl = difs if j else sums
                    for k in range(4):
                        pe.wait_ge(*((u_l, k + 1) if o == 0 else (g_l, 4 + k + 1)))
                        c = k * 512 + max(j - 1, 0) * P
                        mm = three(b[:, :], hi[:, c:c + P], lo[:, c:c + P], sh[:, k, :], sl[:, k, :], k == 0, k == 3)
                    complete(mm, first + 4 + j, w if j == 4 else None)
                mods(w)
                if o == 0:
                    norm_bc(0)


            def gram_bank(j):
                if j >= 2:
                    who, value = gram_free(j - 2)
                    pe.wait_ge(gfree[who], value)
                return bank[4 + j % 2]

            def pairs(h, step):
                j = GRAM_PER_HEAD * h + step
                q, k = a_q[:, h % 2, :], a_k[:, h % 2, :]
                if step == 0:
                    pe.wait_ge(a_keys, h + 1)
                    pe.wait_ge(*free_of(FIRST[f"q{h}"]))
                elif step == 1:
                    pe.wait_ge(a_qf, h + 1)
                else:
                    pe.wait_ge(a_lvl, 8 * h + step - 1)
                b = gram_bank(j)
                if step <= NLEV:
                    for t in range(TB):
                        mm = pe.matmul(b[:, t * P:(t + 1) * P], k[:, t * P:(t + 1) * P], q[:, t * P:(t + 1) * P],
                                       start=True, stop=True)
                elif step == NLEV + 1:
                    for t in (0, 2):
                        mm = pe.matmul(b[:, t * P:(t + 1) * P], k[:, t * P:(t + 1) * P], q[:, (t + 1) * P:(t + 2) * P],
                                       start=True, stop=True)
                else:
                    for t in (0, 1):
                        mm = pe.matmul(b[:, t * 256:(t + 1) * 256], k[:, t * P:(t + 1) * P], q[:, 256:512],
                                       start=True, stop=True)
                mm.then_inc(gram_ready, 1)

            def head_out(h):
                if h == 0:
                    pe.wait_ge(free["act"], FREES[FIRST["v0"] + 3][1])
                if h == 4:
                    pe.wait_ge(free["act"], FREES[FIRST["v1"] + 3][1])
                pe.wait_ge(gfree["dve"], NLEV * (h + 1))
                pe.wait_ge(gfree["act"], 4 * h + 3)
                b = gram_bank(GRAM_PER_HEAD * h + 10)
                v = a_v[:, :, h * P:(h + 1) * P]
                for t in range(TB):
                    pe.matmul(b[:, t * P:(t + 1) * P], v[:, t, :], a_p[:, h % 2, t, :], start=(t == 0), stop=False,
                              skip_group_check=True)
                for t in (0, 2):
                    pe.matmul(b[:, (t + 1) * P:(t + 2) * P], v[:, t, :], a_off[:, t * P // 2:t * P // 2 + P],
                              start=False, stop=False, skip_group_check=True)
                for t in (0, 1):
                    mm = pe.matmul(b[:, 256:512], v[:, t, :], a_off[:, 256 + t * 256:512 + t * 256], start=False, stop=(t == 1),
                                   skip_group_check=True)
                mm.then_inc(gram_ready, 1)

            def head_cols(h):
                pe.wait_ge(gfree["act"], 4 * (h + 1))
                pe.wait_ge(*released(h))
                norm_cols(1 + h, sq[h % 2])

            def do(events):
                for kind, h, step in events:
                    if kind == "pair":
                        pairs(h, step)
                    elif kind == "out":
                        head_out(h)
                    elif kind == "columns":
                        head_cols(h)
                    elif kind == "spread":
                        norm_bc(1 + h)

            for idx, (label, i) in enumerate(A_SLOTS):
                def hook(k, idx=idx):
                    do(events_at(idx, k))

                if label == "p0":
                    slot_std(label, i, FIRST[f"zf{i}"], U_MIX0, hook=hook)
                elif label == "g0":
                    slot_std(label, i, FIRST[f"g{i}"], U_MIX0, hook=hook)
                else:
                    slot_tok(label, i, FIRST[f"v{i // 2}"], U_MIX0, hook=hook)
            do(A_LATE)
            for i in range(4):
                slot_std("wo0", i, FIRST["wo0"] + 2 * i, U_YA)

            def ffn(layer, ucount, gcount):
                for g in range(FFN_G + 1):
                    if g < FFN_G:
                        for i in (2 * g, 2 * g + 1):
                            slot_std(f"fi{layer}", i, FIRST[f"fi{layer}_{i}"], ucount)
                    if g:
                        slot_out(f"fo{layer}", g - 1, FIRST[f"fo{layer}_{g - 1}"], gcount)

            norm("ffn0")
            ffn("0", U_FFN0, G_FFN0)

            norm("kv")
            for i in range(4):
                slot_std("kk", i, FIRST["kk"] + 2 * i, U_KV)
            for i in range(4):
                slot_tok("vv", i, FIRST[f"vv{i // 2}"], U_KV)
            for i in range(4):
                slot_std("qq", i, FIRST["qq"] + 2 * i, U_MIX1)
            pe.wait_ge(free["act"], FREES[FIRST["qq"] + 7][1])

            def scores(h):
                for j in range(TB):
                    if h:
                        pe.wait_ge(at_sc, 4 * (h - 1) + j + 1)
                    n = (j + 1) * P
                    r = (h % 2) * HD
                    pe.matmul(bank[j][:, 0:n], b_q[r:r + HD, h // 2, j * P:n], b_k[r:r + HD, h // 2, 0:n],
                              start=True, stop=True).then_inc(at_s, 1)

            def turn(h):
                pe.wait_ge(at_p, h + 1)
                for j in range(TB):
                    n = 4 * h + j
                    if n >= 2:
                        pe.wait_ge(at_pt, n - 1)
                    for i in range(j + 1):
                        c = b_off[j] + i * P
                        mm = pe.matmul(bank[4 + j % 2][:, i * P:(i + 1) * P], b_s[h % 2][:, c:c + P], b_dg[:, h % 2, j, :],
                                       start=True, stop=True)
                    mm.then_inc(at_tr, 1)

            def weighted(h):
                pe.wait_ge(at_pt, 4 * (h + 1))
                r = (h % 2) * HD
                if h % 2 == 0 and h >= 4:
                    pe.wait_ge(u_l, U_O + h // 2 - 1)
                for i in range(TB):
                    mm = pe.matmul(bank[6 + h // 2 % 2][r:r + HD, i * P:SEQ], b_v[:, i, h * HD:(h + 1) * HD], b_pt[:, i, i * P:SEQ],
                                   start=(i == 0), stop=(i == 3), skip_group_check=True)
                mm.then_inc(at_o, 1)

            pe.wait_ge(mod_col, NVMOD)
            pe.wait_ge(*released(NORM["kv"]))
            scores(0)
            scores(1)
            for h in range(B_HEADS):
                turn(h)
                if h + 2 < B_HEADS:
                    scores(h + 2)
                weighted(h)
            for i in range(4):
                slot_std("wo1", i, FIRST["wo1"] + 2 * i, U_O)
            norm("ffn1")
            ffn("1", U_FFN1, G_FFN1)

            norm("final")
            norm("pre2")
            slot_std("mgate", 0, FIRST["mgate"], U_PRE2, nout=1)
            for i in range(4):
                slot_std("mqk", i, FIRST["mqk"] + 2 * i, U_PRE2)
                if i == 1:
                    pe.wait_ge(mg_rows, 1)
                    for what in range(2):
                        for d in range(2):
                            for j in range(TB):
                                c = (what * 8 + d * TB + j) * M_HEADS
                                rows = (gs if what == 0 else gt)[0:M_HEADS, d, j * P:(j + 1) * P]
                                mm = pe.transpose(bank[7][:, c:c + M_HEADS], rows, ident[0:M_HEADS, 0:M_HEADS])
                    mm.then_inc(mg_tr, 1)
            for i in range(2):
                slot_tok("mv", i, FIRST["mv"], U_PRE2)
            for i in range(2):
                slot_std("mo", i, FIRST["mo"] + 2 * i, U_PRE2)
            pe.wait_ge(m_in, 32)
            pe.wait_ge(mg_cc, 2)
            pe.wait_ge(free["act"], FREES[FIRST["mv"] + 3][1])
            pe.wait_ge(cv_q, 8)
            pe.wait_ge(free["act"], FREES[FIRST["mo"] + 3][1])

            def bounds(h):
                for d in range(2):
                    if h:
                        pe.wait_ge(ml_a, 2 * h)
                    pe.matmul(bank[d][:, :], m_sel[0:M_HEADS, h, :], gi[0:M_HEADS, d, :],
                              start=True, stop=True).then_inc(ml_mb, 1)

            bounds(0)
            for h in range(M_HEADS):
                for i in range(TB):
                    n = 4 * h + i
                    if n >= 2:
                        pe.wait_ge(ml_p, 2 * (n - 1))
                    pe.matmul(bank[2 + i % 2][:, :], m_qk[:, 4 + h, i * P:(i + 1) * P], m_qk[:, h, :],
                              start=True, stop=True).then_inc(ml_s, 1)
                if h + 1 < M_HEADS:
                    bounds(h + 1)
                pe.wait_ge(ml_p, 8 * (h + 1))
                if h:
                    pe.wait_ge(ml_nev, 2 * h)
                for d in range(2):
                    order = range(TB) if d == 0 else range(TB - 1, -1, -1)
                    for i in order:
                        a, z = (i * P, SEQ) if d == 0 else (0, (i + 1) * P)
                        o = m_off[d][i]
                        mm = pe.matmul(bank[4 + d][:, a:z], m_v[:, i, h * P:(h + 1) * P], m_w[:, 2 * (h % 2) + d, o:o + z - a],
                                       start=(i == order[0]), stop=(i == order[-1]), skip_group_check=True)
                    mm.then_inc(ml_num, 1)
                if h:
                    pe.wait_ge(ml_h, h)
                for d in range(2):
                    pe.wait_ge(ml_sum, 2 * h + d + 1)
                    for j in range(TB):
                        mm = pe.matmul(bank[6][:, d * TB + j:d * TB + j + 1], m_sum[:, d, j * P:(j + 1) * P], onec[:, :],
                                       start=True, stop=True)
                mm.then_inc(ml_den, 1)
                for d in range(2):
                    pe.wait_ge(ml_rd, 2 * h + d + 1)
                    pe.matmul(bank[6 + d][:, :], ones[:, :], gs[:, d, :], start=True, stop=True).then_inc(ml_bc, 1)
            pe.wait_ge(ml_h, M_HEADS)
            for h in range(M_HEADS):
                pe.wait_ge(ml_sq, h + 1)
                for j in range(TB):
                    mm = pe.matmul(bank[7][:, h * TB + j:h * TB + j + 1], sq[h % 2][:, j * P:(j + 1) * P], onec[:, :],
                                   start=True, stop=True)
                mm.then_inc(ml_col, 1)
            for i in range(6):
                slot_std("h2", i, FIRST["h2"] + 2 * i, U_PRE2)
                if i == 0:
                    for h in range(M_HEADS):
                        pe.wait_ge(ml_diag, h + 1)
                        pe.matmul(bank[4 + h][:, :], ones[:, :], m_dg[h], start=True, stop=True).then_inc(ml_nbc, 1)
                for c in (2 * i - 2, 2 * i - 1):
                    if c >= 0:
                        pe.wait_ge(*free_of(FIRST["h2"] + c))
                        if c >= 2:
                            pe.wait_ge(tr_ev, c - 1)
                        elif c == 0:
                            pe.wait_ge(ml_y, 4)
                        for j in range(TB):
                            mm = pe.transpose(bank[4 + c % 2][:, j * P:(j + 1) * P], cv[:, c % 2, j * P:(j + 1) * P], ident[:, :])
                        mm.then_inc(tr_done, 1)
            for c in (10, 11):
                pe.wait_ge(*free_of(FIRST["h2"] + c))
                pe.wait_ge(tr_ev, c - 1)
                for j in range(TB):
                    mm = pe.transpose(bank[4 + c % 2][:, j * P:(j + 1) * P], cv[:, c % 2, j * P:(j + 1) * P], ident[:, :])
                mm.then_inc(tr_done, 1)
            for o in (0, 1):
                (wa, hi_a, lo_a), (wb, hi_b, lo_b) = weights("dft", 4 * o), weights("dft", 4 * o + 1)
                for f in range(4):
                    for name, w, hi, lo in (("fa", wa, hi_a, lo_a), ("fb", wb, hi_b, lo_b)):
                        n = FIRST[f"{name}{o}_{f}"]
                        b = claim(n)
                        for k in range(4):
                            pe.wait_ge(g_l, G_Z[o] + k + 1)
                            c = k * 512 + f * P
                            mm = three(b[:, :], hi[:, c:c + P], lo[:, c:c + P], g_hi[:, k, :], g_lo[:, k, :], k == 0, k == 3)
                        complete(mm, n, w if f == 3 else None)
                slot_four("dft", 4 * o + 2, FIRST[f"iy{o}"], u_hi[:, 0:4, :], u_lo[:, 0:4, :],
                          lambda k, o=o: (u_l, U_Y[o] + 2 * k + 1), stop=False)
                slot_four("dft", 4 * o + 3, FIRST[f"iy{o}"], u_hi[:, 4:8, :], u_lo[:, 4:8, :],
                          lambda k, o=o: (u_l, U_Y[o] + 2 * k + 2), start=False)
            pe.wait_ge(hy_n, 4)
            for c in range(4):
                if c >= 2:
                    pe.wait_ge(hy_yf, c - 1)
                for j in range(TB):
                    mm = pe.transpose(bank[4 + c % 2][:, j * P:(j + 1) * P], h_A[:, j, c * P:(c + 1) * P], ident[:, :])
                mm.then_inc(hy_tr, 1)
            for i in range(4):
                slot_std("wo2", i, FIRST["wo2"] + 2 * i, U_MIX2)
            norm("post2")
            norm("mlp_pre2")
            for g in range(MLP_G + 1):
                if g < MLP_G:
                    slot_std("mi", g, FIRST[f"mi{g}"], U_MLP)
                if g:
                    slot_out("mout", g - 1, FIRST[f"mout{g - 1}"], G_MLP)
            norm("mlp_post2")


        @block.scalar
        def _(act):
            fed = [0]

            def feed(upto):
                while fed[0] <= min(upto, NW - 1):
                    w = fed[0]
                    s = W_STREAM[w]
                    act.wait_ge(raw_in[s % raw_ring], 16 * (s // raw_ring + 1))
                    if w >= hi_ring:
                        act.wait_ge(product, USED[w - hi_ring])
                    act.activation(w_hi[w % hi_ring][:, :], raw[s % raw_ring][:, :], ACT.Copy).then_inc(hi_done, 1)
                    fed[0] += 1

            def ahead(label, i):
                feed(W_AT[(label, i)] + hi_ring - 1)

            def read(n):
                act.wait_ge(product, READY[n])
                return bank[n % 4]

            def evacuate(n, dst, func=ACT.Copy, **kw):
                act.activation(dst, read(n)[:, :], func, **kw).then_inc(free["act"], 1)

            def squares(name, src, chunks=range(KC)):
                for c in chunks:
                    act.wait_ge(*finished(name, c))
                    if 8 * MAIN[name] + c >= 2:
                        act.wait_ge(sq_add, 8 * MAIN[name] + c - 1)
                    act.activation(sq[c % 2], src[:, c, :], ACT.Square).then_inc(sq_done, 1)

            def root(n):
                act.wait_ge(n_col, n + 1)
                scale = 1.0 / P if 1 <= n <= A_HEADS else 1.0 / D
                act.activation(rt[:, 0:TB], bank[6][:, 0:TB], ACT.Sqrt, bias=zcol[:, 1:2], scale=scale).then_inc(n_root, 1)

            def upper_u(name, count, shift, reuse, between=None):
                fp = FROM_NORM[name]
                for c in range(KC):
                    act.wait_ge(u_t, fp + c + 1)
                    act.wait_ge(product, reuse(c))
                    act.activation(u_hi[:, c, :], tn[c % 4], ACT.Identity, bias=shift(c)).then_inc(u_h, 1)
                    if between and c % 2:
                        between(c // 2)

            def modulated(name, count, scale, shift, reuse, between=None):
                act.wait_ge(mod_col, shift + 1)
                upper_u(name, count, lambda c: mcol(shift, c), reuse, between)

            def plain(name, count, gain, reuse):
                upper_u(name, count, lambda c: zcol[:, 0:1], reuse)

            act.wait_ge(vec_in, 16)
            act.wait_ge(const_ready, 4)
            act.activation(cact[:, :], vcols("c"), ACT.Silu).then_inc(cact_ready, 1)
            act.wait_ge(lb_d, 1)
            act.activation(lbt[:, 1, :], lbt[:, 0, :], ACT.Exp).then_inc(lb_e, 1)
            act.dma_start(H[:, :, :], A["x"].rearrange("(c p) t -> p c t", p=P)).then_inc(x_in, 16)
            for i in range(3):
                b = read(i)
                act.activation(f_a[0:FH, 0, :], b[0:FH, :], ACT.Identity, bias=vcol("filt_b", i)[0:FH]).then_inc(free["act"], 1)
                act.wait_ge(free["act"], i + 1)
                act.activation(f_a[0:FH, 1, :], f_a[0:FH, 0, :], ACT.Identity, bias=zcol[0:FH, 0:1],
                               scale=vcol("filt_fr", i)[0:FH]).then_inc(f_arg, 1)
                act.wait_ge(f_red, i + 1)
                act.activation(f_h[0:FH, i, :], f_a[0:FH, 3, :], ACT.Sin).then_inc(f_sin, 1)
            half = 0
            for o in (0, 1):
                for t in range(TB):
                    for x in (0, 1):
                        act.wait_ge(tap_done, 8 * o + 2 * t + x + 1)
                        src = tap[:, 2 * x + t % 2, :]
                        if o:
                            act.wait_ge(product, used("spec", 1))
                        if o == x:
                            act.activation(g_hi[:, t, :], src, ACT.Copy).then_inc(g_h, 1)
                        else:
                            act.activation(u_hi[:, t + 4 * o, :], src, ACT.Copy).then_inc(u_h, 1)
                    if t == 1:
                        feed(0)
                if o == 0:
                    feed(1)
                    squares("mix0", H)
                first = FIRST[f"spec{o}"]
                def spectrum(f):
                    nonlocal half
                    n = first + f + f // TB
                    e = 8 * o + f
                    if e >= 2:
                        act.wait_ge(spec_out[e % 2], 16 * (e // 2))
                    st = spec_st[:, e % 2, :]
                    b = read(n)
                    if f % TB:
                        act.activation(st, b[:, :], ACT.Copy, scale=2.0 / (2 * SEQ)).then_inc(free["act"], 1)
                    else:
                        act.activation(st, b[:, :], ACT.Copy, scale=2.0 / (2 * SEQ)).then_inc(spec_ev, 1)
                        half += 1
                        act.wait_ge(spec_ev, half)
                        src, scale = (b[0:1, :], 1.0 / (2 * SEQ)) if f == 0 else (spec_ny[0:1, :], 1.0)
                        act.activation(st[0:1, :], src, ACT.Copy, scale=scale).then_inc(free["act"], 1)
                    act.wait_ge(free["act"], FREES[n][1])
                    act.dma_start(spec_dram[o, f // TB, f % TB], st).then_inc(spec_out[e % 2], 16)

                ahead("spec", 2 * o)
                for f in range(TB):
                    spectrum(f)
                ahead("spec", 2 * o + 1)
                b = read(first + TB)
                act.activation(spec_ny[0:1, :], b[0:1, :], ACT.Copy, scale=1.0 / (2 * SEQ)).then_inc(free["act"], 1)
                act.wait_ge(free["act"], FREES[first + TB][1])
                if o == 0:
                    root(0)
                    for f in range(TB, 2 * TB):
                        spectrum(f)
                else:
                    modulated("mix0", U_MIX0, SC1_0, SH1_0, lambda c: used("spec", 1) if c < 4 else READY[first + TB],
                              lambda x: spectrum(TB + x))

            act.wait_ge(spec_out[0], 16 * 8)
            act.wait_ge(spec_out[1], 16 * 8)

            def do(events):
                for kind, h, step in events:
                    if kind == "columns":
                        root(1 + h)
                    if kind == "out":
                        step = PAIR_STEPS
                    if kind not in ("pair", "out") or step < NLEV:
                        continue
                    act.wait_ge(gram_ready, GRAM_PER_HEAD * h + step + 1)
                    b = bank[4 + (GRAM_PER_HEAD * h + step) % 2]
                    if step == NLEV:
                        act.wait_ge(gfree["dve"], NLEV * (h + 1))
                        blocks = b[:, :].rearrange("p (t s) -> p t s", t=TB)
                        act.activation(a_p[0:64, h % 2, :, 64:P], blocks[0:64, :, 64:P], ACT.Copy).then_inc(gfree["act"], 1)
                    elif step == NLEV + 1:
                        blocks = b[:, :].rearrange("p (t two s) -> p t two s", t=2, two=2)
                        act.activation(a_off[:, 0:256].rearrange("p (t s) -> p t s", t=2), blocks[:, :, 0, :], ACT.Copy).then_inc(gfree["act"], 1)
                    elif step == NLEV + 2:
                        act.activation(a_off[:, 256:768], b[:, :], ACT.Copy).then_inc(gfree["act"], 1)
                    else:
                        if h >= 2:
                            act.wait_ge(a_yd, h - 1)
                        act.activation(uf[h % 2], b[:, :], ACT.Copy).then_inc(a_os, 1)
                        act.wait_ge(n_col, h + 1 if h < 2 else h)
                        act.activation(sq[h % 2], b[:, :], ACT.Square).then_inc(gfree["act"], 1)

            for idx, (label, i) in enumerate(A_SLOTS):
                ahead(label, i)
                for k in range(HOOKS - 1):
                    do(events_at(idx, k))
                if label == "p0":
                    if i >= 1:
                        act.wait_ge(a_keys, i)
                    evacuate(FIRST[f"zf{i}"], zf, ACT.Sigmoid)
                    if i >= 2:
                        act.wait_ge(gram_ready, GRAM_PER_HEAD * (i - 2) + 10)
                    evacuate(FIRST[f"q{i}"], a_q[:, i % 2, :], ACT.Silu)
                elif label == "g0":
                    for j in (0, 1):
                        h = 2 * i + j
                        if h >= 4:
                            act.wait_ge(a_gated, h - 3)
                        evacuate(FIRST[f"g{i}"] + j, a_gate[:, h % 4, :], ACT.Silu)
                elif i % 2:
                    for j in range(TB):
                        evacuate(FIRST[f"v{i // 2}"] + j, a_v[:, j, (i // 2) * 512:(i // 2 + 1) * 512])
                do(events_at(idx, HOOKS - 1))
            do(A_LATE)

            def split_y(heads):
                for h in heads:
                    act.wait_ge(a_gated, h + 1)
                    act.wait_ge(product, used("g0", 3))
                    act.activation(u_hi[:, h, :], a_y[:, h, :], ACT.Copy).then_inc(u_h, 1)

            split_y(range(A_HEADS))
            for i in range(4):
                ahead("wo0", i)
                squares("ffn0", H, (2 * i, 2 * i + 1))

            def ffn(layer, ucount, gcount, sg):
                for g in range(FFN_G + 1):
                    if g < FFN_G:
                        for i in (2 * g, 2 * g + 1):
                            n = FIRST[f"fi{layer}_{i}"]
                            ahead(f"fi{layer}", i)
                            if i >= 2:
                                act.wait_ge(*free_of(FIRST[f"fi{layer}_{i - 2}"] + 1))
                            act.activation(ff_s[:, i % 2, :], read(n)[:, :], ACT.Silu).then_inc(sg_done, 1)
                            act.wait_ge(*free_of(n + 1))
                            if g >= 2:
                                act.wait_ge(product, used(f"fo{layer}", g - 2))
                            act.activation(g_hi[:, (gcount + i) % NG, :], ff_h[:, i % 2, :], ACT.Copy).then_inc(g_h, 1)
                    if g:
                        ahead(f"fo{layer}", g - 1)

            root(NORM["ffn0"])
            modulated("ffn0", U_FFN0, SC2_0, SH2_0, lambda c: used("wo0", 3))
            ffn("0", U_FFN0, G_FFN0, 0)

            squares("kv", H)
            root(NORM["kv"])
            modulated("kv", U_KV, KSC, KSH, lambda c: used("fi0", FFN_CH - 1))
            for i in range(4):
                ahead("kk", i)
                for j in (0, 1):
                    evacuate(FIRST["kk"] + 2 * i + j, b_k[:, 2 * i + j, :])
            for i in range(4):
                ahead("vv", i)
                if i % 2:
                    for j in range(TB):
                        evacuate(FIRST[f"vv{i // 2}"] + j, b_v[:, j, (i // 2) * 512:(i // 2 + 1) * 512])
            modulated("mix1", U_MIX1, SC1_1, SH1_1, lambda c: used("vv", 3))
            for i in range(4):
                ahead("qq", i)
                for j in (0, 1):
                    evacuate(FIRST["qq"] + 2 * i + j, b_q[:, 2 * i + j, :])

            def exponential(h, j):
                x = 4 * (h % 2) + j
                act.wait_ge(at_mx, 4 * h + j + 1)
                s = b_s[h % 2][:, b_off[j]:b_off[j] + (j + 1) * P]
                act.activation(s, s, ACT.Exp, bias=b_mx[:, x:x + 1], accum_out=b_sm[:, x:x + 1]).then_inc(at_e, 1)

            for j in range(TB):
                exponential(0, j)
            for h in range(B_HEADS):
                if h:
                    act.wait_ge(at_o, h)
                    if h % 2 == 0:
                        pc = h // 2 - 1
                        act.wait_ge(product, used("qq", 3))
                        act.activation(u_hi[:, pc, :], bank[6 + pc % 2][:, :], ACT.Copy).then_inc(u_h, 1)
                for j in range(TB):
                    act.wait_ge(at_tr, 4 * h + j + 1)
                    b = bank[4 + j % 2][:, 0:(j + 1) * P].rearrange("p (i q) -> p i q", q=P)
                    act.activation(b_pt[:, 0:j + 1, j * P:(j + 1) * P], b, ACT.Copy).then_inc(at_pt, 1)
                    if h + 1 < B_HEADS:
                        exponential(h + 1, j)
            act.wait_ge(at_o, B_HEADS)
            act.activation(u_hi[:, 7, :], bank[7][:, :], ACT.Copy).then_inc(u_h, 1)
            for i in range(4):
                ahead("wo1", i)
                squares("ffn1", H, (2 * i, 2 * i + 1))
            root(NORM["ffn1"])
            modulated("ffn1", U_FFN1, SC2_1, SH2_1, lambda c: used("wo1", 3))
            ffn("1", U_FFN1, G_FFN1, FFN_CH)

            squares("final", H)
            root(NORM["final"])
            squares("pre2", H)
            root(NORM["pre2"])
            plain("pre2", U_PRE2, "pre2", lambda c: used("fi1", FFN_CH - 1))

            def middle_tap(n, c, count):
                act.activation(cv[:, count % 2, :], read(n)[:, :], ACT.Identity, bias=vcol("conv_b", c),
                               scale=vcol("conv_w", 20 + c)).then_inc(cv_y, 1)

            def query_key(c):
                act.wait_ge(*free_of(FIRST["mqk"] + c))
                act.activation(m_qk[:, c, :], cv[:, c % 2, :], ACT.Silu).then_inc(cv_q, 1)

            ahead("mgate", 0)
            evacuate(FIRST["mgate"], g_all, ACT.Identity, bias=vcol("b_gates"))
            act.wait_ge(mg_q, 1)
            act.activation(gt[0:M_HEADS], gt[0:M_HEADS], ACT.Exp, scale=-1.0).then_inc(mg_e, 1)
            act.wait_ge(mg_e, 1)
            act.activation(gt[0:M_HEADS], gt[0:M_HEADS], ACT.Ln, bias=onec[0:M_HEADS, 0:1]).then_inc(mg_l, 1)
            for i in range(4):
                ahead("mqk", i)
                for c in (2 * i, 2 * i + 1):
                    if c >= 2:
                        act.wait_ge(cv_q, c - 1)
                    middle_tap(FIRST["mqk"] + c, c, c)
                for c in (2 * i, 2 * i + 1):
                    query_key(c)
                if i == 2:
                    act.wait_ge(mg_tr, 1)
                    act.wait_ge(mg_cc, 1)
                    act.activation(m_em, bank[7][:, 32:64], ACT.Exp, scale=-1.0).then_inc(mg_cc, 1)
            for i in range(2):
                ahead("mv", i)
            for j in range(TB):
                evacuate(FIRST["mv"] + j, m_v[:, j, :])
            for i in range(2):
                ahead("mo", i)
                for j in (0, 1):
                    evacuate(FIRST["mo"] + 2 * i + j, m_og[:, 2 * i + j, :], ACT.Sigmoid)

            def weights_of(h):
                for d in range(2):
                    act.wait_ge(ml_a, 2 * h + d + 1)
                    w = m_w[:, 2 * (h % 2) + d, :]
                    act.activation(w, w, ACT.Exp, scale=-1.0).then_inc(ml_w, 1)

            weights_of(0)
            for h in range(M_HEADS):
                for d in range(2):
                    act.wait_ge(ml_num, 2 * h + d + 1)
                    if h:
                        act.wait_ge(ml_h, h)
                    act.activation(scr[:, 2 + d, :], bank[4 + d][:, :], ACT.Copy).then_inc(ml_nev, 1)
                if h + 1 < M_HEADS:
                    weights_of(h + 1)
            act.wait_ge(ml_h, M_HEADS)
            for h in range(M_HEADS):
                if h >= 2:
                    act.wait_ge(ml_col, h - 1)
                act.activation(sq[h % 2], m_h[:, h, :], ACT.Square).then_inc(ml_sq, 1)
            act.wait_ge(ml_col, M_HEADS)
            act.activation(rt[:, :], bank[7][:, 0:16], ACT.Sqrt, bias=zcol[:, 1:2], scale=1.0 / P).then_inc(ml_root, 1)

            def turned(c):
                act.wait_ge(tr_done, c + 1)
                b = bank[4 + c % 2][:, :].rearrange("p (j f) -> p j f", j=TB)
                act.activation(h_tok[c // 4][:, :, (c % 4) * P:(c % 4 + 1) * P], b, ACT.Copy).then_inc(tr_ev, 1)

            for i in range(6):
                ahead("h2", i)
                for c in (2 * i, 2 * i + 1):
                    if c >= 2:
                        act.wait_ge(tr_done, c - 1)
                    middle_tap(FIRST["h2"] + c, 8 + c, c)
                    if c >= 2:
                        turned(c - 2)
            turned(10)
            turned(11)
            for o in (0, 1):
                for k in range(4):
                    if o == 0:
                        act.wait_ge(tr_ev, 4)
                    else:
                        act.wait_ge(*free_of(FIRST["iy0"] + k))
                        act.wait_ge(product, used("dft", 1))
                    act.activation(g_hi[:, k, :], h_tok[o][:, k, :], ACT.Copy).then_inc(g_h, 1)
                ahead("dft", 4 * o)
                for f in range(5):
                    if f < 4:
                        if o:
                            act.wait_ge(hy_y, 4)
                        evacuate(FIRST[f"fa{o}_{f}"], h_A[:, f, :])
                        if f == 3:
                            ahead("dft", 4 * o + 1)
                    if f:
                        e = f - 1
                        act.wait_ge(hy_y, 4 * o + e + 1)
                        act.wait_ge(product, used("h2", 5) if o == 0 else used("dft", 3))
                        for x in (0, 1):
                            act.activation(u_hi[:, 4 * x + e, :], h_t[:, 2 + 2 * (e % 2) + x, :], ACT.Copy).then_inc(u_h, 1)
                ahead("dft", 4 * o + 2)
                if o == 0:
                    ahead("dft", 3)
            act.wait_ge(product, used("dft", 6))
            for h in range(M_HEADS):
                act.activation(u_hi[:, h, :], m_h[:, h, :], ACT.Copy).then_inc(u_h, 1)
            ahead("dft", 7)
            for j in range(TB):
                act.wait_ge(*free_of(FIRST["iy1"] + j))
                if j >= 2:
                    act.wait_ge(hy_rs, j - 1)
                act.activation(sq[j % 2], h_tok[2][:, j, :], ACT.Square).then_inc(hy_sq, 1)
            act.wait_ge(hy_rs, TB)
            act.activation(h_r, h_m, ACT.Sqrt, bias=zcol[:, 1:2], scale=1.0 / 64).then_inc(hy_rt, 1)
            for c in range(4):
                act.wait_ge(hy_tr, c + 1)
                act.wait_ge(u_l, U_MIX2 + 4 + max(c - 1, 0))
                act.activation(uf[c % 2], bank[4 + c % 2][:, :], ACT.Identity, bias=zcol[:, 0:1],
                               scale=vcol("hyena_norm", c)).then_inc(hy_yf, 1)
                act.wait_ge(hy_yf, c + 1)
                act.wait_ge(product, used("dft", 7))
                act.activation(u_hi[:, 4 + c, :], uf[c % 2], ACT.Copy).then_inc(u_h, 1)
            for i in range(4):
                ahead("wo2", i)
                squares("post2", Facc, (2 * i, 2 * i + 1))
            root(NORM["post2"])
            squares("mlp_pre2", H)
            root(NORM["mlp_pre2"])
            plain("mlp_pre2", U_MLP, "mlp_pre2", lambda c: used("wo2", 3))
            for g in range(MLP_G + 1):
                if g < MLP_G:
                    ahead("mi", g)
                    for i in (2 * g, 2 * g + 1):
                        n = FIRST[f"mi{g}"] + i % 2
                        if i >= 2:
                            act.wait_ge(*free_of(FIRST[f"mi{g - 1}"] + i % 2))
                        act.activation(ff_s[:, i % 2, :], read(n)[:, :], ACT.Relu).then_inc(sg_done, 1)
                if g:
                    ahead("mout", g - 1)
                if g < MLP_G:
                    for i in (2 * g, 2 * g + 1):
                        n = FIRST[f"mi{g}"] + i % 2
                        act.wait_ge(*free_of(n))
                        if g >= 2:
                            act.wait_ge(product, used("mout", g - 2))
                        act.activation(g_hi[:, (G_MLP + i) % NG, :], ff_h[:, i % 2, :], ACT.Copy).then_inc(g_h, 1)
            squares("mlp_post2", Facc)
            root(NORM["mlp_post2"])

        @block.vector
        def _(dve):
            links = [0]

            def link(ins):
                ins.then_inc(vlink, 1)
                links[0] += 1
                dve.wait_ge(vlink, links[0])

            fed = [0]

            def take_mods(point):
                sums, vectors = MOD_POINTS[point]
                dve.wait_ge(mod_sum, sums)
                for e in range(MOD_POINTS[point - 1][1] if point else 0, vectors):
                    b0 = VEC["mod_b0"][0] + e * KC
                    dve.tensor_tensor(modc[:, e * KC:(e + 1) * KC], bank[7][:, e * KC:(e + 1) * KC], vec[:, b0:b0 + KC],
                                      ALU.add).then_inc(mod_col, 1)
                    if e in SCALES:
                        idx, gain = SCALES[e]
                        dve.wait_ge(mod_col, e + 1)
                        dve.scalar_tensor_tensor(acol[:, idx * KC:(idx + 1) * KC], modc[:, e * KC:(e + 1) * KC], 1.0, vcols(gain),
                                                 ALU.add, ALU.mult).then_inc(acol_done, 1)
                dve.wait_ge(mod_col, vectors)

            def feed(upto):
                while fed[0] <= min(upto, NW - 1):
                    w = fed[0]
                    dve.wait_ge(hi_done, w + 1)
                    dve.tensor_tensor(w_lo[w % hi_ring][:, :], raw[W_STREAM[w] % raw_ring][:, :], w_hi[w % hi_ring][:, :].bitcast(F32),
                                      ALU.subtract).then_inc(lo_done, 1)
                    fed[0] += 1

            def ahead(label, i):
                feed(W_AT[(label, i)] + hi_ring - 1)

            def read(n):
                dve.wait_ge(product, READY[n])
                return bank[n % 4]

            def lower_u(n, k, src):
                dve.wait_ge(u_h, n + 1)
                dve.tensor_tensor(u_lo[:, k, :], src, u_hi[:, k, :].bitcast(F32), ALU.subtract).then_inc(u_l, 1)

            def lower_g(n, src):
                dve.wait_ge(g_h, n + 1)
                dve.tensor_tensor(g_lo[:, n % NG, :], src, g_hi[:, n % NG, :].bitcast(F32), ALU.subtract).then_inc(g_l, 1)

            def add_square(name, c):
                k = MAIN[name]
                dve.wait_ge(sq_done, 8 * k + c + 1)
                if c == 0:
                    if NORM[name]:
                        dve.wait_ge(n_col, NORM[name])
                    dve.tensor_copy(ssum, sq[0]).then_inc(sq_add, 1)
                else:
                    dve.wait_ge(sq_add, 8 * k + c)
                    dve.tensor_tensor(ssum, ssum, sq[c % 2], ALU.add).then_inc(sq_add, 1)

            def sums(name):
                for c in range(KC):
                    add_square(name, c)

            def on_diagonal(dst, col):
                return dve.tensor_tensor(dst, ident[:, :].unsqueeze(1).broadcast_to((P, TB, P)),
                                         col.unsqueeze(2).broadcast_to((P, TB, P)), ALU.mult)

            def factors(n):
                dve.wait_ge(n_root, n + 1)
                link(dve.reciprocal(rc[:, 0:TB], rt[:, 0:TB]))
                if n:
                    dve.wait_ge(n_bc, n)
                on_diagonal(diag, rc[:, 0:TB]).then_inc(n_diag, 1)

            def normalised(name, n, count, gain, shift=None):
                dve.wait_ge(n_bc, n + 1)
                if shift is not None:
                    dve.wait_ge(mod_col, shift + 1)

                def lower(c):
                    dve.wait_ge(u_h, count + c + 1)
                    hi = u_hi[:, c, :].bitcast(F32)
                    if shift is None:
                        ins = dve.tensor_tensor(u_lo[:, c, :], tn[c % 4], hi, ALU.subtract)
                    else:
                        ins = dve.scalar_tensor_tensor(u_lo[:, c, :], tn[c % 4], mcol(shift, c), hi, ALU.add, ALU.subtract)
                    ins.then_inc(u_l, 1)

                for c in range(KC):
                    if c >= 4:
                        dve.wait_ge(u_l, count + c - 3)
                    dve.scalar_tensor_tensor(tn[c % 4], H[:, c, :], gain(c), bank[6][:, :], ALU.mult, ALU.mult).then_inc(u_t, 1)
                    if c >= 2:
                        lower(c - 2)
                lower(6)
                lower(7)

            def modulated(name, n, count, scale, shift):
                idx = SCALES[scale][0]
                dve.wait_ge(acol_done, idx + 1)
                normalised(name, n, count, lambda c: acol[:, idx * KC + c:idx * KC + c + 1], shift)

            def residual(first, c, gate, before):
                n = FIRST[first] + c
                b = read(n)
                dve.wait_ge(*before)
                dve.scalar_tensor_tensor(H[:, c, :], b[:, :], mcol(gate, c), H[:, c, :], ALU.mult, ALU.add).then_inc(free["dve"], 1)

            def sum_mod(m):
                s = M_STREAM[m]
                src, acc = raw[s % raw_ring], macc[:, m % MRING, :]
                dve.wait_ge(cact_ready, 1)
                dve.wait_ge(raw_in[s % raw_ring], 16 * (s // raw_ring + 1))
                if m >= MRING:
                    dve.wait_ge(mod_sum, m - MRING + 1)
                link(dve.tensor_scalar(acc, src[:, 0:256], cact[:, 0:1], None, ALU.mult))
                for k in range(1, KC):
                    ins = dve.scalar_tensor_tensor(acc, src[:, k * 256:(k + 1) * 256], cact[:, k:k + 1], acc, ALU.mult, ALU.add)
                    if k < KC - 1:
                        link(ins)
                    else:
                        ins.then_inc(m_done, 1)

            dve.wait_ge(vec_in, 16)
            dve.wait_ge(const_ready, 4)
            dve.tensor_tensor(lbt[:, 0, :], vcols("a_lb"), vcols("a_lb"), ALU.subtract).then_inc(lb_d, 1)
            dve.wait_ge(lb_e, 1)
            link(dve.reciprocal(lbt[:, 2, :], lbt[:, 1, :]))
            link(dve.tensor_tensor(lbt[:, 3, :], lbt[:, 1, :], lbt[:, 2, :], ALU.mult))
            link(dve.tensor_tensor(lbt[:, 4, :], lbt[:, 3, :], lbt[:, 3, :], ALU.subtract))
            link(dve.tensor_scalar(lbt[:, 5, :], lbt[:, 4, :], -1.0, 1.0, ALU.mult, ALU.add))
            link(dve.tensor_scalar(lbt[:, 6, :], lbt[:, 5, :], -1.0, None, ALU.mult))
            for i in range(3):
                a, k, r, s = (f_a[0:FH, x, :] for x in (1, 2, 0, 3))
                dve.wait_ge(f_arg, i + 1)
                link(dve.tensor_scalar(k, a, 1.0 / TWO_PI, ROUND, ALU.mult, ALU.add))
                link(dve.tensor_scalar(k, k, -ROUND, None, ALU.add))
                link(dve.scalar_tensor_tensor(r, k, -TWO_PI_HI, a, ALU.mult, ALU.add))
                link(dve.scalar_tensor_tensor(r, k, -(TWO_PI - TWO_PI_HI), r, ALU.mult, ALU.add))
                dve.tensor_scalar(s, r, 3.1415925, -3.1415925, ALU.min, ALU.max).then_inc(f_red, 1)
                sum_mod(i)
            dve.wait_ge(taps_in, 16 * 4)

            def lower_taps(o, t):
                for x in (0, 1):
                    src = tap[:, 2 * x + t % 2, :]
                    if o == x:
                        lower_g(4 * o + t, src)
                    else:
                        lower_u(4 * o + t, 4 * o + t, src)

            for o in (0, 1):
                for t in range(TB):
                    first = FIRST[f"taps{o}"] + 2 * t
                    for d, dst in ((0, f_tf), (1, f_tb)):
                        dve.tensor_tensor(dst, read(first + d)[:, :], win[:, t, :], ALU.mult).then_inc(free["dve"], 1)
                    dve.wait_ge(*free_of(first + 1))
                    if t == 0:
                        dve.memset(f_tb[0:1, :], 0.0)
                        link(dve.tensor_tensor(f_tf[0:1, :], f_tf[0:1, :], f_bias[0:1, o * HW:(o + 1) * HW], ALU.add))
                    dve.tensor_tensor(tap[:, t % 2, :], f_tf, f_tb, ALU.add).then_inc(tap_done, 1)
                    dve.tensor_tensor(tap[:, 2 + t % 2, :], f_tf, f_tb, ALU.subtract).then_inc(tap_done, 1)
                    dve.wait_ge(tap_done, 8 * o + 2 * t + 2)
                    if t:
                        lower_taps(o, t - 1)
                    if o == 0 and t == 2:
                        feed(0)
                lower_taps(o, TB - 1)
                if o == 0:
                    feed(1)
                    dve.wait_ge(x_in, 16)
                    sums("mix0")
                    factors(0)
                ahead("spec", 2 * o)
                ahead("spec", 2 * o + 1)

            take_mods(MODS_MIX0)
            modulated("mix0", 0, U_MIX0, SC1_0, SH1_0)
            dve.wait_ge(spec_out[0], 16 * 8)
            dve.wait_ge(spec_out[1], 16 * 8)
            dve.wait_ge(mask_ready, 1)
            link(dve.memset(a_p, 0.0))

            def head_keys(h):
                lb, oml, noml = (lbt[:, x, h:h + 1] for x in (4, 5, 6))
                f, k = a_tot[:, h % 2, :], a_k[:, h % 2, :]
                dve.wait_ge(*free_of(FIRST[f"zf{h}"]))
                link(dve.tensor_scalar(f, zf, oml, lb, ALU.mult, ALU.add))
                dve.tensor_scalar(f, f, MIN_FORGET, None, ALU.max)
                if h >= 2:
                    dve.wait_ge(gram_ready, GRAM_PER_HEAD * (h - 2) + 10)
                dve.tensor_scalar(k, zf, 1.0, noml, ALU.subtract, ALU.mult).then_inc(a_keys, 1)

            def level(h, step):
                f, k, q = a_tot[:, h % 2, :], a_k[:, h % 2, :], a_q[:, h % 2, :]
                j = GRAM_PER_HEAD * h + step
                dve.wait_ge(gram_ready, j + 1)
                if step == 0:
                    dve.wait_ge(a_keys, h + 1)
                    dve.tensor_tensor(q, q, f, ALU.mult).then_inc(a_qf, 1)
                    dve.wait_ge(a_qf, h + 1)
                else:
                    m = 1 << (step - 1)
                    n = SEQ // m
                    tot = f if m == 1 else ssum[:, SEQ - 2 * n:SEQ - n]
                    even, odd = (tot.rearrange("p (n two) -> p n two", two=2)[:, :, x] for x in (0, 1))
                    if step > 1:
                        dve.wait_ge(a_lvl, 8 * h + step - 1)
                    if m < 128:
                        dve.tensor_tensor(ssum[:, SEQ - n:SEQ - n // 2], even, odd, ALU.mult)
                    spread = (P, n // 2, m)
                    dve.tensor_tensor(right_half(q, m), right_half(q, m), even.unsqueeze(2).broadcast_to(spread), ALU.mult)
                    dve.tensor_tensor(left_half(k, m), left_half(k, m), odd.unsqueeze(2).broadcast_to(spread), ALU.mult).then_inc(a_lvl, 1)
                if step < NLEV:
                    b = bank[4 + j % 2]
                    if step:
                        dve.wait_ge(gfree["dve"], NLEV * h + step)
                    dve.copy_predicated(a_p[:, h % 2, :, :], a_mask[:, step, :].unsqueeze(1).broadcast_to((P, TB, P)),
                                        b[:, :].rearrange("p (t s) -> p t s", t=TB)).then_inc(gfree["dve"], 1)

            def do(events):
                for kind, h, step in events:
                    if kind == "pair" and step <= NLEV + 1:
                        level(h, step)
                    elif kind == "diagonal":
                        factors(1 + h)
                    elif kind == "result":
                        dve.wait_ge(a_os, h + 1)
                        dve.wait_ge(n_bc, 1 + h + 1)
                        dve.scalar_tensor_tensor(a_y[:, h, :], bank[6][:, :], vcol("a_out_norm"), uf[h % 2], ALU.mult, ALU.mult).then_inc(a_yd, 1)

            def gated(h):
                dve.wait_ge(a_yd, h + 1)
                dve.wait_ge(*free_of(FIRST[f"g{h // 2}"] + h % 2))
                dve.tensor_tensor(a_y[:, h, :], a_y[:, h, :], a_gate[:, h % 4, :], ALU.mult).then_inc(a_gated, 1)

            results = gates = gated_heads = 0
            for idx, (label, i) in enumerate(A_SLOTS):
                for k in range(HOOKS):
                    do(events_at(idx, k))
                    results += sum(kind == "result" for kind, _, _ in events_at(idx, k))
                    if gated_heads < min(results, gates):
                        gated(gated_heads)
                        gated_heads += 1
                    if k == 2:
                        ahead(label, i)
                if label == "p0":
                    head_keys(i)
                if label == "g0":
                    gates = 2 * i + 2
            do(A_LATE)
            for h in range(gated_heads, A_HEADS):
                gated(h)
            take_mods(MODS_WO0)
            for h in range(A_HEADS):
                lower_u(U_YA + h, h, a_y[:, h, :])
            for i in range(4):
                ahead("wo0", i)
                for c in (2 * i, 2 * i + 1):
                    residual("wo0", c, G1_0, (x_in, 16))
                    if c:
                        add_square("ffn0", c - 1)

            def ffn(layer, gcount, sg, gate, mixer, after):
                def lag(i):
                    if i >= 0:
                        lower_g(gcount + i, ff_h[:, i % 2, :])

                for g in range(FFN_G + 1):
                    if g < FFN_G:
                        for i in (2 * g, 2 * g + 1):
                            n = FIRST[f"fi{layer}_{i}"]
                            ahead(f"fi{layer}", i)
                            lag(i - 1)
                            dve.wait_ge(sg_done, sg + i + 1)
                            dve.tensor_tensor(ff_h[:, i % 2, :], ff_s[:, i % 2, :], read(n + 1)[:, :], ALU.mult).then_inc(free["dve"], 1)
                    else:
                        lag(FFN_CH - 1)
                    if g:
                        if g == 1 and layer == "0":
                            take_mods(MODS_OUT0)
                        for c in range(KC):
                            before = FIRST[mixer] if g == 1 else FIRST[f"fo{layer}_{g - 2}"]
                            residual(f"fo{layer}_{g - 1}", c, gate, free_of(before + c))
                            if c == 1:
                                ahead(f"fo{layer}", g - 1)
                            if g == FFN_G and c:
                                add_square(after, c - 1)

            add_square("ffn0", KC - 1)
            factors(NORM["ffn0"])
            take_mods(MODS_FFN0)
            modulated("ffn0", NORM["ffn0"], U_FFN0, SC2_0, SH2_0)
            ffn("0", G_FFN0, 0, G2_0, "wo0", "kv")

            add_square("kv", KC - 1)
            factors(NORM["kv"])
            take_mods(MODS_ALL)
            modulated("kv", NORM["kv"], U_KV, KSC, KSH)
            for label in ("kk", "vv"):
                for i in range(4):
                    ahead(label, i)
            modulated("mix1", NORM["kv"], U_MIX1, SC1_1, SH1_1)
            for i in range(4):
                ahead("qq", i)

            def scores(h):
                def maximum(j):
                    x = 4 * (h % 2) + j
                    dve.wait_ge(at_sc, 4 * h + j + 1)
                    dve.tensor_reduce(b_mx[:, x:x + 1], b_s[h % 2][:, b_off[j]:b_off[j] + (j + 1) * P], AX.X, ALU.max,
                                      negate=True).then_inc(at_mx, 1)

                dve.wait_ge(rel_ready, h + 1)
                for j in range(TB):
                    n = (j + 1) * P
                    dve.wait_ge(at_s, 4 * h + j + 1)
                    if h >= 2:
                        dve.wait_ge(at_tr, 4 * (h - 2) + j + 1)
                    y = SEQ - P - j * P
                    dve.scalar_tensor_tensor(b_s[h % 2][:, b_off[j]:b_off[j] + n], bank[j][:, 0:n], HD ** -0.5,
                                             b_T[:, h % 2, y:y + n], ALU.mult, ALU.add).then_inc(at_sc, 1)
                    if j:
                        maximum(j - 1)
                maximum(TB - 1)

            scores(0)
            scores(1)

            def inverse_sums(h):
                x = 4 * (h % 2)
                dve.wait_ge(at_e, 4 * (h + 1))
                link(dve.reciprocal(b_rc[:, x:x + 4], b_sm[:, x:x + 4]))
                on_diagonal(b_dg[:, h % 2, :, :], b_rc[:, x:x + 4]).then_inc(at_p, 1)

            inverse_sums(0)
            for h in range(B_HEADS):
                if h + 1 < B_HEADS:
                    inverse_sums(h + 1)
                if h + 2 < B_HEADS:
                    scores(h + 2)
                if h and h % 2 == 0:
                    lower_u(U_O + h // 2 - 1, h // 2 - 1, bank[6 + (h // 2 - 1) % 2][:, :])
            lower_u(U_O + 7, 7, bank[7][:, :])
            for i in range(4):
                ahead("wo1", i)
                for c in (2 * i, 2 * i + 1):
                    residual("wo1", c, G1_1, free_of(FIRST[f"fo0_{FFN_G - 1}"] + c))
                    if c:
                        add_square("ffn1", c - 1)
            add_square("ffn1", KC - 1)
            factors(NORM["ffn1"])
            modulated("ffn1", NORM["ffn1"], U_FFN1, SC2_1, SH2_1)
            ffn("1", G_FFN1, FFN_CH, G2_1, "wo1", "final")

            add_square("final", KC - 1)
            factors(NORM["final"])
            dve.wait_ge(n_bc, NORM["final"] + 1)
            for c in range(KC):
                dve.scalar_tensor_tensor(H[:, c, :], bank[6][:, :], vcol("final_norm", c), H[:, c, :], ALU.mult, ALU.mult).then_inc(h_upd, 1)
                if c:
                    add_square("pre2", c - 1)
            dve.wait_ge(h_upd, KC)
            add_square("pre2", KC - 1)
            factors(NORM["pre2"])
            normalised("pre2", NORM["pre2"], U_PRE2, lambda c: vcol("pre2", c))

            def outer_taps(n, c, count):
                y, b = cv[:, count % 2, :], read(n)
                w = VEC["conv_w"][0]
                dve.wait_ge(cv_y, count + 1)
                link(dve.scalar_tensor_tensor(y[:, 1:SEQ], b[:, 0:SEQ - 1], vec[:, w + c:w + c + 1], y[:, 1:SEQ], ALU.mult, ALU.add))
                dve.scalar_tensor_tensor(y[:, 0:SEQ - 1], b[:, 1:SEQ], vec[:, w + 40 + c:w + 40 + c + 1], y[:, 0:SEQ - 1],
                                         ALU.mult, ALU.add).then_inc(free["dve"], 1)

            ahead("mgate", 0)
            dve.wait_ge(*free_of(FIRST["mgate"]))
            for d in range(2):
                dve.tensor_copy(gi[0:M_HEADS, d, :], g_all[64 * d:64 * d + M_HEADS, :])
                link(dve.tensor_copy(gf[0:M_HEADS, d, :], g_all[64 * d + 32:64 * d + 32 + M_HEADS, :]))
            rows = [x[0:M_HEADS] for x in (gi, gf, gt, gs)]
            r_i, r_f, r_t, r_s = rows
            dve.scalar_tensor_tensor(r_t, r_f, -1.0, r_f, ALU.mult, ALU.max).then_inc(mg_q, 1)
            def order(ap, d):
                return ap[:, d, :] if d == 0 else ap[:, d, ::-1]

            for i in range(4):
                ahead("mqk", i)
                for c in (2 * i, 2 * i + 1):
                    outer_taps(FIRST["mqk"] + c, c, c)
                if i == 0:
                    dve.wait_ge(mg_l, 1)

                    link(dve.scalar_tensor_tensor(r_f, r_f, 0.0, r_t, ALU.min, ALU.subtract))
                    for d in range(2):
                        ins = dve.tensor_tensor_scan(order(r_t, d), order(r_f, d), order(r_f, d), 0.0, ALU.add, ALU.bypass)
                    link(ins)
                    link(dve.tensor_tensor(r_s, r_i, r_t, ALU.subtract))
                    for d in range(2):
                        ins = dve.tensor_tensor_scan(order(r_i, d), order(r_s, d), order(r_s, d), 0.0, ALU.max, ALU.max)
                    link(ins)
                    dve.tensor_tensor(r_t, r_t, r_i, ALU.add).then_inc(mg_rows, 1)
                if i == 2:
                    dve.wait_ge(mg_tr, 1)
                    dve.tensor_copy(m_cc, bank[7][:, 0:32]).then_inc(mg_cc, 1)
            for i in range(2):
                ahead("mv", i)
            for i in range(2):
                ahead("mo", i)
            dve.wait_ge(mg_cc, 2)
            em = m_em.rearrange("p (x h) -> p x h", h=M_HEADS)

            def exponents(h):
                if h >= 2:
                    dve.wait_ge(ml_den, h - 1)
                for d in range(2):
                    dve.wait_ge(ml_mb, 2 * h + d + 1)
                    for i in range(TB):
                        a, z = (i * P, SEQ) if d == 0 else (0, (i + 1) * P)
                        o = m_off[d][i]
                        x = (d * TB + i) * M_HEADS + h
                        ins = dve.tensor_scalar(m_w[:, 2 * (h % 2) + d, o:o + z - a], bank[d][:, a:z], m_cc[:, x:x + 1], 0.0,
                                                ALU.subtract, ALU.max)
                    ins.then_inc(ml_a, 1)

            exponents(0)
            for h in range(M_HEADS):
                dve.wait_ge(ml_m, 2 * h + 2)
                for i in range(TB):
                    dve.wait_ge(ml_s, 4 * h + i + 1)
                    for d in range(2):
                        a, z = (i * P, SEQ) if d == 0 else (0, (i + 1) * P)
                        w = m_w[:, 2 * (h % 2) + d, m_off[d][i]:m_off[d][i] + z - a]
                        dve.scalar_tensor_tensor(w, bank[2 + i % 2][:, a:z], P ** -0.5, w, ALU.mult, ALU.mult).then_inc(ml_p, 1)
                if h + 1 < M_HEADS:
                    exponents(h + 1)
                dve.wait_ge(ml_den, h + 1)
                link(dve.tensor_tensor(m_dd[:, 0:8], bank[6][:, 0:8], em[:, :, h], ALU.max))
                link(dve.scalar_tensor_tensor(m_dd[:, 0:8], bank[6][:, 0:8], -1.0, m_dd[:, 0:8], ALU.mult, ALU.max))
                link(dve.reciprocal(m_rd[:, 0:8], m_dd[:, 0:8]))
                for d in range(2):
                    on_diagonal(gs[:, d, :].rearrange("p (a b) -> p a b", a=TB), m_rd[:, d * TB:(d + 1) * TB]).then_inc(ml_rd, 1)
                dve.wait_ge(ml_nev, 2 * h + 2)
                dve.wait_ge(ml_bc, 2 * h + 2)
                dve.tensor_tensor(m_h[:, h, :], scr[:, 2, :], bank[6][:, :], ALU.mult)
                link(dve.tensor_tensor(scr[:, 3, :], scr[:, 3, :], bank[7][:, :], ALU.mult))
                link(dve.tensor_tensor(m_h[:, h, :], m_h[:, h, :], scr[:, 3, :], ALU.add))
                dve.wait_ge(*free_of(FIRST["mo"] + 3))
                dve.tensor_tensor(m_h[:, h, :], m_h[:, h, :], m_og[:, h, :], ALU.mult).then_inc(ml_h, 1)
            dve.wait_ge(ml_root, 1)
            link(dve.reciprocal(rc[:, :], rt[:, :]))
            for h in range(M_HEADS):
                on_diagonal(m_dg[h], rc[:, h * TB:(h + 1) * TB]).then_inc(ml_diag, 1)
            ahead("h2", 0)
            for h in range(M_HEADS):
                dve.wait_ge(ml_nbc, h + 1)
                dve.scalar_tensor_tensor(m_h[:, h, :], bank[4 + h][:, :], vcol("mlstm_norm", h), m_h[:, h, :],
                                         ALU.mult, ALU.mult).then_inc(ml_y, 1)

            for i in range(6):
                ahead("h2", i)
                for c in (2 * i, 2 * i + 1):
                    outer_taps(FIRST["h2"] + c, 8 + c, 8 + c)
            for o in (0, 1):
                for k in range(4):
                    lower_g(G_Z[o] + k, h_tok[o][:, k, :])
                ahead("dft", 4 * o)

                def lower_product(f, o=o):
                    lower_u(U_Y[o] + 2 * f, f, h_t[:, 2 + 2 * (f % 2), :])
                    lower_u(U_Y[o] + 2 * f + 1, 4 + f, h_t[:, 3 + 2 * (f % 2), :])

                for f in range(4):
                    e = 4 * o + f
                    if f == 3:
                        ahead("dft", 4 * o + 1)
                    if f >= 2:
                        dve.wait_ge(u_l, U_Y[o] + 2 * (f - 1))
                    dve.wait_ge(sp_in[f % 2], 32 * (e // 2 + 1))
                    dve.wait_ge(*free_of(FIRST[f"fa{o}_{f}"]))
                    b = read(FIRST[f"fb{o}_{f}"])
                    za, ka, kb = h_A[:, f, :], h_kA[:, f % 2, :], h_kB[:, f % 2, :]
                    aa, bb, ab, ba = h_t[:, 0, :], h_t[:, 1, :], scr[:, 6, :], scr[:, 7, :]
                    yc, ys = h_t[:, 2 + 2 * (f % 2), :], h_t[:, 3 + 2 * (f % 2), :]
                    dve.tensor_tensor(aa, za, ka, ALU.mult)
                    dve.tensor_tensor(bb, b[:, :], kb, ALU.mult)
                    dve.tensor_tensor(ab, za, kb, ALU.mult)
                    dve.tensor_tensor(ba, b[:, :], ka, ALU.mult).then_inc(free["dve"], 1)
                    dve.wait_ge(*free_of(FIRST[f"fb{o}_{f}"]))
                    dve.tensor_tensor(yc, aa, bb, ALU.subtract)
                    ins = dve.tensor_tensor(ys, ab, ba, ALU.add)
                    if f == 0:
                        link(ins)
                        dve.tensor_copy(yc[0:1, :], aa[0:1, :])
                        ins = dve.tensor_copy(ys[0:1, :], bb[0:1, :])
                    ins.then_inc(hy_y, 1)
                    dve.wait_ge(hy_y, e + 1)
                    if f:
                        lower_product(f - 1)
                lower_product(3)
                ahead("dft", 4 * o + 2)
                ahead("dft", 4 * o + 3)
                for j in range(TB):
                    x = h_tok[o + 1][:, j, :]
                    dve.tensor_tensor(x, read(FIRST[f"iy{o}"] + j)[:, :], x, ALU.mult).then_inc(free["dve"], 1)
            groups = h_m.rearrange("p (j g) -> p j g", j=TB)
            for h in range(M_HEADS):
                lower_u(U_MIX2 + h, h, m_h[:, h, :])
            for j in range(TB):
                dve.wait_ge(hy_sq, j + 1)
                dve.tensor_reduce(groups[:, j, :], sq[j % 2].rearrange("p (g e) -> p g e", g=8), AX.X, ALU.add).then_inc(hy_rs, 1)
            dve.wait_ge(hy_rt, 1)
            link(dve.reciprocal(h_m, h_r))
            for j in range(TB):
                dve.tensor_tensor(h_A[:, j, :].rearrange("p (g e) -> p g e", g=8),
                                  h_tok[2][:, j, :].rearrange("p (g e) -> p g e", g=8),
                                  groups[:, j, :].unsqueeze(2).broadcast_to((P, 8, 64)), ALU.mult).then_inc(hy_n, 1)
            for c in range(4):
                lower_u(U_MIX2 + 4 + c, 4 + c, uf[c % 2])
            for i in range(4):
                ahead("wo2", i)
                for c in (2 * i, 2 * i + 1):
                    dve.tensor_copy(Facc[:, c, :], read(FIRST["wo2"] + c)[:, :]).then_inc(free["dve"], 1)
                    if c:
                        add_square("post2", c - 1)

            def add_normalised(name, gain, before, after=None):
                dve.wait_ge(n_bc, NORM[name] + 1)
                for c in range(KC):
                    link(dve.scalar_tensor_tensor(tn[c % 2], Facc[:, c, :], vcol(gain, c), bank[6][:, :], ALU.mult, ALU.mult))
                    dve.tensor_tensor(H[:, c, :], H[:, c, :], tn[c % 2], ALU.add).then_inc(h_upd, 1)
                    if after and c:
                        add_square(after, c - 1)
                dve.wait_ge(h_upd, before + KC)

            add_square("post2", KC - 1)
            factors(NORM["post2"])
            add_normalised("post2", "post2", 8, "mlp_pre2")
            add_square("mlp_pre2", KC - 1)
            factors(NORM["mlp_pre2"])
            normalised("mlp_pre2", NORM["mlp_pre2"], U_MLP, lambda c: vcol("mlp_pre2", c))

            def lower_hidden(i):
                lower_g(G_MLP + i, ff_h[:, i % 2, :])

            for g in range(MLP_G + 1):
                if g < MLP_G:
                    ahead("mi", g)
                    for i in (2 * g, 2 * g + 1):
                        dve.wait_ge(sg_done, 2 * FFN_CH + i + 1)
                        if i >= 2:
                            dve.wait_ge(g_l, G_MLP + i - 1)
                        n = FIRST[f"mi{g}"] + i % 2
                        dve.tensor_tensor(ff_h[:, i % 2, :], ff_s[:, i % 2, :], read(n)[:, :], ALU.mult).then_inc(free["dve"], 1)
                if g == 0:
                    lower_hidden(0)
                    lower_hidden(1)
                if g:
                    for c in range(KC):
                        if c == 2:
                            ahead("mout", g - 1)
                        if c in (4, 5) and g < MLP_G:
                            lower_hidden(2 * g + c - 4)
                        b = read(FIRST[f"mout{g - 1}"] + c)
                        if g == 1:
                            dve.tensor_copy(Facc[:, c, :], b[:, :]).then_inc(free["dve"], 1)
                        else:
                            dve.wait_ge(*free_of(FIRST[f"mout{g - 2}"] + c))
                            dve.tensor_tensor(Facc[:, c, :], Facc[:, c, :], b[:, :], ALU.add).then_inc(free["dve"], 1)
                        if g == MLP_G and c:
                            add_square("mlp_post2", c - 1)
            add_square("mlp_post2", KC - 1)
            factors(NORM["mlp_post2"])
            add_normalised("mlp_post2", "mlp_post2", 16)


def table_of(label, i):
    if label == "spec":
        return "cos" if i % 2 == 0 else "sin"
    if label == "dft":
        return ("cos", "sin", "cos", "sin_back")[i % 4]
    return None


W_SOURCE, PACKED = [], []
for _item in W_LIST:
    _key = table_of(*_item) or _item
    if _key not in PACKED:
        PACKED.append(_key)
    W_SOURCE.append(PACKED.index(_key))
M_SOURCE = len(PACKED)


def pack(inputs):
    import numpy as np
    f = {k: np.asarray(v) for k, v in inputs.items()}
    out = {}

    def columns(v):
        return np.asarray(v).reshape(-1, P).T

    table = np.zeros((P, NVEC), np.float32)

    def put(name, value):
        a, z = VEC[name]
        assert value.shape[1] == z - a, name
        table[:value.shape[0], a:z] = value

    put("c", columns(f["c"]))
    put("mod_b0", columns(f["mod_b"][0]))
    put("kv_mod_b", columns(f["kv_mod_b"]))
    put("mod_b1", columns(f["mod_b"][1]))
    for i in (0, 1):
        put(f"norm_mix{i}", columns(f["norm_mix"][i]))
        put(f"norm_ffn{i}", columns(f["norm_ffn"][i]))
    for name, key in (("kv_norm", "kv_norm"), ("final_norm", "final_norm"), ("pre2", "norm_mix_pre_2"),
                      ("post2", "norm_mix_post_2"), ("mlp_pre2", "norm_mlp_pre_2"), ("mlp_post2", "norm_mlp_post_2"),
                      ("a_lb", "a_lb"), ("a_out_norm", "a_out_norm"), ("conv_w", "conv_w_2"), ("conv_b", "conv_b_2"),
                      ("mlstm_norm", "mlstm_norm_w_2"), ("hyena_norm", "hyena_norm_w_2")):
        put(name, columns(f[key]))
    put("filt_b", np.stack([f["filt_b1_2"], f["filt_b2_2"], f["filt_b3_2"]], 1))
    put("filt_fr", f["filt_freq_2"].T)
    gate_rows = np.array([32 * q + h for q in range(4) for h in range(M_HEADS)])
    gates = np.zeros((P, 1), np.float32)
    gates[gate_rows, 0] = f["b_gates_2"]
    put("b_gates", gates)
    out["vec"] = table

    t = np.arange(SEQ)
    turns = (t[:, None] * t[None, :]) % (2 * SEQ)
    cos = np.cos(np.pi * turns / SEQ)
    sin = np.sin(np.pi * turns / SEQ)
    sign = 1.0 - 2.0 * (t % 2)
    forward, back = sin.copy(), sin.copy()
    forward[:, 0] = sign
    back[0, :] = sign
    tables = {"cos": cos, "sin": forward, "sin_back": back}

    def by_rows(w, k):
        return w.reshape(k, P, -1).transpose(1, 0, 2)

    w_in, w2 = f["a_w_in"][0], f["w_in_2"]
    kv = f["kv_w"]

    def std(w, i):
        return by_rows(w[:, 256 * i:256 * (i + 1)], KC)

    def pair(w, a, b):
        return by_rows(np.concatenate([w[:, a:a + P], w[:, b:b + P]], 1), KC)

    def tok(w, i):
        n, half = divmod(i, 2)
        return by_rows(w[half * 512:(half + 1) * 512, n * 512:(n + 1) * 512], 4)

    def rows(w, g):
        return by_rows(w[256 * g:256 * (g + 1)], 2)

    def slot(label, i):
        if label == "v0":
            return tok(w_in[:, 2048:3072], i)
        if label == "p0":
            return pair(w_in, 1024 + P * i, P * i)
        if label == "g0":
            return std(w_in[:, 3072:], i)
        if label[:2] in ("fi", "fo"):
            n = int(label[2])
            return pair(f["ffn_w_in"][n], P * i, FFN + P * i) if label[1] == "i" else rows(f["ffn_w_out"][n], i)
        if label == "vv":
            return tok(kv[:, D:], i)
        if label == "mv":
            return tok(w2[:, 2560:3072], i)
        if label == "mgate":
            w = np.zeros((D, 256), np.float32)
            w[:, gate_rows] = w2[:, 3584:3600]
            return by_rows(w, KC)
        if label == "mout":
            return rows(f["w_mlp_out_2"], i)
        src = {"wo0": f["a_w_out"][0], "kk": kv[:, :D], "qq": f["b_w_q"][0], "wo1": f["b_w_o"][0], "mqk": w2, "mo": w2[:, 3072:],
               "h2": w2[:, 1024:], "wo2": f["w_out_2"], "mi": f["w_mlp_in_2"]}[label]
        return std(src, i)

    wts = np.empty((M_SOURCE + NM, P, SLOT), np.float32)
    for n, key in enumerate(PACKED):
        wts[n] = (by_rows(tables[key], TB) if isinstance(key, str) else slot(*key)).reshape(P, SLOT)
    mods = [f["mod_w"][0], f["kv_mod_w"], f["mod_w"][1]]
    n = M_SOURCE
    for w in mods:
        for i in range(w.shape[1] // 256):
            wts[n] = std(w, i).reshape(P, SLOT)
            n += 1
    out["wts"] = wts

    out["filt_w1"] = f["filt_w1_2"]
    f32 = np.float32
    bands = (FE - 1) // 2
    lin = np.linspace(0.0, 1.0, SEQ, dtype=f32)[:, None]
    ang = f32(TWO_PI) * np.arange(SEQ, dtype=f32)[:, None] / f32(SEQ)
    fq = np.linspace(1e-4, bands - 1, bands, dtype=f32)[None, :]
    out["filt_z"] = np.concatenate([lin, np.cos(fq * ang), -np.sin(fq * ang)], -1).T.astype(f32)
    out["filt_w23"] = np.stack([f["filt_w2_2"], f["filt_w3_2"]], 1)
    out["filt_w4"] = f["filt_w4_2"]
    deltas = np.linspace(math.log(1e-2) / 1.5, math.log(1e-2) / 0.3, HW, dtype=f32)
    out["window"] = by_rows(np.exp(-lin * np.abs(deltas)[None, :]).astype(f32), TB)
    out["filt_bias"] = f["filt_bias_2"].reshape(1, 2 * HW)
    out["ident"] = np.eye(P, dtype=f32)
    out["x"] = f["x"][0].T
    s, q = np.arange(P)[:, None], np.arange(P)[None, :]
    masks = [s == q]
    for lev in range(NLEV - 1):
        m = 1 << lev
        masks.append((s // (2 * m) == q // (2 * m)) & (s // m % 2 == 0) & (q // m % 2 == 1))
    out["masks"] = np.stack(masks, 1).reshape(P, NLEV * P).astype(f32)
    far = np.clip(np.arange(SEQ)[None, :] - np.arange(SEQ - P, SEQ)[:, None], -REL_CLIP, CHUNK - 1) + REL_CLIP
    out["rel"] = f["b_rel_bias"][0][far].transpose(2, 0, 1)
    out["tri"] = np.stack([q >= s, q <= s], 1).astype(f32)
    out["sel"] = np.stack([np.repeat((np.arange(M_HEADS) == h)[:, None], P, 1) for h in range(M_HEADS)], 1).astype(f32)
    return out


def kernel(**inputs):
    import numpy as np
    import concourse.bacc as bacc
    from concourse.bass_utils import run_bass_kernel_spmd

    nc = bacc.Bacc("TRN2", target_bir_lowering=False, num_devices=1)
    arrays, A = {}, {}
    for name, a in pack(inputs).items():
        a = np.ascontiguousarray(a)
        arrays[f"in_{name}"] = a
        A[name] = nc.dram_tensor(f"in_{name}", a.shape, mybir.dt.from_np(a.dtype), kind="ExternalInput").ap()
    A["out"] = nc.dram_tensor("out", (D, SEQ), F32, kind="ExternalOutput").ap()
    build(nc, A)
    r = run_bass_kernel_spmd(nc, [arrays], core_ids=[0])
    return np.ascontiguousarray(r.results[0]["out"].T).reshape(1, SEQ, D)
```
